# Optimizing a Trainium2 kernel written in Bass

```python
import jax, jax.numpy as jnp
from jax import lax
import numpy as np

D_MODEL = 1024
BATCH = 1
SEQ = 1024
DEPTH = 1
DEC_BATCH = 8
DEC_SEQ = 4
PAST_LEN = 8192
PAGE_SIZE = 128

D_MIX = D_MODEL
D_CONV = D_MIX // 2
D_LRU = D_MIX - D_CONV
CONV_GROUPS = 8
LRU_HEADS = 8
LRU_HEAD_DIM = D_LRU // LRU_HEADS
CONV_WIDTH = 31
LRU_CONV_WIDTH = 4
LRU_C = 8.0
D_FF = 2816
D_PLE = 256
D_IN = 2 * D_CONV + 2 * D_LRU
EPS = 1e-6
FFN_RES_WEIGHT = 0.5

kernel_name = "hymba_conformer_rglru_macaron_step"

def rmsnorm(x, g):
    xf = x.astype(jnp.float32)
    y = xf * lax.rsqrt(jnp.mean(xf * xf, axis=-1, keepdims=True) + EPS)
    return (y * g.astype(jnp.float32)).astype(x.dtype)

def swiglu_ffn(x, w_gu, w_down):
    gu = x @ w_gu
    gate, up = jnp.split(gu, 2, axis=-1)
    return (jax.nn.silu(gate) * up) @ w_down

def causal_dwconv(xp, w, b):
    c = xp.shape[-1]
    y = lax.conv_general_dilated(xp, w[:, None, :].astype(xp.dtype), window_strides=(1,),
                                 padding='VALID', dimension_numbers=('NWC', 'WIO', 'NWC'),
                                 feature_group_count=c)
    return y + b

def lru_combine(left, right):
    a_l, b_l = left
    a_r, b_r = right
    return a_l * a_r, a_r * b_l + b_r

def mixer_block(x, conv_buf, lconv_buf, h0, pre_g, post_g, w_in, conv_w, conv_b, conv_norm_g,
                lru_conv_w, lru_conv_b, lru_wa, lru_ba, lru_wx, lru_bx, lru_lambda, w_out):
    bsz, t, _ = x.shape
    h = rmsnorm(x, pre_g)
    u = h @ w_in
    u_val, u_glu, u_x, u_gelu = jnp.split(u, [D_CONV, 2 * D_CONV, 2 * D_CONV + D_LRU], axis=-1)

    g = u_val * jax.nn.sigmoid(u_glu)
    gp = jnp.concatenate([conv_buf.astype(g.dtype), g], axis=1)
    c = causal_dwconv(gp, conv_w, conv_b)
    c = jax.nn.silu(rmsnorm(c, conv_norm_g))
    new_conv_buf = gp[:, -(CONV_WIDTH - 1):, :]

    xp = jnp.concatenate([lconv_buf.astype(u_x.dtype), u_x], axis=1)
    xc = causal_dwconv(xp, lru_conv_w, lru_conv_b)
    new_lconv_buf = xp[:, -(LRU_CONV_WIDTH - 1):, :]
    xh = xc.reshape(bsz, t, LRU_HEADS, LRU_HEAD_DIM)
    r = jax.nn.sigmoid(jnp.einsum('bthi,hij->bthj', xh, lru_wa).reshape(bsz, t, D_LRU) + lru_ba)
    i_g = jax.nn.sigmoid(jnp.einsum('bthi,hij->bthj', xh, lru_wx).reshape(bsz, t, D_LRU) + lru_bx)
    log_a = -LRU_C * r.astype(jnp.float32) * jax.nn.softplus(-lru_lambda.astype(jnp.float32))
    a = jnp.exp(log_a)
    bterm = jnp.sqrt(-jnp.expm1(2.0 * log_a)) * (i_g * xc).astype(jnp.float32)
    bterm = bterm.at[:, 0, :].add(a[:, 0, :] * h0.astype(jnp.float32))
    _, hs = lax.associative_scan(lru_combine, (a, bterm), axis=1)
    h_last = hs[:, -1, :].astype(h0.dtype)
    yb = hs.astype(x.dtype) * jax.nn.gelu(u_gelu)

    out = jnp.concatenate([c, yb], axis=-1) @ w_out
    return x + rmsnorm(out, post_g), new_conv_buf, new_lconv_buf, h_last

def decoder_layer(x, p, conv_buf, lconv_buf, h0, l,
                  ffn1_pre_g, ffn1_post_g, ffn1_w_gu, ffn1_w_down,
                  mix_pre_g, mix_post_g, w_in, conv_w, conv_b, conv_norm_g,
                  lru_conv_w, lru_conv_b, lru_wa, lru_ba, lru_wx, lru_bx, lru_lambda, w_out,
                  ffn2_pre_g, ffn2_post_g, ffn2_w_gu, ffn2_w_down,
                  ple_norm_g, ple_w_gate, ple_w_proj, ple_post_g):
    x = x + FFN_RES_WEIGHT * rmsnorm(swiglu_ffn(rmsnorm(x, ffn1_pre_g[l]), ffn1_w_gu[l], ffn1_w_down[l]),
                                     ffn1_post_g[l])
    x, cb, lcb, hl = mixer_block(x, conv_buf, lconv_buf, h0, mix_pre_g[l], mix_post_g[l], w_in[l],
                                 conv_w[l], conv_b[l], conv_norm_g[l], lru_conv_w[l], lru_conv_b[l],
                                 lru_wa[l], lru_ba[l], lru_wx[l], lru_bx[l], lru_lambda[l], w_out[l])
    x = x + FFN_RES_WEIGHT * rmsnorm(swiglu_ffn(rmsnorm(x, ffn2_pre_g[l]), ffn2_w_gu[l], ffn2_w_down[l]),
                                     ffn2_post_g[l])
    gate = jax.nn.sigmoid(rmsnorm(x, ple_norm_g[l]) @ ple_w_gate[l])
    e = p @ ple_w_proj[l]
    x = x + rmsnorm(gate * e, ple_post_g[l])
    return x, cb, lcb, hl

def setup_inputs(seed: int = 0) -> dict:
    key = jax.random.key(seed)
    ks = iter(jax.random.split(key, 40))
    f32 = jnp.float32

    def nrm(shape, scale):
        return jax.random.normal(next(ks), shape, f32) * scale

    def gain(shape):
        return 1.0 + 0.05 * jax.random.normal(next(ks), shape, f32)

    x_prompt = nrm((BATCH, SEQ, D_MODEL), 1.0)
    x_sample = nrm((DEC_BATCH, DEC_SEQ, D_MODEL), 1.0)
    cache_conv = nrm((DEPTH, DEC_BATCH, CONV_WIDTH - 1, D_CONV), 0.5)
    state_lru_conv = nrm((DEPTH, DEC_BATCH, LRU_CONV_WIDTH - 1, D_LRU), 0.5)
    state_lru_h = nrm((DEPTH, DEC_BATCH, D_LRU), 0.5)
    p_prompt = nrm((DEPTH, BATCH, SEQ, D_PLE), 1.0)
    p_sample = nrm((DEPTH, DEC_BATCH, DEC_SEQ, D_PLE), 1.0)

    u = jax.random.uniform(next(ks), (DEPTH, D_LRU), f32, minval=0.9, maxval=0.999)
    a0 = u ** (1.0 / LRU_C)
    lru_lambda = jnp.log(a0) - jnp.log1p(-a0)

    return {
        "x_prompt": x_prompt, "x_sample": x_sample,
        "cache_conv": cache_conv, "state_lru_conv": state_lru_conv, "state_lru_h": state_lru_h,
        "p_prompt": p_prompt, "p_sample": p_sample,
        "ffn1_pre_g": gain((DEPTH, D_MODEL)), "ffn1_post_g": gain((DEPTH, D_MODEL)),
        "ffn1_w_gu": nrm((DEPTH, D_MODEL, 2 * D_FF), D_MODEL ** -0.5),
        "ffn1_w_down": nrm((DEPTH, D_FF, D_MODEL), D_FF ** -0.5),
        "mix_pre_g": gain((DEPTH, D_MODEL)), "mix_post_g": gain((DEPTH, D_MODEL)),
        "w_in": nrm((DEPTH, D_MODEL, D_IN), D_MODEL ** -0.5),
        "conv_w": nrm((DEPTH, CONV_WIDTH, D_CONV), CONV_WIDTH ** -0.5),
        "conv_b": nrm((DEPTH, D_CONV), 0.01),
        "conv_norm_g": gain((DEPTH, D_CONV)),
        "lru_conv_w": nrm((DEPTH, LRU_CONV_WIDTH, D_LRU), LRU_CONV_WIDTH ** -0.5),
        "lru_conv_b": nrm((DEPTH, D_LRU), 0.01),
        "lru_wa": nrm((DEPTH, LRU_HEADS, LRU_HEAD_DIM, LRU_HEAD_DIM), LRU_HEAD_DIM ** -0.5),
        "lru_ba": nrm((DEPTH, D_LRU), 0.01),
        "lru_wx": nrm((DEPTH, LRU_HEADS, LRU_HEAD_DIM, LRU_HEAD_DIM), LRU_HEAD_DIM ** -0.5),
        "lru_bx": nrm((DEPTH, D_LRU), 0.01),
        "lru_lambda": lru_lambda,
        "w_out": nrm((DEPTH, D_MIX, D_MODEL), D_MIX ** -0.5),
        "ffn2_pre_g": gain((DEPTH, D_MODEL)), "ffn2_post_g": gain((DEPTH, D_MODEL)),
        "ffn2_w_gu": nrm((DEPTH, D_MODEL, 2 * D_FF), D_MODEL ** -0.5),
        "ffn2_w_down": nrm((DEPTH, D_FF, D_MODEL), D_FF ** -0.5),
        "ple_norm_g": gain((DEPTH, D_MODEL)),
        "ple_w_gate": nrm((DEPTH, D_MODEL, D_MODEL), D_MODEL ** -0.5),
        "ple_w_proj": nrm((DEPTH, D_PLE, D_MODEL), D_PLE ** -0.5),
        "ple_post_g": gain((DEPTH, D_MODEL)),
    }

def reference(x_prompt, x_sample, cache_conv, state_lru_conv, state_lru_h, p_prompt, p_sample,
              ffn1_pre_g, ffn1_post_g, ffn1_w_gu, ffn1_w_down,
              mix_pre_g, mix_post_g, w_in, conv_w, conv_b, conv_norm_g,
              lru_conv_w, lru_conv_b, lru_wa, lru_ba, lru_wx, lru_bx, lru_lambda, w_out,
              ffn2_pre_g, ffn2_post_g, ffn2_w_gu, ffn2_w_down,
              ple_norm_g, ple_w_gate, ple_w_proj, ple_post_g):
    dt = x_prompt.dtype
    xp, xs = x_prompt, x_sample
    conv_p, lconv_p, h_p = [], [], []
    conv_s, lconv_s, h_s = [], [], []
    for l in range(DEPTH):
        zc = jnp.zeros((BATCH, CONV_WIDTH - 1, D_CONV), dt)
        zl = jnp.zeros((BATCH, LRU_CONV_WIDTH - 1, D_LRU), dt)
        zh = jnp.zeros((BATCH, D_LRU), state_lru_h.dtype)
        xp, cb, lcb, hl = decoder_layer(
            xp, p_prompt[l], zc, zl, zh, l,
            ffn1_pre_g, ffn1_post_g, ffn1_w_gu, ffn1_w_down,
            mix_pre_g, mix_post_g, w_in, conv_w, conv_b, conv_norm_g,
            lru_conv_w, lru_conv_b, lru_wa, lru_ba, lru_wx, lru_bx, lru_lambda, w_out,
            ffn2_pre_g, ffn2_post_g, ffn2_w_gu, ffn2_w_down,
            ple_norm_g, ple_w_gate, ple_w_proj, ple_post_g)
        conv_p.append(cb); lconv_p.append(lcb); h_p.append(hl)
        xs, cb, lcb, hl = decoder_layer(
            xs, p_sample[l], cache_conv[l], state_lru_conv[l], state_lru_h[l], l,
            ffn1_pre_g, ffn1_post_g, ffn1_w_gu, ffn1_w_down,
            mix_pre_g, mix_post_g, w_in, conv_w, conv_b, conv_norm_g,
            lru_conv_w, lru_conv_b, lru_wa, lru_ba, lru_wx, lru_bx, lru_lambda, w_out,
            ffn2_pre_g, ffn2_post_g, ffn2_w_gu, ffn2_w_down,
            ple_norm_g, ple_w_gate, ple_w_proj, ple_post_g)
        conv_s.append(cb); lconv_s.append(lcb); h_s.append(hl)
    new_conv_p = jnp.stack(conv_p)
    new_lru_conv_p = jnp.stack(lconv_p)
    new_lru_h_p = jnp.stack(h_p)
    new_conv_s = jnp.stack(conv_s)
    new_lru_conv_s = jnp.stack(lconv_s)
    new_lru_h_s = jnp.stack(h_s)
    return (xp, xs, new_conv_p, new_lru_conv_p, new_lru_h_p, new_conv_s, new_lru_conv_s, new_lru_h_s)


_drawn_inputs = setup_inputs


def setup_inputs(seed=0):
    import zlib

    import numpy as np

    out = dict(_drawn_inputs(seed))
    spreads = {}
    factors = {'conv_b': 5.181,
     'lru_ba': 21.346,
     'lru_bx': 8.0,
     'ffn2_pre_g': 2.842,
     'ffn2_post_g': 4.067,
     'ple_norm_g': 19.666,
     'ple_post_g': 2.958}
    for name, (base, spread) in spreads.items():
        noise = np.random.default_rng([zlib.crc32(name.encode()), seed]).standard_normal(out[name].shape)
        drawn = base * np.exp(spread * noise) if base else spread * noise
        out[name] = __import__('jax').numpy.asarray(drawn.astype(out[name].dtype))
    for name, factor in factors.items():
        out[name] = (out[name] * factor).astype(out[name].dtype)
    return out
```

```python
from contextlib import ExitStack

import concourse.bass as bass
from concourse import mybir

F32 = mybir.dt.float32
F32R = mybir.dt.float32r
ALU = mybir.AluOpType
ACT = mybir.ActivationFunctionType

P = 128
D = 1024
KT = D // P
FF = 2816
NJ = 4
PLE = 256
PT = PLE // P
SEQ, NB, DEC = 1024, 8, 4
TOK = SEQ + NB * DEC
NC = 3
C = TOK // NC
LAST = SEQ - 2 * C
CW, LW = 31, 4
CH, LH = CW - 1, LW - 1
EPS = 1e-6
G = 2
NI = FF // P // G
WIDE = 256
BANKS = 6
STEP = NC * (2 * G + KT)

VECTORS = [("ffn1_pre_g", 8), ("ffn1_post_g", 8), ("mix_pre_g", 8), ("mix_post_g", 8),
           ("ffn2_pre_g", 8), ("ffn2_post_g", 8), ("ple_norm_g", 8), ("ple_post_g", 8),
           ("conv_b", 4), ("conv_norm_g", 4), ("lru_conv_b", 4), ("lru_ba", 4), ("lru_bx", 4),
           ("lru_lambda", 4), ("lru_conv_w", 16)]
ROW = {}
for _name, _n in VECTORS:
    ROW[_name] = sum(n for _, n in VECTORS[:len(ROW)])
NROWS = sum(n for _, n in VECTORS)


def ring_plan():
    at, n = {}, 0

    def put(*key):
        nonlocal n
        at[key if len(key) > 1 else key[0]] = n
        n += 1

    put("params")
    for c in range(NC):
        for k in range(KT):
            put("xT", c, k)
    at["ffn", 0] = n
    n += NI * STEP
    for c in range(NC):
        for t in range(4):
            put("vg", c, t)
    for s in range(2):
        put("cache", s)
    for u in (2, 3):
        for c in range(NC):
            for t in range(2):
                put("in", u, c, t)
    for s in range(3):
        put("convout", s)
    for u in (4, 5, 6):
        for c in range(NC):
            for t in range(2):
                put("in", u, c, t)
    put("state")
    for c in range(NC):
        for t in range(2):
            put("in", 7, c, t)
    for c in range(NC):
        for m in range(KT):
            put("wout", c, m)
    at["ffn", 1] = n
    n += NI * STEP
    for c in range(NC):
        for k in range(PT):
            put("pT", c, k)
    for c in range(NC):
        for q in range(4):
            for t in range(4):
                put("ple", c, q, t)
            if (c, q) in ((1, 3), (2, 3)):
                for s in range(6):
                    put("yT", c - 1, s)
    for s in range(6):
        put("yT", 2, s)
    return at, n


NORMS = ([("pre1", c, KT) for c in range(NC)]
         + [("post1", 0, KT), ("post1", 1, KT), ("pre2", 0, KT), ("post1", 2, KT),
            ("pre2", 1, KT), ("pre2", 2, KT)]
         + [("conv", c, NJ) for c in range(NC)]
         + [(n, c, KT) for c in range(NC) for n in ("post2", "pre3")]
         + [("post3", 0, KT), ("post3", 1, KT), ("pre4", 0, KT), ("post3", 2, KT),
            ("pre4", 1, KT), ("pre4", 2, KT)]
         + [("post4", c, KT) for c in range(NC)])
NORM = {(n, c): i for i, (n, c, _) in enumerate(NORMS)}
TILES = [t for _, _, t in NORMS]
SQ0 = [sum(TILES[:i]) for i in range(len(TILES) + 1)]
ADD0 = [sum(t - 1 for t in TILES[:i]) for i in range(len(TILES) + 1)]


def aux_plan():
    at, n = {}, 0
    first = NORM["conv", 0]
    for i in range(first):
        at["norm", i] = n
        n += 1
    for x in range(4 * NC):
        for which in "ri":
            at[which, x] = n
            n += 1
    for i in range(first, len(NORMS)):
        at["norm", i] = n
        n += 1
    return at


RING, RING_N = ring_plan()
AUX = aux_plan()
WIDE0 = {"ffn1": 0, "mix": 2 * NI, "ffn2": 2 * NI + 8 + 4 * NC, "ple": 4 * NI + 8 + 4 * NC}
N_WIDE = WIDE0["ple"] + 4 * NC


def cols(c):
    return slice(C * c, C * c + C)


def build(nc, a, out):
    ctx = ExitStack()
    with ctx:
        base = (nc.sbuf_base + 63) // 64 * 64
        at = [base]

        def place(name, shape, dt=F32, offset=None):
            size = 4
            for s in shape[1:]:
                size *= s
            if offset is None:
                offset = at[0]
                at[0] += (size + 31) // 32 * 32
            t = nc.alloc_sbuf_tensor_at(name, [P] + list(shape[1:]), dt, offset=offset)
            return t, offset, offset + (size + 31) // 32 * 32

        def tile(name, shape, dt=F32):
            return place(name, shape, dt)[0]

        x_hi = tile("x_hi", [P, KT, TOK], F32R)
        x_lo = tile("x_lo", [P, KT, TOK], F32R)
        w_hi = [tile(f"w_hi{s}", [P, KT * WIDE], F32R) for s in range(2)]
        w_lo = [tile(f"w_lo{s}", [P, KT * WIDE], F32R) for s in range(2)]
        raw = tile("raw", [P, KT * WIDE])
        rstd_pre = tile("rstd_pre", [P, TOK])
        rstd_post, norm_at, _ = place("rstd_post", [P, 2, C])
        ssum = tile("ssum", [P, C])
        std = tile("std", [P, C])
        sq, sq_at, _ = place("sq", [P, 2, C])
        ident = tile("ident", [P, P])
        ones = tile("ones", [P, P])
        params = tile("params", [P, 3 * P])
        half_g = tile("half_g", [P, 2 * KT])
        eps_t = tile("eps_t", [P, 1])
        sp = tile("sp", [P, 8, NJ])
        st_out = tile("st_out", [P, NJ, 36])
        pool0 = at[0]

        acc = tile("acc", [P, KT, TOK])
        a_hi = tile("a_hi", [P, G, TOK], F32R)
        a_lo = tile("a_lo", [P, G, TOK], F32R)
        wd_hi, wd_at, _ = place("wd_hi", [P, G * D], F32R)
        wd_lo = tile("wd_lo", [P, G * D], F32R)
        rawd, rawd_at, _ = place("rawd", [P, G * D])
        tmp_g, tmp_at, _ = place("tmp_g", [P, 2, C])
        tmp_u = tile("tmp_u", [P, 2, C])
        tmp_s = tile("tmp_s", [P, 2, C])
        tmp_a = tile("tmp_a", [P, 2, C])
        ffn_end = at[0]
        x_in, _, _ = place("x_in", [P, 3 * NC, D], offset=pool0)
        rows = place("rows", [P, 3 * P], offset=wd_at)[0]
        st_rows = place("st_rows", [P, NJ * P], offset=wd_at + 4 * 3 * P)[0]
        p_in = place("p_in", [P, 3 * NC, PLE], offset=tmp_at)[0]
        y_stage = place("y_stage", [P, 2, D], offset=rawd_at)[0]

        at[0] = pool0
        y_hi, yh_at, _ = place("y_hi", [P, KT, TOK], F32R)
        y_lo, yl_at, _ = place("y_lo", [P, KT, TOK], F32R)
        gp, g_at, _ = place("gp", [P, NJ, CH + SEQ])
        mix_end = at[0]
        gs, _, e = place("gs", [P, NJ, NB, CH + DEC], offset=norm_at)
        assert e <= sq_at
        ge = place("ge", [P, 2, C], offset=sq_at)[0]
        assert max(ffn_end, mix_end) <= nc.sbuf_usable_end, (ffn_end, mix_end, nc.sbuf_usable_end)
        row = 4 * TOK
        conv = place("conv", [P, NJ, TOK], offset=yl_at)[0]
        hs = place("hs", [P, NJ, TOK], offset=yl_at + 4 * row)[0]
        cache_in = place("cache_in", [P, 2, NJ * P], offset=yl_at + 4 * row)[0]
        gs_new = place("gs_new", [P, NJ, NB * CH], offset=yl_at + 4 * row)[0]
        gate_raw = place("gate_raw", [P, 2, NJ, P], offset=yl_at + 4 * row + 4096)[0]
        cv_stage = place("cv_stage", [P, 3, NJ * P], offset=yl_at + 6 * row)[0]
        ux_p, _, e = place("ux_p", [P, 2, LH + SEQ], offset=yh_at)
        ux_s, _, e = place("ux_s", [P, 2, NB, LH + DEC], offset=e)
        xc_hi, _, e = place("xc_hi", [P, 2, C], F32R, offset=e)
        xc_lo, _, e = place("xc_lo", [P, 2, C], F32R, offset=e)
        assert e <= yh_at + 4 * row
        st_stage = place("st_stage", [P, NJ * P], offset=yh_at)[0]
        gw_hi, _, e = place("gw_hi", [P, 2, NJ, P], F32R, offset=yh_at + 4 * row)
        gw_lo, _, e = place("gw_lo", [P, 2, NJ, P], F32R, offset=e)
        assert e <= yh_at + 6 * row
        xc = place("xc", [P, 2, C], offset=yh_at + 6 * row)[0]
        lru_r = place("lru_r", [P, C], offset=yh_at + 6 * row + 8 * C)[0]
        lru_i = place("lru_i", [P, C], offset=yh_at + 6 * row + 12 * C)[0]
        lru_a = place("lru_a", [P, C], offset=yh_at + 6 * row + 16 * C)[0]
        lru_q = place("lru_q", [P, C], offset=yh_at + 6 * row + 20 * C)[0]
        glu = place("glu", [P, 2, C], offset=yl_at + 6 * row)[0]
        oc = place("oc", [P, KT, C], offset=g_at)[0]

        ps = ctx.enter_context(nc.psum_tensor("ps", [P, BANKS, 512], F32))
        ps_aux = ctx.enter_context(nc.psum_tensor("ps_aux", [P, 2, 512], F32))

        def f32(t):
            return t.bitcast(F32)

        def vec(name, k):
            return params[:, ROW[name] + k:ROW[name] + k + 1]

        def conv_w(tap, j):
            n = P + tap * NJ + j
            return params[:, n:n + 1]

        def st_in(j, r0, r1):
            return params[:, 2 * P + 32 * j + r0:2 * P + 32 * j + r1]

        def sem(name):
            return ctx.enter_context(nc.semaphore(name))

        const_ready = sem("const_ready")
        rows_in = sem("rows_in")
        x_read = [sem(f"x_read{c}") for c in range(NC)]
        psum_full = sem("psum_full")
        psum_free = sem("psum_free")
        aux_full = sem("aux_full")
        aux_free = sem("aux_free")
        raw_in = sem("raw_in")
        wide_hi = sem("wide_hi")
        wide_lo = sem("wide_lo")
        rawd_in = sem("rawd_in")
        down_hi = sem("down_hi")
        down_lo = sem("down_lo")
        silu_done = sem("silu_done")
        prod_done = sem("prod_done")
        a_hi_done = sem("a_hi_done")
        a_lo_done = sem("a_lo_done")
        sq_done = sem("sq_done")
        add_done = sem("add_done")
        rstd_done = sem("rstd_done")
        x_new = sem("x_new")
        x_hi_done = sem("x_hi_done")
        x_lo_done = sem("x_lo_done")
        half_done = sem("half_done")
        sp_act = sem("sp_act")
        dve_own = sem("dve_own")
        act_own = sem("act_own")
        sig_done = sem("sig_done")
        glu_done = sem("glu_done")
        cache_read = sem("cache_read")
        gate_in = sem("gate_in")
        gate_zero = sem("gate_zero")
        gw_hi_done = sem("gw_hi_done")
        gw_lo_done = sem("gw_lo_done")
        gs_new_done = sem("gs_new_done")
        conv_step = sem("conv_step")
        xc_done = sem("xc_done")
        xc_hi_done = sem("xc_hi_done")
        xc_lo_done = sem("xc_lo_done")
        lru_act = sem("lru_act")
        lru_gain = sem("lru_gain")
        lru_sqrt = sem("lru_sqrt")
        scan_done = sem("scan_done")
        gelu_done = sem("gelu_done")
        yb_done = sem("yb_done")
        yb_hi_done = sem("yb_hi_done")
        yb_lo_done = sem("yb_lo_done")
        cn_done = sem("cn_done")
        cn_silu = sem("cn_silu")
        yc_lo_done = sem("yc_lo_done")
        conv_out = sem("conv_out")
        states_out = sem("states_out")
        p_read = sem("p_read")
        pt_hi = sem("pt_hi")
        gate_sig = sem("gate_sig")
        y_fin = sem("y_fin")
        y_out = [sem(f"y_out{s}") for s in range(2)]

        block = ctx.enter_context(nc.Block())

        gu_src = [a[f"ffn{f}_w_gu"][0].rearrange("(k p) (s i n) -> s i p k n", p=P, s=2, n=WIDE)
                  for f in (1, 2)]
        down_src = [a[f"ffn{f}_w_down"][0].rearrange("(i t p) n -> i p t n", t=G, p=P)
                    for f in (1, 2)]
        win_src = a["w_in"][0].rearrange("(k p) (u n) -> u p k n", p=P, n=WIDE)
        wout_src = a["w_out"][0].rearrange("(k p) (u n) -> u p k n", p=P, n=WIDE)
        pg_src = a["ple_w_gate"][0].rearrange("(k p) (u n) -> u p k n", p=P, n=WIDE)
        IN_UNITS = [0, 2, 1, 3, 4, 5, 6, 7]

        def wide_src(v):
            if v < WIDE0["mix"]:
                return gu_src[0][v % 2, v // 2]
            if v < WIDE0["mix"] + 8:
                return win_src[IN_UNITS[v - WIDE0["mix"]]]
            if v < WIDE0["ffn2"]:
                return wout_src[(v - WIDE0["mix"]) % 4]
            if v < WIDE0["ple"]:
                v -= WIDE0["ffn2"]
                return gu_src[1][v % 2, v // 2]
            return pg_src[(v - WIDE0["ple"]) % 4]

        def wide_gain(v):
            if v < WIDE0["mix"]:
                return "ffn1_pre_g"
            if v < WIDE0["mix"] + 8:
                return "mix_pre_g"
            if v < WIDE0["ffn2"]:
                return None
            return "ffn2_pre_g" if v < WIDE0["ple"] else "ple_norm_g"

        def wide_last_use(v):
            if v < WIDE0["mix"] or WIDE0["ffn2"] <= v < WIDE0["ple"]:
                f = int(v >= WIDE0["ffn2"])
                v -= WIDE0["ffn2"] if f else 0
                return RING["ffn", f] + STEP * (v // 2) + 4 * NC - 1 + v % 2
            if v < WIDE0["mix"] + 8:
                u = v - WIDE0["mix"]
                return RING["vg", 2, 3] + 1 if u < 2 else RING["in", u, 2, 1] + 1
            if v < WIDE0["ffn2"]:
                c, q = divmod(v - WIDE0["mix"] - 8, 4)
                return RING["wout", c, 2 * q + 1] + 1
            c, q = divmod(v - WIDE0["ple"], 4)
            return RING["ple", c, q, 3] + 1

        @block.sync
        def _(sp_eng):
            eng = sp_eng

            def load_wide(v, src=None):
                if not isinstance(v, int) or v > 0:
                    eng.wait_ge(wide_lo, v)
                eng.dma_start(raw[:, :].rearrange("p (k n) -> p k n", k=KT),
                              wide_src(v) if src is None else src).then_inc(raw_in, 16)

            def load_down(d, src):
                if not isinstance(d, int) or d > 0:
                    eng.wait_ge(down_lo, d)
                eng.dma_start(rawd[:, :].rearrange("p (t n) -> p t n", t=G), src).then_inc(rawd_in, 16)

            def ffn_loads(f):
                v0, d0 = WIDE0[f"ffn{f + 1}"], NI * f
                load_down(d0, down_src[f][0])
                load_wide(v0 + 2)
                load_wide(v0 + 3)
                with eng.Fori(1, NI - 1) as i:
                    load_down(i + d0, down_src[f][i])
                    load_wide(i * 2 + (v0 + 2), gu_src[f][0, i + 1])
                    load_wide(i * 2 + (v0 + 3), gu_src[f][1, i + 1])
                load_down(d0 + NI - 1, down_src[f][NI - 1])
                load_wide(v0 + 2 * NI)
                load_wide(v0 + 2 * NI + 1)

            def store(n):
                c, q = divmod(n, 3)
                w, r0 = min(P, C - P * q), C * c + P * q
                eng.wait_ge(psum_free, RING["yT", c, 2 * q + 1] + 1)
                if n == 8:
                    w = LAST - 2 * P
                    eng.dma_start(out["y_sample"].rearrange("b t n -> (b t) n"),
                                  y_stage[w:w + NB * DEC, n % 2, :]).then_inc(y_out[n % 2], 16)
                eng.dma_start(out["y_prompt"][0, r0:r0 + w, :], y_stage[0:w, n % 2, :]
                              ).then_inc(y_out[n % 2], 16)

            for name, n in VECTORS:
                src = a[name] if name != "lru_conv_w" else a[name][0]
                eng.dma_start(rows[ROW[name]:ROW[name] + n, 0:P],
                              src.rearrange("a (k p) -> (a k) p", p=P)).then_inc(rows_in, 16)
            eng.dma_start(rows[0:CW * NJ, P:2 * P],
                          a["conv_w"][0].rearrange("a (k p) -> (a k) p", p=P)).then_inc(rows_in, 16)
            eng.dma_start(st_rows[0:NB * LH, :],
                          a["state_lru_conv"][0].rearrange("b w n -> (b w) n")).then_inc(rows_in, 16)
            eng.dma_start(st_rows[NB * LH:NB * LH + NB, :], a["state_lru_h"][0]).then_inc(rows_in, 16)
            load_wide(0)
            load_wide(1)
            ffn_loads(0)
            eng.wait_ge(psum_full, RING["ffn", 0] + NI * STEP)
            for s in range(2):
                eng.dma_start(cache_in[0:4 * CH, s, :],
                              a["cache_conv"][0, 4 * s:4 * s + 4].rearrange("b w n -> (b w) n")
                              ).then_inc(cache_read, 16)
            eng.wait_ge(gate_zero, 1)
            for g, name in enumerate(("lru_wa", "lru_wx")):
                w = a[name][0].rearrange("(j two) r n -> two r j n", two=2)
                for half in range(2):
                    eng.dma_start(gate_raw[64 * half:64 * half + 64, g, :, 64 * half:64 * half + 64],
                                  w[half]).then_inc(gate_in, 16)
            for v in range(WIDE0["mix"] + 2, WIDE0["mix"] + 6):
                load_wide(v)
            eng.wait_ge(psum_free, RING["convout", 2] + 1)
            eng.dma_start(out["conv_p"][0, 0], cv_stage[0:CH, 0, :]).then_inc(conv_out, 16)
            for s in range(2):
                eng.dma_start(out["conv_s"][0, 4 * s:4 * s + 4].rearrange("b w n -> (b w) n"),
                              cv_stage[0:4 * CH, 1 + s, :]).then_inc(conv_out, 16)
            for v in range(WIDE0["mix"] + 6, WIDE0["mix"] + 9):
                load_wide(v)
            eng.wait_ge(psum_free, RING["state"] + 1)
            for dst, r in ((out["lconv_p"][0, 0], 0),
                           (out["lconv_s"][0].rearrange("b w n -> (b w) n"), LH),
                           (out["h_p"][0], LH + NB * LH), (out["h_s"][0], LH + NB * LH + 1)):
                eng.dma_start(dst, st_stage[r:r + dst.shape[0], :]).then_inc(states_out, 16)
            for v in range(WIDE0["mix"] + 9, WIDE0["ffn2"] + 2):
                load_wide(v)
            eng.wait_ge(psum_full, RING["ffn", 1])
            eng.wait_ge(x_lo_done, 24 * 2)
            ffn_loads(1)
            load_down(2 * NI, a["ple_w_proj"][0].rearrange("(t p) n -> p t n", p=P))
            eng.wait_ge(a_lo_done, 2 * NI * NC * G)
            for c in range(NC):
                for q in range(3):
                    n, r0 = (P, C * c + P * q) if q < 2 else (C - 2 * P, C * c + 2 * P)
                    if c == 2 and q == 2:
                        n = LAST - 2 * P
                        eng.dma_start(p_in[n:n + NB * DEC, 8, :],
                                      a["p_sample"][0].rearrange("b t n -> (b t) n")
                                      ).then_inc(p_read, 16)
                    eng.dma_start(p_in[0:n, 3 * c + q, :], a["p_prompt"][0, 0, r0:r0 + n, :]
                                  ).then_inc(p_read, 16)
            for v in range(WIDE0["ple"] + 2, N_WIDE - 1):
                load_wide(v)
            for n in range(3):
                store(n)
            load_wide(N_WIDE - 1)
            for n in range(3, 9):
                store(n)
            for s in range(2):
                eng.wait_ge(y_out[s], (96, 64)[s])
            eng.wait_ge(conv_out, 48)
            eng.wait_ge(states_out, 64)

        @block.gpsimd
        def _(eng):
            eng.memset(ident[:, :], 0.0).then_inc(const_ready, 1)
            eng.memset(ones[:, :], 1.0).then_inc(const_ready, 1)
            eng.memset(eps_t[:, :], EPS).then_inc(const_ready, 1)
            eng.wait_ge(const_ready, 3)
            eng.affine_select(out=ident[:, :], in_=ident[:, :], compare_op=ALU.not_equal, fill=1.0,
                              base=0, pattern=[[-1, P]], channel_multiplier=1
                              ).then_inc(const_ready, 1)

        @block.tensor
        def _(eng):
            def bank(n, ncols=C):
                if n >= BANKS:
                    eng.wait_ge(psum_free, n - BANKS + 1)
                return ps[:, n % BANKS, 0:ncols]

            def bank_at(base_n, off):
                eng.wait_ge(psum_free, base_n + (off - BANKS + 1))

            def passes(dst, wh, wl, xh, xl, first, last):
                eng.matmul(dst, wl, xh, start=first, stop=False)
                eng.matmul(dst, wh, xl, start=False, stop=False)
                return eng.matmul(dst, wh, xh, start=False, stop=last)

            def wide(s, k, t):
                sl = slice(k * WIDE + t * P, k * WIDE + t * P + P)
                return w_hi[s][:, sl], w_lo[s][:, sl]

            def tile_product(dst, s, t, c):
                for k in range(KT):
                    wh, wl = wide(s, k, t)
                    mm = passes(dst, wh, wl, x_hi[:, k, cols(c)], x_lo[:, k, cols(c)],
                                k == 0, k == KT - 1)
                mm.then_inc(psum_full, 1)

            def batch_products(n0, specs, c, x0):
                dsts = [bank(n0 + i) for i in range(len(specs))]
                for k in range(KT):
                    if x0 is None:
                        eng.wait_ge(psum_free, RING["xT", c, k] + 1)
                    else:
                        eng.wait_ge(x_lo_done, x0 + 8 * c + k + 1)
                    for dst, (s, t) in zip(dsts, specs):
                        wh, wl = wide(s, k, t)
                        mm = passes(dst, wh, wl, x_hi[:, k, cols(c)], x_lo[:, k, cols(c)],
                                    k == 0, k == KT - 1)
                        if k == KT - 1:
                            mm.then_inc(psum_full, 1)

            def norm_sum(name, c):
                i = NORM[name, c]
                n = AUX["norm", i]
                eng.wait_ge(add_done, ADD0[i + 1])
                if n >= 2:
                    eng.wait_ge(aux_free, n - 1)
                eng.matmul(ps_aux[:, n % 2, 0:C], ones[:, :], ssum[:, :], start=True, stop=True
                           ).then_inc(aux_full, 1)

            def down_products(c, n_of, a_count, wait_bank):
                eng.wait_ge(a_lo_done, a_count)
                for m in range(KT):
                    wait_bank(m)
                    dst = ps[:, n_of(m) % BANKS, 0:C]
                    for t in range(G):
                        sl = slice(t * D + m * P, t * D + m * P + P)
                        mm = passes(dst, wd_hi[:, sl], wd_lo[:, sl], a_hi[:, t, cols(c)],
                                    a_lo[:, t, cols(c)], t == 0, t == G - 1)
                    mm.then_inc(psum_full, 1)

            SPECS = [(0, 0), (1, 0), (0, 1), (1, 1)]

            def ffn_step(f, i, first=False, x0=None, hook=None, mid_down=None):
                R, V, Q, E = (RING["ffn", f], WIDE0[f"ffn{f + 1}"], NI * NC * G * f, NI * f)
                eng.wait_ge(wide_lo, i * 2 + (V + 2))
                for c in range(NC):
                    if first:
                        batch_products(R + 4 * c, SPECS, c, x0)
                        if hook:
                            hook(c)
                        continue
                    for t, (s, h) in enumerate(SPECS):
                        off = 4 * c + t
                        bank_at(i * STEP, R + off)
                        tile_product(ps[:, (R + off) % BANKS, 0:C], s, h, c)
                eng.wait_ge(down_lo, i + (E + 1))
                for c in range(NC):
                    off = 4 * NC + KT * c
                    down_products(c, lambda m: R + off + m, i * (NC * G) + (Q + 2 * c + 2),
                                  lambda m: bank_at(i * STEP, R + off + m))
                    if mid_down:
                        mid_down(c)

            def ffn(f, x0, hook, mid_down):
                ffn_step(f, 0, first=True, x0=x0, hook=hook)
                with eng.Fori(1, NI - 1) as i:
                    ffn_step(f, i)
                ffn_step(f, NI - 1, mid_down=mid_down)

            eng.wait_ge(const_ready, 4)
            eng.wait_ge(rows_in, 16 * (len(VECTORS) + 3))
            dst = bank(0, 512)
            eng.transpose(dst[:, 0:NROWS], rows[0:NROWS, 0:P], ident[0:NROWS, 0:NROWS])
            eng.transpose(dst[:, P:P + CW * NJ], rows[0:CW * NJ, P:2 * P],
                          ident[0:CW * NJ, 0:CW * NJ])
            for j in range(NJ):
                mm = eng.transpose(dst[:, 2 * P + 32 * j:2 * P + 32 * j + 32],
                                   st_rows[0:32, j * P:j * P + P], ident[0:32, 0:32])
            mm.then_inc(psum_full, 1)

            def to_features(src, n, c, k):
                dst = bank(n)
                for q in range(3):
                    w = min(P, C - P * q)
                    mm = eng.transpose(dst[:, P * q:P * q + w],
                                       src[0:w, 3 * c + q, k * P:k * P + P], ident[0:w, 0:w])
                mm.then_inc(psum_full, 1)

            for c in range(NC):
                eng.wait_ge(x_read[c], 48 + 16 * (c == 2))
                for k in range(KT):
                    to_features(x_in, RING["xT", c, k], c, k)
                norm_sum("pre1", c)

            def down_norms(name):
                def mid(c):
                    if c >= 1:
                        norm_sum(name, c - 1)
                return mid

            ffn(0, None, None, down_norms("post1"))

            eng.wait_ge(wide_lo, WIDE0["mix"] + 2)
            for c in range(NC):
                batch_products(RING["vg", c, 0], [(0, 0), (0, 1), (1, 0), (1, 1)], c, 0)
                norm_sum("pre2", c)
                if c == 0:
                    norm_sum("post1", 2)
            eng.wait_ge(cache_read, 32)
            for s in range(2):
                dst = bank(RING["cache", s], 4 * 4 * CH)
                for j in range(NJ):
                    mm = eng.transpose(dst[:, j * 4 * CH:(j + 1) * 4 * CH],
                                       cache_in[0:4 * CH, s, j * P:j * P + P],
                                       ident[0:4 * CH, 0:4 * CH])
                mm.then_inc(psum_full, 1)

            def lru_gates(x):
                j, c, t = lru_tile(x)
                eng.wait_ge(xc_lo_done, x + 1)
                for g, which in enumerate("ri"):
                    n = AUX[which, x]
                    eng.wait_ge(aux_free, n - 1)
                    passes(ps_aux[:, n % 2, 0:C], gw_hi[:, g, j, :], gw_lo[:, g, j, :],
                           xc_hi[:, x % 2, :], xc_lo[:, x % 2, :], True, True
                           ).then_inc(aux_full, 1)

            def in_unit(u, behind=None):
                eng.wait_ge(wide_lo, WIDE0["mix"] + u + 1)
                for c in range(NC):
                    for t in range(2):
                        tile_product(bank(RING["in", u, c, t]), u % 2, t, c)
                        if behind:
                            behind(2 * c + t)

            in_unit(2)
            in_unit(3)
            eng.wait_ge(gs_new_done, 1)
            for s in range(3):
                n = RING["convout", s]
                if n >= BANKS:
                    eng.wait_ge(psum_free, n - BANKS + 1)
                for j in range(NJ):
                    src = gp[:, j, SEQ:SEQ + CH] if s == 0 else \
                        gs_new[:, j, (4 * s - 4) * CH:4 * s * CH]
                    w = CH if s == 0 else 4 * CH
                    mm = eng.transpose(ps[0:w, n % BANKS, j * P:j * P + P], src, ident[:, :])
                mm.then_inc(psum_full, 1)
            eng.wait_ge(gw_lo_done, 1)
            in_unit(4, lambda s: s > 0 and lru_gates(s - 1))
            in_unit(5, lambda s: lru_gates(s + 5))
            in_unit(6, lambda s: s == 0 and lru_gates(11))
            eng.wait_ge(scan_done, 12)
            n = RING["state"]
            eng.wait_ge(psum_free, n - BANKS + 1)
            for j in range(NJ):
                mm = eng.transpose(ps[0:36, n % BANKS, j * P:j * P + P], st_out[:, j, :], ident[:, :])
            mm.then_inc(psum_full, 1)
            in_unit(7)

            def out_unit(c, q):
                v = WIDE0["mix"] + 8 + 4 * c + q
                eng.wait_ge(wide_lo, v + 1)
                if q == 0:
                    eng.wait_ge(yc_lo_done, NJ * (c + 1))
                    eng.wait_ge(yb_lo_done, 12)
                for t in range(2):
                    dst = bank(RING["wout", c, 2 * q + t])
                    for k in range(KT):
                        wh, wl = wide(v % 2, k, t)
                        mm = passes(dst, wh, wl, y_hi[:, k, cols(c)], y_lo[:, k, cols(c)],
                                    k == 0, k == KT - 1)
                    mm.then_inc(psum_full, 1)

            norm_sum("conv", 0)
            norm_sum("conv", 1)
            for c in range(NC):
                out_unit(c, 0)
                if c == 0:
                    norm_sum("conv", 2)
                else:
                    norm_sum("post2", c - 1)
                out_unit(c, 1)
                if c > 0:
                    norm_sum("pre3", c - 1)
                out_unit(c, 2)
                out_unit(c, 3)
            norm_sum("post2", 2)

            ffn(1, 24, lambda c: c == 0 and norm_sum("pre3", 2), down_norms("post3"))

            eng.wait_ge(p_read, 16 * 10)
            for c in range(NC):
                for k in range(PT):
                    to_features(p_in, RING["pT", c, k], c, k)

            def ple_unit(c, q):
                v = WIDE0["ple"] + 4 * c + q
                eng.wait_ge(wide_lo, v + 1)
                if q == 0:
                    batch_products(RING["ple", c, 0, 0], [(v % 2, 0), (v % 2, 1)], c, 48)
                else:
                    for t in range(2):
                        tile_product(bank(RING["ple", c, q, t]), v % 2, t, c)
                if (c, q) == (0, 0):
                    eng.wait_ge(down_lo, 2 * NI + 1)
                    eng.wait_ge(psum_free, RING["pT", 2, 1] + 1)
                for t in range(2):
                    dst = bank(RING["ple", c, q, 2 + t])
                    for k in range(PT):
                        sl = slice(k * D + (2 * q + t) * P, k * D + (2 * q + t) * P + P)
                        mm = passes(dst, wd_hi[:, sl], wd_lo[:, sl], a_hi[:, k, cols(c)],
                                    a_lo[:, k, cols(c)], k == 0, k == PT - 1)
                    mm.then_inc(psum_full, 1)

            def to_tokens(c):
                for q in range(3):
                    w = min(P, C - P * q)
                    for half in range(2):
                        n = RING["yT", c, 2 * q + half]
                        eng.wait_ge(psum_free, n - BANKS + 1)
                        for k in range(4):
                            kk = 4 * half + k
                            eng.wait_ge(y_fin, KT * c + kk + 1)
                            mm = eng.transpose(ps[0:w, n % BANKS, k * P:k * P + P],
                                               acc[:, kk, C * c + P * q:C * c + P * q + w],
                                               ident[:, :])
                        mm.then_inc(psum_full, 1)

            ple_unit(0, 0)
            norm_sum("pre4", 0)
            norm_sum("post3", 2)
            for q in (1, 2, 3):
                ple_unit(0, q)
            ple_unit(1, 0)
            norm_sum("pre4", 1)
            ple_unit(1, 1)
            norm_sum("pre4", 2)
            ple_unit(1, 2)
            norm_sum("post4", 0)
            ple_unit(1, 3)
            to_tokens(0)
            for q in (0, 1):
                ple_unit(2, q)
            norm_sum("post4", 1)
            for q in (2, 3):
                ple_unit(2, q)
            to_tokens(1)
            norm_sum("post4", 2)
            to_tokens(2)

        @block.scalar
        def _(eng):
            own = [0]

            def done(ins):
                own[0] += 1
                ins.then_inc(act_own, 1)
                eng.wait_ge(act_own, own[0])

            def split_wide(v, gain=None, last_use=None):
                s, gain = (v % 2, wide_gain(v)) if isinstance(v, int) else gain
                if last_use is None and v >= 2:
                    last_use = wide_last_use(v - 2)
                if last_use is not None:
                    eng.wait_ge(psum_full, last_use)
                eng.wait_ge(raw_in, v * 16 + 16)
                if gain is None:
                    eng.activation(w_hi[s][:, :], raw[:, :], ACT.Copy).then_inc(wide_hi, 1)
                    return
                for k in range(KT):
                    sl = slice(k * WIDE, (k + 1) * WIDE)
                    ins = eng.activation(w_hi[s][:, sl], raw[:, sl], ACT.Copy, scale=vec(gain, k))
                ins.then_inc(wide_hi, 1)

            def split_down(d, last_use=None):
                if last_use is not None:
                    eng.wait_ge(psum_full, last_use)
                eng.wait_ge(rawd_in, d * 16 + 16)
                eng.activation(wd_hi[:, :], rawd[:, :], ACT.Copy).then_inc(down_hi, 1)

            def square(i, m, src, src_sem=None, count=None):
                if src_sem is not None:
                    eng.wait_ge(src_sem, count)
                if m == 0:
                    if i > 0:
                        eng.wait_ge(aux_full, AUX["norm", i - 1] + 1)
                    dst = ssum[:, :]
                else:
                    if ADD0[i] + max(0, m - 2) > 0:
                        eng.wait_ge(add_done, ADD0[i] + max(0, m - 2))
                    dst = sq[:, m % 2, :]
                eng.activation(dst, src, ACT.Square).then_inc(sq_done, 1)

            def root(name, c):
                i = NORM[name, c]
                n = AUX["norm", i]
                width = P * TILES[i]
                eng.wait_ge(aux_full, n + 1)
                if i > 0:
                    eng.wait_ge(rstd_done, i)
                eng.activation(std[:, :], ps_aux[:, n % 2, 0:C], ACT.Sqrt, scale=1.0 / width,
                               bias=eps_t[:, :]).then_inc(aux_free, 1)

            def squares(name, c, src, sem_, count0):
                i = NORM[name, c]
                for m in range(TILES[i]):
                    square(i, m, src(m), sem_, count0 + m + 1)

            def apply(name, c, x0, src):
                i = NORM[name, c]
                for m in range(KT):
                    eng.wait_ge(x_new, x0 + m + 1)
                    eng.activation(x_hi[:, m, cols(c)], src(m), ACT.Copy).then_inc(x_hi_done, 1)
                    square(i, m, src(m))

            def pair(f, i, c, h):
                R, Q = RING["ffn", f], NI * NC * G * f
                q, n = NC * G * i + (Q + 2 * c + h), STEP * i + (R + 4 * c + 2 * h)
                b = h
                eng.wait_ge(psum_free, n + 1)
                if f or not isinstance(i, int) or i or c:
                    eng.wait_ge(prod_done, q - 1)
                eng.activation(tmp_s[:, b, :], tmp_g[:, b, :], ACT.Silu).then_inc(silu_done, 1)
                eng.wait_ge(prod_done, q + 1)
                if not isinstance(i, int) or i:
                    eng.wait_ge(psum_full, STEP * i + (R - STEP + 4 * NC + KT * (c + 1)))
                eng.activation(a_hi[:, h, cols(c)], tmp_a[:, b, :], ACT.Copy).then_inc(a_hi_done, 1)

            def ffn_step(f, i, last=False):
                R, V, E = RING["ffn", f], WIDE0[f"ffn{f + 1}"], NI * f
                gain = f"ffn{f + 1}_pre_g"
                for c in range(NC):
                    for h in range(G):
                        pair(f, i, c, h)
                    if c == 0:
                        split_down(i + E, None if isinstance(i, int) and i == 0 else i * STEP + R)
                for s in range(2):
                    if last:
                        split_wide(V + 2 * NI + s)
                    else:
                        split_wide(i * 2 + (V + 2 + s), (s, gain), i * STEP + (R + 4 * NC - 1 + s))

            def ffn(f):
                ffn_step(f, 0)
                with eng.Fori(1, NI - 1) as i:
                    ffn_step(f, i)
                ffn_step(f, NI - 1, last=True)

            for c in range(NC):
                for q in range(3):
                    n, r0 = (P, C * c + P * q) if q < 2 else (C - 2 * P, C * c + 2 * P)
                    if c == 2 and q == 2:
                        n = LAST - 2 * P
                        eng.dma_start(x_in[n:n + NB * DEC, 8, :],
                                      a["x_sample"].rearrange("b t n -> (b t) n")
                                      ).then_inc(x_read[c], 16)
                    eng.dma_start(x_in[0:n, 3 * c + q, :], a["x_prompt"][0, r0:r0 + n, :]
                                  ).then_inc(x_read[c], 16)
            eng.wait_ge(const_ready, 4)
            eng.wait_ge(half_done, 1)
            eng.activation(sp[:, 1, :], sp[:, 0, :], ACT.Exp).then_inc(sp_act, 1)
            split_wide(0)
            for c in range(NC):
                for k in range(KT):
                    n = RING["xT", c, k]
                    eng.wait_ge(psum_full, n + 1)
                    eng.activation(x_hi[:, k, cols(c)], ps[:, n % BANKS, 0:C], ACT.Copy)
                    square(NORM["pre1", c], k, ps[:, n % BANKS, 0:C])
                root("pre1", c)
                if c == 0:
                    split_wide(1)

            def behind_ffn(f, post, pre, batch):
                n0 = RING["ffn", f] + (NI - 1) * STEP + 4 * NC
                tile_of = lambda c: (lambda m: acc[:, m, cols(c)])
                for c in (0, 1):
                    squares(post, c, tile_of(c), psum_free, n0 + KT * c)
                    root(post, c)
                if f:
                    p_to_features()
                apply(pre, 0, 24 * 2 * f, tile_of(0))
                if f:
                    split_down(2 * NI, RING["ffn", 1] + NI * STEP)
                root(pre, 0)
                batch(0)
                squares(post, 2, tile_of(2), psum_free, n0 + KT * 2)
                root(post, 2)
                apply(pre, 1, 24 * 2 * f + 8, tile_of(1))

            def p_to_features():
                for c in range(NC):
                    for k in range(PT):
                        n = RING["pT", c, k]
                        eng.wait_ge(psum_full, n + 1)
                        eng.activation(a_hi[:, k, cols(c)], ps[:, n % BANKS, 0:C], ACT.Copy
                                       ).then_inc(pt_hi, 1)

            ffn(0)

            def sigmoid_glu(n, ring_n):
                b = n % 2
                eng.wait_ge(psum_free, ring_n + 1)
                eng.activation(glu[:, b, :], glu[:, b, :], ACT.Sigmoid).then_inc(sig_done, 1)

            def glu_batch(c):
                for t in range(2):
                    sigmoid_glu(2 * c + t, RING["vg", c, 2 + t])

            behind_ffn(0, "post1", "pre2", glu_batch)
            root("pre2", 1)
            glu_batch(1)
            apply("pre2", 2, 16, lambda m: acc[:, m, cols(2)])
            root("pre2", 2)
            glu_batch(2)
            split_wide(WIDE0["mix"] + 2)
            eng.wait_ge(gate_in, 64)
            eng.activation(gw_hi[:, :, :, :], gate_raw[:, :, :, :], ACT.Copy).then_inc(gw_hi_done, 1)
            split_wide(WIDE0["mix"] + 3)
            split_wide(WIDE0["mix"] + 4)
            for c in range(NC):
                for t in range(2):
                    sigmoid_glu(6 + 2 * c + t, RING["in", 3, c, t])
            split_wide(WIDE0["mix"] + 5)

            def lru_front(x):
                eng.wait_ge(xc_done, x + 1)
                if x >= 2:
                    eng.wait_ge(aux_full, AUX["i", x - 2] + 1)
                eng.activation(xc_hi[:, x % 2, :], xc[:, x % 2, :], ACT.Copy).then_inc(xc_hi_done, 1)

            def lru_gates(x):
                j, c, t = lru_tile(x)
                nr, ni = AUX["r", x], AUX["i", x]
                if x > 0:
                    eng.wait_ge(scan_done, x)
                eng.wait_ge(aux_full, nr + 1)
                eng.activation(lru_r[:, :], ps_aux[:, nr % 2, 0:C], ACT.Sigmoid,
                               bias=vec("lru_ba", j)).then_inc(aux_free, 1)
                eng.wait_ge(aux_full, ni + 1)
                eng.activation(lru_i[:, :], ps_aux[:, ni % 2, 0:C], ACT.Sigmoid,
                               bias=vec("lru_bx", j)).then_inc(aux_free, 1)
                eng.wait_ge(aux_free, nr + 1)
                eng.activation(lru_a[:, :], lru_r[:, :], ACT.Exp, scale=sp[:, 6, j:j + 1]
                               ).then_inc(lru_act, 1)
                eng.wait_ge(lru_act, 3 * x + 1)
                eng.activation(lru_r[:, :], lru_r[:, :], ACT.Tanh, scale=sp[:, 7, j:j + 1]
                               ).then_inc(lru_act, 1)
                eng.activation(lru_q[:, :], lru_a[:, :], ACT.Square).then_inc(lru_act, 1)

            def lru_root(x):
                eng.wait_ge(lru_gain, x + 1)
                eng.activation(lru_q[:, :], lru_q[:, :], ACT.Sqrt).then_inc(lru_sqrt, 1)

            for x in range(12):
                lru_front(x)
                if x > 0:
                    lru_root(x - 1)
                lru_gates(x)
                if x == 5:
                    split_wide(WIDE0["mix"] + 6)

            def gelu_tile(n):
                j, c, t = lru_tile(n)
                b = n % 2
                eng.wait_ge(psum_free, RING["in", 6 + n // 6, c, t] + 1)
                eng.activation(ge[:, b, :], ge[:, b, :], ACT.Gelu_apprx_tanh).then_inc(gelu_done, 1)
                eng.wait_ge(yb_done, n + 1)
                if n == 0:
                    eng.wait_ge(aux_full, AUX["i", 11] + 1)
                eng.activation(y_hi[:, NJ + j, cols(c)], ge[:, b, :], ACT.Copy
                               ).then_inc(yb_hi_done, 1)

            split_wide(WIDE0["mix"] + 7)
            lru_root(11)
            for n in range(12):
                gelu_tile(n)
                if n == 5:
                    split_wide(WIDE0["mix"] + 8)
            split_wide(WIDE0["mix"] + 9)

            for c in range(NC):
                i = NORM["conv", c]
                if c == 0:
                    eng.wait_ge(conv_step, 2 * CW * NJ)
                    eng.wait_ge(yb_lo_done, 12)
                for j in range(NJ):
                    square(i, j, conv[:, j, cols(c)])
                root("conv", c)
                for j in range(NJ):
                    n = NJ * c + j
                    eng.wait_ge(cn_done, n + 1)
                    done(eng.activation(conv[:, j, cols(c)], conv[:, j, cols(c)], ACT.Silu,
                                        scale=vec("conv_norm_g", j)))
                    if n == 0:
                        eng.wait_ge(states_out, 64)
                    eng.activation(y_hi[:, j, cols(c)], conv[:, j, cols(c)], ACT.Copy
                                   ).then_inc(cn_silu, 1)

            for c in range(NC):
                i = NORM["post2", c]
                for m in range(KT):
                    square(i, m, oc[:, m, :], psum_free, RING["wout", c, m] + 1)
                    if m % 2:
                        v = WIDE0["mix"] + 8 + 4 * c + m // 2 + 2
                        split_wide(v)
                root("post2", c)
                apply("pre3", c, 24 + 8 * c, lambda m: oc[:, m, :])
                if c < 2:
                    root("pre3", c)

            f2_first = [True]

            def ffn2_first_step():
                R, V, E = RING["ffn", 1], WIDE0["ffn2"], NI
                for c in range(NC):
                    for h in range(G):
                        pair(1, 0, c, h)
                    if c == 0:
                        root("pre3", 2)
                        split_down(E)
                for s in range(2):
                    split_wide(V + 2 + s)

            ffn2_first_step()
            with eng.Fori(1, NI - 1) as i:
                ffn_step(1, i)
            ffn_step(1, NI - 1, last=True)

            def gate_unit(c, q):
                for t in range(2):
                    n = 8 * c + 2 * q + t
                    eng.wait_ge(psum_free, RING["ple", c, q, t] + 1)
                    if n >= 2:
                        c0, q0 = divmod(n - 2, 8)
                        eng.wait_ge(psum_free, RING["ple", c0, q0 // 2, 2 + t] + 1)
                    eng.activation(tmp_s[:, t, :], tmp_g[:, t, :], ACT.Sigmoid
                                   ).then_inc(gate_sig, 1)
                v = WIDE0["ple"] + 4 * c + q + 2
                if v < N_WIDE:
                    split_wide(v)

            def z_squares(c):
                i = NORM["post4", c]
                for m in range(KT):
                    square(i, m, acc[:, m, cols(c)], psum_free,
                           RING["ple", c, m // 2, 2 + m % 2] + 1)

            behind_ffn(1, "post3", "pre4", lambda c: gate_unit(0, 0))
            for q in (1, 2, 3):
                gate_unit(0, q)
            root("pre4", 1)
            gate_unit(1, 0)
            apply("pre4", 2, 48 + 16, lambda m: acc[:, m, cols(2)])
            gate_unit(1, 1)
            root("pre4", 2)
            z_squares(0)
            gate_unit(1, 2)
            root("post4", 0)
            gate_unit(1, 3)
            gate_unit(2, 0)
            z_squares(1)
            gate_unit(2, 1)
            root("post4", 1)
            gate_unit(2, 2)
            gate_unit(2, 3)
            z_squares(2)
            root("post4", 2)

        @block.vector
        def _(eng):
            own = [0]

            def mark(ins):
                own[0] += 1
                ins.then_inc(dve_own, 1)
                return own[0]

            def done(ins):
                mark(ins)
                eng.wait_ge(dve_own, own[0])

            def bank(n):
                eng.wait_ge(psum_full, n + 1)
                return ps[:, n % BANKS, 0:C]

            def bank_at(reg, n):
                eng.wait_ge(psum_full, reg + (n + 1))
                return ps[:, n % BANKS, 0:C]

            def split_wide(v, s=None, gain=""):
                if s is None:
                    s, gain = v % 2, wide_gain(v)
                eng.wait_ge(wide_hi, v + 1)
                if gain is None:
                    eng.tensor_tensor(w_lo[s][:, :], raw[:, :], f32(w_hi[s][:, :]), ALU.subtract
                                      ).then_inc(wide_lo, 1)
                    return
                for k in range(KT):
                    sl = slice(k * WIDE, (k + 1) * WIDE)
                    ins = eng.scalar_tensor_tensor(w_lo[s][:, sl], raw[:, sl], vec(gain, k),
                                                   f32(w_hi[s][:, sl]), ALU.mult, ALU.subtract)
                ins.then_inc(wide_lo, 1)

            def split_down(d):
                eng.wait_ge(down_hi, d + 1)
                eng.tensor_tensor(wd_lo[:, :], rawd[:, :], f32(wd_hi[:, :]), ALU.subtract
                                  ).then_inc(down_lo, 1)

            def add_square(i, m):
                eng.wait_ge(sq_done, SQ0[i] + m + 1)
                if ADD0[i] + m - 1 > 0:
                    eng.wait_ge(add_done, ADD0[i] + m - 1)
                eng.tensor_tensor(ssum[:, :], ssum[:, :], sq[:, m % 2, :], ALU.add
                                  ).then_inc(add_done, 1)

            post_buf = {}

            def invert(name, c):
                i = NORM[name, c]
                eng.wait_ge(aux_free, AUX["norm", i] + 1)
                if name.startswith("pre"):
                    dst = rstd_pre[:, cols(c)]
                else:
                    post_buf[name, c] = len(post_buf) % 2
                    dst = rstd_post[:, post_buf[name, c], :]
                eng.reciprocal(dst, std[:, :]).then_inc(rstd_done, 1)

            def rstd(name, c):
                eng.wait_ge(rstd_done, NORM[name, c] + 1)
                return rstd_pre[:, cols(c)] if name.startswith("pre") else \
                    rstd_post[:, post_buf[name, c], :]

            def apply(post, c, x0, src, gain, pre, after=None):
                r = rstd(post, c)
                n = own[0]
                for m0 in range(0, KT, 2):
                    for m in (m0, m0 + 1):
                        n1 = mark(eng.tensor_tensor(src(m), src(m), r, ALU.mult))
                    for m in (m0, m0 + 1):
                        eng.wait_ge(dve_own, n1 - 1 + (m - m0))
                        n2 = mark(eng.scalar_tensor_tensor(src(m), src(m), gain(m),
                                                           f32(x_hi[:, m, cols(c)]),
                                                           ALU.mult, ALU.add))
                    for m in (m0, m0 + 1):
                        eng.wait_ge(dve_own, n2 - 1 + (m - m0))
                        eng.tensor_tensor(src(m), src(m), f32(x_lo[:, m, cols(c)]), ALU.add
                                          ).then_inc(x_new if pre else y_fin, 1)
                    if pre:
                        for m in (m0 - 2, m0 - 1) if m0 else ():
                            apply_tail(c, m, x0, src, pre)
                if pre:
                    for m in (KT - 2, KT - 1):
                        apply_tail(c, m, x0, src, pre)

            def apply_tail(c, m, x0, src, pre):
                eng.wait_ge(x_hi_done, x0 + m + 1)
                eng.tensor_tensor(x_lo[:, m, cols(c)], src(m), f32(x_hi[:, m, cols(c)]),
                                  ALU.subtract).then_inc(x_lo_done, 1)
                if m:
                    add_square(NORM[pre, c], m)

            def pair(f, i, c, h):
                R, Q = RING["ffn", f], NI * NC * G * f
                q, n = NC * G * i + (Q + 2 * c + h), STEP * i + (R + 4 * c + 2 * h)
                off = R + 4 * c + 2 * h
                warm = f or not isinstance(i, int) or i or c
                r = rstd_pre[:, cols(c)]
                src = bank_at(i * STEP, off)
                if warm:
                    eng.wait_ge(silu_done, q - 1)
                eng.tensor_tensor(tmp_g[:, h, :], src, r, ALU.mult).then_inc(psum_free, 1)
                src = bank_at(i * STEP, off + 1)
                if warm:
                    eng.wait_ge(prod_done, q - 1)
                eng.tensor_tensor(tmp_u[:, h, :], src, r, ALU.mult).then_inc(psum_free, 1)
                eng.wait_ge(silu_done, q + 1)
                eng.wait_ge(psum_free, n + 2)
                if warm:
                    eng.wait_ge(a_lo_done, q - 1)
                eng.tensor_tensor(tmp_a[:, h, :], tmp_s[:, h, :], tmp_u[:, h, :], ALU.mult
                                  ).then_inc(prod_done, 1)
                eng.wait_ge(a_hi_done, q + 1)
                eng.tensor_tensor(a_lo[:, h, cols(c)], tmp_a[:, h, :], f32(a_hi[:, h, cols(c)]),
                                  ALU.subtract).then_inc(a_lo_done, 1)

            def down(f, i, c, m):
                off = RING["ffn", f] + 4 * NC + KT * c + m
                src = bank_at(i * STEP, off)
                if isinstance(i, int) and i == 0:
                    eng.tensor_copy(acc[:, m, cols(c)], src).then_inc(psum_free, 1)
                    return
                eng.wait_ge(psum_free, STEP * i + (off - STEP + 1))
                eng.tensor_tensor(acc[:, m, cols(c)], src, acc[:, m, cols(c)], ALU.add
                                  ).then_inc(psum_free, 1)

            def ffn_step(f, i, invert_pre=None):
                V, E = WIDE0[f"ffn{f + 1}"], NI * f
                gain = f"ffn{f + 1}_pre_g"
                for c in range(NC):
                    for h in range(G):
                        pair(f, i, c, h)
                    if c == 0:
                        if invert_pre:
                            invert(*invert_pre)
                            eng.wait_ge(rstd_done, NORM[invert_pre] + 1)
                        split_down(i + E)
                split_wide(i * 2 + (V + 2), 0, gain)
                for c in range(NC):
                    for m in range(KT):
                        down(f, i, c, m)
                    if c == 1:
                        split_wide(i * 2 + (V + 3), 1, gain)

            def ffn_last(f, post):
                i, V, E = NI - 1, WIDE0[f"ffn{f + 1}"], NI * f
                for c in range(NC):
                    for h in range(G):
                        pair(f, i, c, h)
                    if c == 0:
                        split_down(i + E)
                split_wide(V + 2 * NI)
                for c in range(NC):
                    for m in range(KT):
                        down(f, i, c, m)
                        if c and m > 1:
                            add_square(NORM[post, c - 1], m - 1)
                    if c:
                        add_square(NORM[post, c - 1], KT - 1)
                    if c == 1:
                        invert(post, 0)
                        split_wide(V + 2 * NI + 1)

            acc_tile = lambda c: (lambda m: acc[:, m, cols(c)])

            def behind_ffn(f, post, pre, batch, middle=None):
                x0 = 24 * 2 * f
                gain = lambda m: half_g[:, KT * f + m:KT * f + m + 1]
                if f:
                    p_to_features()
                apply(post, 0, x0, acc_tile(0), gain, pre)
                if f:
                    split_down(2 * NI)
                invert(post, 1)
                invert(pre, 0)
                batch(0)
                for m in range(1, KT):
                    add_square(NORM[post, 2], m)
                apply(post, 1, x0 + 8, acc_tile(1), gain, pre)
                invert(post, 2)
                return gain

            def p_to_features():
                for c in range(NC):
                    for k in range(PT):
                        n = RING["pT", c, k]
                        eng.wait_ge(pt_hi, PT * c + k + 1)
                        eng.tensor_tensor(a_lo[:, k, cols(c)], ps[:, n % BANKS, 0:C],
                                          f32(a_hi[:, k, cols(c)]), ALU.subtract
                                          ).then_inc(psum_free, 1)

            eng.wait_ge(psum_full, 1)
            width = 2 * P
            n = mark(eng.tensor_copy(params[:, 0:NROWS], ps[:, 0, 0:NROWS]))
            n = mark(eng.tensor_copy(params[:, P:P + CW * NJ], ps[:, 0, P:P + CW * NJ]))
            eng.tensor_copy(params[:, width:3 * P], ps[:, 0, width:3 * P]).then_inc(psum_free, 1)
            eng.wait_ge(dve_own, n)
            lam = params[:, ROW["lru_lambda"]:ROW["lru_lambda"] + NJ]
            done(eng.tensor_scalar(sp[:, 2, :], lam, -1.0, None, ALU.mult))
            eng.tensor_tensor(sp[:, 0, :], sp[:, 2, :], lam, ALU.min).then_inc(half_done, 1)
            for f in range(2):
                g0 = ROW[f"ffn{f + 1}_post_g"]
                done(eng.tensor_scalar(half_g[:, KT * f:KT * f + KT], params[:, g0:g0 + KT], 0.5,
                                       None, ALU.mult))
            eng.wait_ge(sp_act, 1)
            done(eng.tensor_scalar(sp[:, 3, :], sp[:, 1, :], 2.0, None, ALU.add))
            done(eng.reciprocal(sp[:, 4, :], sp[:, 3, :]))
            done(eng.tensor_tensor(sp[:, 3, :], sp[:, 1, :], sp[:, 4, :], ALU.mult))
            done(eng.tensor_tensor(sp[:, 4, :], sp[:, 3, :], sp[:, 3, :], ALU.mult))
            done(eng.tensor_scalar(sp[:, 5, :], sp[:, 4, :], 1.0 / 17, 1.0 / 15, ALU.mult, ALU.add))
            for d in (13, 11, 9, 7, 5, 3, 1):
                done(eng.tensor_tensor(sp[:, 5, :], sp[:, 5, :], sp[:, 4, :], ALU.mult))
                done(eng.tensor_scalar(sp[:, 5, :], sp[:, 5, :], 1.0 / d, None, ALU.add))
            done(eng.tensor_tensor(sp[:, 5, :], sp[:, 5, :], sp[:, 3, :], ALU.mult))
            done(eng.tensor_scalar(sp[:, 2, :], sp[:, 2, :], 0.0, None, ALU.max))
            done(eng.scalar_tensor_tensor(sp[:, 5, :], sp[:, 5, :], 2.0, sp[:, 2, :], ALU.mult,
                                          ALU.add))
            done(eng.tensor_scalar(sp[:, 6, :], sp[:, 5, :], -8.0, None, ALU.mult))
            done(eng.tensor_scalar(sp[:, 7, :], sp[:, 5, :], 8.0, None, ALU.mult))
            split_wide(0)

            for c in range(NC):
                i = NORM["pre1", c]
                for k in range(KT):
                    n = RING["xT", c, k]
                    eng.wait_ge(sq_done, SQ0[i] + k + 1)
                    eng.tensor_tensor(x_lo[:, k, cols(c)], ps[:, n % BANKS, 0:C],
                                      f32(x_hi[:, k, cols(c)]), ALU.subtract
                                      ).then_inc(psum_free, 1)
                    eng.wait_ge(psum_free, n + 1)
                    if k:
                        add_square(i, k)
                invert("pre1", c)
                if c == 0:
                    split_wide(1)

            eng.wait_ge(rstd_done, NC)
            ffn_step(0, 0)
            with eng.Fori(1, NI - 1) as i:
                ffn_step(0, i)
            ffn_last(0, "post1")

            glu_n = [0]

            def parts(c):
                return C if c < 2 else LAST

            def put_g(c, j, src, r, op_in1=None):
                w = parts(c)
                ins = eng.tensor_tensor(gp[:, j, CH + C * c:CH + C * c + w], src[:, 0:w],
                                        r[:, 0:w], ALU.mult)
                if c == 2:
                    ins = eng.tensor_tensor(
                        gs[:, j, :, CH:CH + DEC],
                        src[:, w:C].rearrange("p (b t) -> p b t", b=NB),
                        r[:, w:C].rearrange("p (b t) -> p b t", b=NB), ALU.mult)
                ins.then_inc(psum_free, 1)

            def value(n, c, j):
                put_g(c, j, bank(n), rstd("pre2", c))

            def glu_gate(n, c, j):
                b = glu_n[0] % 2
                src = bank(n)
                if glu_n[0] >= 2:
                    eng.wait_ge(glu_done, glu_n[0] - 1)
                eng.tensor_tensor(glu[:, b, :], src, rstd("pre2", c), ALU.mult
                                  ).then_inc(psum_free, 1)
                glu_n[0] += 1

            def glu_mult(k, c, j):
                eng.wait_ge(sig_done, k + 1)
                w = parts(c)
                dst = gp[:, j, CH + C * c:CH + C * c + w]
                ins = eng.tensor_tensor(dst, dst, glu[:, k % 2, 0:w], ALU.mult)
                if c == 2:
                    dst = gs[:, j, :, CH:CH + DEC]
                    ins = eng.tensor_tensor(
                        dst, dst, glu[:, k % 2, w:C].rearrange("p (b t) -> p b t", b=NB), ALU.mult)
                ins.then_inc(glu_done, 1)

            def vg_batch(c):
                for j in range(2):
                    value(RING["vg", c, j], c, j)
                for j in range(2):
                    glu_gate(RING["vg", c, 2 + j], c, j)
                for j in range(2):
                    eng.wait_ge(psum_free, RING["vg", c, j] + 1)
                    glu_mult(2 * c + j, c, j)

            gain1 = behind_ffn(0, "post1", "pre2", vg_batch)
            invert("pre2", 1)
            vg_batch(1)
            apply("post1", 2, 16, acc_tile(2), gain1, "pre2")
            invert("pre2", 2)
            vg_batch(2)
            eng.wait_ge(psum_full, RING["ffn", 0] + NI * STEP)
            eng.memset(gate_raw[:, :, :, :], 0.0).then_inc(gate_zero, 1)
            n_hist = mark(eng.memset(gp[:, :, 0:CH], 0.0))
            n_ux0 = mark(eng.memset(ux_p[:, :, 0:LH], 0.0))
            for s in range(2):
                n = RING["cache", s]
                eng.wait_ge(psum_full, n + 1)
                for j in range(NJ):
                    ins = eng.tensor_copy(
                        gs[:, j, 4 * s:4 * s + 4, 0:CH],
                        ps[:, n % BANKS, j * 4 * CH:(j + 1) * 4 * CH].rearrange(
                            "p (b w) -> p b w", b=4))
                ins.then_inc(psum_free, 1)
            eng.wait_ge(psum_free, RING["cache", 1] + 1)
            eng.wait_ge(dve_own, n_ux0)
            split_wide(WIDE0["mix"] + 2)
            eng.wait_ge(gw_hi_done, 1)
            eng.tensor_tensor(gw_lo[:, :, :, :], gate_raw[:, :, :, :], f32(gw_hi[:, :, :, :]),
                              ALU.subtract).then_inc(gw_lo_done, 1)
            split_wide(WIDE0["mix"] + 3)

            conv_n = [0]

            def conv_taps(count):
                for n in range(conv_n[0], min(conv_n[0] + count, CW * NJ)):
                    two, r = divmod(n, 2 * CW)
                    tap, j = r // 2, 2 * two + r % 2
                    if n >= 2:
                        eng.wait_ge(conv_step, 2 * n - 2)
                    if r == 0:
                        eng.wait_ge(glu_done, 6 * (two + 1))
                    dst_p, src_p = conv[:, j, 0:SEQ], gp[:, j, tap:tap + SEQ]
                    dst_s = conv[:, j, SEQ:TOK].rearrange("p (b t) -> p b t", b=NB)
                    src_s = gs[:, j, :, tap:tap + DEC]
                    for dst, src in ((dst_p, src_p), (dst_s, src_s)):
                        if tap == 0:
                            ins = eng.tensor_scalar(dst, src, conv_w(0, j), vec("conv_b", j),
                                                    ALU.mult, ALU.add)
                        else:
                            ins = eng.scalar_tensor_tensor(dst, src, conv_w(tap, j), dst,
                                                           ALU.mult, ALU.add)
                        ins.then_inc(conv_step, 1)
                    conv_n[0] = n + 1

            for c in range(NC):
                for t in range(2):
                    value(RING["in", 2, c, t], c, 2 + t)
                    conv_taps(4)
            split_wide(WIDE0["mix"] + 4)
            for c in range(NC):
                for t in range(2):
                    glu_gate(RING["in", 3, c, t], c, 2 + t)
                    conv_taps(4)
                    eng.wait_ge(psum_free, RING["in", 2, c, t] + 1)
                    glu_mult(6 + 2 * c + t, c, 2 + t)
            split_wide(WIDE0["mix"] + 5)
            eng.wait_ge(glu_done, 4 * NC)
            eng.tensor_copy(gs_new[:, :, :].rearrange("p j (b w) -> p (j b) w", w=CH),
                            gs[:, :, :, DEC:DEC + CH].rearrange("p j b w -> p (j b) w")
                            ).then_inc(gs_new_done, 1)
            for s in range(3):
                n = RING["convout", s]
                w = CH if s == 0 else 4 * CH
                eng.wait_ge(psum_full, n + 1)
                eng.tensor_copy(cv_stage[0:w, s, :], ps[0:w, n % BANKS, :]).then_inc(psum_free, 1)

            def lru_front(x):
                j, c, t = lru_tile(x)
                if c == 0:
                    if x >= 6:
                        eng.wait_ge(xc_done, x)
                    done(eng.tensor_copy(ux_s[:, t, :, 0:LH],
                                         st_in(j, 0, NB * LH).rearrange("p (b w) -> p b w", b=NB)))
                src = bank(RING["in", 4 + x // 6, c, t])
                r = rstd("pre2", c)
                w = parts(c)
                ins = eng.tensor_tensor(ux_p[:, t, LH + C * c:LH + C * c + w], src[:, 0:w],
                                        r[:, 0:w], ALU.mult)
                if c == 2:
                    ins = eng.tensor_tensor(
                        ux_s[:, t, :, LH:LH + DEC], src[:, w:C].rearrange("p (b t) -> p b t", b=NB),
                        r[:, w:C].rearrange("p (b t) -> p b t", b=NB), ALU.mult)
                ins.then_inc(psum_free, 1)
                eng.wait_ge(psum_free, RING["in", 4 + x // 6, c, t] + 1)
                if x >= 2:
                    eng.wait_ge(scan_done, x - 1)
                b = x % 2
                for tap in range(LW):
                    wt = params[:, ROW["lru_conv_w"] + tap * NJ + j:][:, 0:1]
                    pieces = [(xc[:, b, 0:w], ux_p[:, t, C * c + tap:C * c + tap + w])]
                    if c == 2:
                        pieces.append((xc[:, b, w:C].rearrange("p (b t) -> p b t", b=NB),
                                       ux_s[:, t, :, tap:tap + DEC]))
                    if tap:
                        eng.wait_ge(dve_own, own[0])
                    for dst, s_ in pieces:
                        if tap == 0:
                            ins = eng.tensor_scalar(dst, s_, wt, vec("lru_conv_b", j), ALU.mult,
                                                    ALU.add)
                        else:
                            ins = eng.scalar_tensor_tensor(dst, s_, wt, dst, ALU.mult, ALU.add)
                        if tap < LW - 1:
                            mark(ins)
                ins.then_inc(xc_done, 1)
                if c == 2:
                    eng.tensor_copy(st_out[:, j, 0:LH], ux_p[:, t, SEQ:SEQ + LH])
                    done(eng.tensor_copy(
                        st_out[:, j, LH:LH + NB * LH].rearrange("p (b w) -> p b w", b=NB),
                        ux_s[:, t, :, DEC:DEC + LH]))
                eng.wait_ge(xc_hi_done, x + 1)
                eng.tensor_tensor(xc_lo[:, b, :], xc[:, b, :], f32(xc_hi[:, b, :]), ALU.subtract
                                  ).then_inc(xc_lo_done, 1)

            def lru_one_minus(x):
                eng.wait_ge(lru_act, 3 * x + 3)
                eng.scalar_tensor_tensor(lru_q[:, :], lru_q[:, :], 1.0, lru_r[:, :], ALU.add,
                                         ALU.mult).then_inc(lru_gain, 1)

            def lru_scan(x):
                j, c, t = lru_tile(x)
                if x == 0:
                    eng.wait_ge(gw_lo_done, 1)
                if x == 6:
                    eng.wait_ge(conv_out, 48)
                done(eng.tensor_tensor(lru_i[:, :], lru_i[:, :], xc[:, x % 2, :], ALU.mult))
                eng.wait_ge(lru_sqrt, x + 1)
                done(eng.tensor_tensor(lru_i[:, :], lru_i[:, :], lru_q[:, :], ALU.mult))
                w = parts(c)
                first = 0.0 if c == 0 else hs[:, j, C * c - 1:C * c]
                if c:
                    eng.wait_ge(scan_done, x - 1)
                ins = eng.tensor_tensor_scan(hs[:, j, C * c:C * c + w], lru_a[:, 0:w],
                                             lru_i[:, 0:w], first, ALU.mult, ALU.add)
                if c == 2:
                    mark(ins)
                    for b in range(NB):
                        o = LAST + DEC * b
                        ins = eng.tensor_tensor_scan(
                            hs[:, j, C * c + o:C * c + o + DEC], lru_a[:, o:o + DEC],
                            lru_i[:, o:o + DEC], st_in(j, 24 + b, 25 + b), ALU.mult, ALU.add)
                    done(ins)
                    n_st = LH + NB * LH
                    eng.tensor_copy(st_out[:, j, n_st:n_st + 1], hs[:, j, SEQ - 1:SEQ])
                    ins = eng.tensor_copy(
                        st_out[:, j, n_st + 1:n_st + 1 + NB],
                        hs[:, j, SEQ:TOK].rearrange("p (b t) -> p b t", b=NB)[:, :, DEC - 1])
                ins.then_inc(scan_done, 1)

            for x in range(12):
                lru_front(x)
                if x:
                    lru_one_minus(x - 1)
                conv_taps(4)
                if x:
                    lru_scan(x - 1)
                if x == 5:
                    split_wide(WIDE0["mix"] + 6)

            def gelu_tile(n):
                j, c, t = lru_tile(n)
                b = n % 2
                src = bank(RING["in", 6 + n // 6, c, t])
                if n >= 2:
                    eng.wait_ge(yb_lo_done, n - 1)
                eng.tensor_tensor(ge[:, b, :], src, rstd("pre2", c), ALU.mult
                                  ).then_inc(psum_free, 1)
                conv_taps(3)
                if n == 0:
                    lru_one_minus(11)
                    conv_taps(2)
                    lru_scan(11)
                eng.wait_ge(gelu_done, n + 1)
                eng.wait_ge(scan_done, 12 if n == 11 else min(12, max(n + 1, 1)))
                eng.tensor_tensor(ge[:, b, :], ge[:, b, :], hs[:, j, cols(c)], ALU.mult
                                  ).then_inc(yb_done, 1)
                eng.wait_ge(yb_hi_done, n + 1)
                eng.tensor_tensor(y_lo[:, NJ + j, cols(c)], ge[:, b, :],
                                  f32(y_hi[:, NJ + j, cols(c)]), ALU.subtract
                                  ).then_inc(yb_lo_done, 1)

            split_wide(WIDE0["mix"] + 7)
            for n in range(12):
                if n == 6:
                    split_wide(WIDE0["mix"] + 8)
                    k = RING["state"]
                    eng.wait_ge(psum_full, k + 1)
                    eng.tensor_copy(st_stage[0:36, :], ps[0:36, k % BANKS, :]).then_inc(psum_free, 1)
                gelu_tile(n)
            conv_taps(CW * NJ)
            split_wide(WIDE0["mix"] + 9)

            def conv_norm_lo(c):
                for j in range(NJ):
                    eng.wait_ge(cn_silu, NJ * c + j + 1)
                    eng.tensor_tensor(y_lo[:, j, cols(c)], conv[:, j, cols(c)],
                                      f32(y_hi[:, j, cols(c)]), ALU.subtract
                                      ).then_inc(yc_lo_done, 1)

            for c in range(NC):
                for j in range(1, NJ):
                    add_square(NORM["conv", c], j)
                if c:
                    conv_norm_lo(c - 1)
                invert("conv", c)
                r = rstd("conv", c)
                if c == 0:
                    eng.wait_ge(conv_step, 2 * CW * NJ)
                for j in range(NJ):
                    eng.tensor_tensor(conv[:, j, cols(c)], conv[:, j, cols(c)], r, ALU.mult
                                      ).then_inc(cn_done, 1)
            conv_norm_lo(2)

            oc_tile = lambda m: oc[:, m, :]
            for c in range(NC):
                for m in range(KT):
                    n = RING["wout", c, m]
                    src = bank(n)
                    if c:
                        eng.wait_ge(x_lo_done, 24 + 8 * c)
                        eng.wait_ge(add_done, ADD0[NORM["pre3", c - 1] + 1])
                    eng.tensor_copy(oc[:, m, :], src).then_inc(psum_free, 1)
                    if m > 1:
                        add_square(NORM["post2", c], m - 1)
                    if m % 2:
                        v = WIDE0["mix"] + 8 + 4 * c + m // 2 + 2
                        split_wide(v)
                add_square(NORM["post2", c], KT - 1)
                invert("post2", c)
                apply("post2", c, 24 + 8 * c, oc_tile, lambda m: vec("mix_post_g", m), "pre3")
                if c < 2:
                    invert("pre3", c)

            eng.wait_ge(x_lo_done, 48)
            ffn_step(1, 0, invert_pre=("pre3", 2))
            with eng.Fori(1, NI - 1) as i:
                ffn_step(1, i)
            ffn_last(1, "post3")

            def ple_unit(c, q):
                for t in range(2):
                    n = 8 * c + 2 * q + t
                    src = bank(RING["ple", c, q, t])
                    if n >= 2:
                        eng.wait_ge(gate_sig, n - 1)
                    eng.tensor_tensor(tmp_g[:, t, :], src, rstd("pre4", c), ALU.mult
                                      ).then_inc(psum_free, 1)
                for t in range(2):
                    n = 8 * c + 2 * q + t
                    src = bank(RING["ple", c, q, 2 + t])
                    eng.wait_ge(gate_sig, n + 1)
                    eng.tensor_tensor(acc[:, 2 * q + t, cols(c)], src, tmp_s[:, t, :], ALU.mult
                                      ).then_inc(psum_free, 1)
                v = WIDE0["ple"] + 4 * c + q + 2
                if v < N_WIDE:
                    split_wide(v)

            def z_adds(c):
                for m in range(1, KT):
                    add_square(NORM["post4", c], m)

            def finish(c):
                invert("post4", c)
                apply("post4", c, None, acc_tile(c), lambda m: vec("ple_post_g", m), None)

            def stage_out(c):
                for q in range(3):
                    w, n = min(P, C - P * q), 3 * c + q
                    if n >= 2:
                        eng.wait_ge(y_out[n % 2], 16 * (n // 2))
                    for half in range(2):
                        k = RING["yT", c, 2 * q + half]
                        eng.wait_ge(psum_full, k + 1)
                        eng.tensor_copy(y_stage[0:w, n % 2, 512 * half:512 * half + 512],
                                        ps[0:w, k % BANKS, :]).then_inc(psum_free, 1)

            gain3 = behind_ffn(1, "post3", "pre4", lambda c: ple_unit(0, 0))
            for q in (1, 2, 3):
                ple_unit(0, q)
            invert("pre4", 1)
            ple_unit(1, 0)
            apply("post3", 2, 48 + 16, acc_tile(2), gain3, "pre4")
            ple_unit(1, 1)
            invert("pre4", 2)
            z_adds(0)
            ple_unit(1, 2)
            finish(0)
            ple_unit(1, 3)
            stage_out(0)
            ple_unit(2, 0)
            z_adds(1)
            ple_unit(2, 1)
            finish(1)
            ple_unit(2, 2)
            ple_unit(2, 3)
            stage_out(1)
            z_adds(2)
            finish(2)
            stage_out(2)


def lru_tile(x):
    u, r = divmod(x, 6)
    c, t = divmod(r, 2)
    return 2 * u + t, c, t


_INS = ["x_prompt", "x_sample", "cache_conv", "state_lru_conv", "state_lru_h", "p_prompt",
        "p_sample", "ffn1_pre_g", "ffn1_post_g", "ffn1_w_gu", "ffn1_w_down", "mix_pre_g",
        "mix_post_g", "w_in", "conv_w", "conv_b", "conv_norm_g", "lru_conv_w", "lru_conv_b",
        "lru_wa", "lru_ba", "lru_wx", "lru_bx", "lru_lambda", "w_out", "ffn2_pre_g",
        "ffn2_post_g", "ffn2_w_gu", "ffn2_w_down", "ple_norm_g", "ple_w_gate", "ple_w_proj",
        "ple_post_g"]
_OUTS = [("y_prompt", (1, SEQ, D)), ("y_sample", (NB, DEC, D)), ("conv_p", (1, 1, CH, NJ * P)),
         ("lconv_p", (1, 1, LH, NJ * P)), ("h_p", (1, 1, NJ * P)),
         ("conv_s", (1, NB, CH, NJ * P)), ("lconv_s", (1, NB, LH, NJ * P)),
         ("h_s", (1, NB, NJ * P))]


def kernel(**inputs):
    import numpy as _np
    import concourse.bacc as _bacc
    from concourse.bass_utils import run_bass_kernel_spmd as _run

    nc = _bacc.Bacc("TRN2", target_bir_lowering=False, num_devices=1)
    arrays, ins, outs = {}, {}, {}
    for name in _INS:
        arr = _np.ascontiguousarray(inputs[name])
        arrays[f"in_{name}_dram"] = arr
        ins[name] = nc.dram_tensor(f"in_{name}_dram", arr.shape, mybir.dt.from_np(arr.dtype),
                                   kind="ExternalInput").ap()
    for i, (name, shape) in enumerate(_OUTS):
        outs[name] = nc.dram_tensor(f"out_{i}_dram", shape, F32, kind="ExternalOutput").ap()
    build(nc, ins, outs)
    r = _run(nc, [arrays], core_ids=[0])
    return tuple(r.results[0][f"out_{i}_dram"] for i in range(len(_OUTS)))
```

```python
from contextlib import ExitStack

import concourse.bass as bass
from concourse import mybir

F32 = mybir.dt.float32
F32R = mybir.dt.float32r
ALU = mybir.AluOpType
ACT = mybir.ActivationFunctionType

P = 128
D = 1024
KT = D // P
FF = 2816
NJ = 4
PLE = 256
PT = PLE // P
SEQ, NB, DEC = 1024, 8, 4
TOK = SEQ + NB * DEC
NC = 3
C = TOK // NC
LAST = SEQ - 2 * C
CW, LW = 31, 4
CH, LH = CW - 1, LW - 1
TP = 15
EPS = 1e-6
G = 2
NI = FF // P // G
WIDE = 256
HALF = KT * WIDE // 2
BANKS = 6
STEP = NC * (2 * G + KT)

VECTORS = [("ffn1_pre_g", 8), ("ffn1_post_g", 8), ("mix_pre_g", 8), ("mix_post_g", 8),
           ("ffn2_pre_g", 8), ("ffn2_post_g", 8), ("ple_norm_g", 8), ("ple_post_g", 8),
           ("conv_b", 4), ("conv_norm_g", 4), ("lru_conv_b", 4), ("lru_ba", 4), ("lru_bx", 4),
           ("lru_lambda", 4), ("lru_conv_w", 16)]
ROW = {}
for _name, _n in VECTORS:
    ROW[_name] = sum(n for _, n in VECTORS[:len(ROW)])
NROWS = sum(n for _, n in VECTORS)


def ring_plan():
    at, n = {}, 0

    def put(*key):
        nonlocal n
        at[key if len(key) > 1 else key[0]] = n
        n += 1

    put("params")
    for c in range(NC):
        for k in range(KT):
            put("xT", c, k)
    at["ffn", 0] = n
    n += NI * STEP
    for c in range(NC):
        for t in range(4):
            put("vg", c, t)
    for s in range(2):
        put("cache", s)
    for u in (2, 3):
        for c in range(NC):
            for t in range(2):
                put("in", u, c, t)
    for x in range(NJ * NC):
        put("in", 4 + x // 6, x % 6 // 2, x % 2)
        put("conv", x // NC, x % NC)
        if x == 0:
            for s in range(3):
                put("convout", s)
    for c in range(NC):
        for t in range(2):
            put("in", 6, c, t)
    put("state")
    for c in range(NC):
        for t in range(2):
            put("in", 7, c, t)
    for c in range(NC):
        for m in range(KT):
            put("wout", c, m)
    at["ffn", 1] = n
    n += NI * STEP
    for c in range(NC):
        for k in range(PT):
            put("pT", c, k)
    for c in range(NC):
        for q in range(4):
            for t in range(4):
                put("ple", c, q, t)
            if (c, q) in ((1, 3), (2, 3)):
                for s in range(6):
                    put("yT", c - 1, s)
    for s in range(6):
        put("yT", 2, s)
    return at, n


NORMS = ([("pre1", c, KT) for c in range(NC)]
         + [("post1", 0, KT), ("post1", 1, KT), ("pre2", 0, KT), ("post1", 2, KT),
            ("pre2", 1, KT), ("pre2", 2, KT)]
         + [("conv", c, NJ) for c in range(NC)]
         + [(n, c, KT) for c in range(NC) for n in ("post2", "pre3")]
         + [("post3", 0, KT), ("post3", 1, KT), ("pre4", 0, KT), ("post3", 2, KT),
            ("pre4", 1, KT), ("pre4", 2, KT)]
         + [("post4", c, KT) for c in range(NC)])
NORM = {(n, c): i for i, (n, c, _) in enumerate(NORMS)}
TILES = [t for _, _, t in NORMS]
SQ0 = [sum(TILES[:i]) for i in range(len(TILES) + 1)]
ADD0 = [sum(t - 1 for t in TILES[:i]) for i in range(len(TILES) + 1)]


def aux_plan():
    at, n = {}, 0
    first = NORM["conv", 0]
    for i in range(first):
        at["norm", i] = n
        n += 1
    for x in range(4 * NC):
        for which in "ri":
            at[which, x] = n
            n += 1
    for i in range(first, len(NORMS)):
        at["norm", i] = n
        n += 1
    return at


RING, RING_N = ring_plan()
AUX = aux_plan()
WIDE0 = {"ffn1": 0, "mix": 2 * NI, "ffn2": 2 * NI + 8 + 4 * NC, "ple": 4 * NI + 8 + 4 * NC}
N_WIDE = WIDE0["ple"] + 4 * NC


def cols(c):
    return slice(C * c, C * c + C)


def build(nc, a, out):
    ctx = ExitStack()
    with ctx:
        base = (nc.sbuf_base + 63) // 64 * 64
        at = [base]

        def place(name, shape, dt=F32, offset=None):
            size = 4
            for s in shape[1:]:
                size *= s
            if offset is None:
                offset = at[0]
                at[0] += (size + 31) // 32 * 32
            t = nc.alloc_sbuf_tensor_at(name, [P] + list(shape[1:]), dt, offset=offset)
            return t, offset, offset + (size + 31) // 32 * 32

        def tile(name, shape, dt=F32):
            return place(name, shape, dt)[0]

        x_hi = tile("x_hi", [P, KT, TOK], F32R)
        x_lo = tile("x_lo", [P, KT, TOK], F32R)
        w_hi = [tile(f"w_hi{s}", [P, KT * WIDE], F32R) for s in range(2)]
        w_lo = [tile(f"w_lo{s}", [P, KT * WIDE], F32R) for s in range(2)]
        raw = tile("raw", [P, KT * WIDE])
        rstd_pre = tile("rstd_pre", [P, TOK])
        rstd_post, norm_at, _ = place("rstd_post", [P, 2, C])
        ssum = tile("ssum", [P, C])
        std = tile("std", [P, C])
        sq, sq_at, _ = place("sq", [P, 2, C])
        ident = tile("ident", [P, P])
        ones = tile("ones", [P, P])
        params = tile("params", [P, 3 * P])
        half_g = tile("half_g", [P, 2 * KT])
        eps_t = tile("eps_t", [P, 1])
        sp = tile("sp", [P, 8, NJ])
        st_out = tile("st_out", [P, NJ, 36])
        pool0 = at[0]

        acc = tile("acc", [P, KT, TOK])
        a_hi = tile("a_hi", [P, G, TOK], F32R)
        a_lo = tile("a_lo", [P, G, TOK], F32R)
        wd_hi, wd_at, _ = place("wd_hi", [P, G * D], F32R)
        wd_lo = tile("wd_lo", [P, G * D], F32R)
        rawd, rawd_at, _ = place("rawd", [P, G * D])
        tmp_g, tmp_at, _ = place("tmp_g", [P, 2, C])
        tmp_u = tile("tmp_u", [P, 2, C])
        tmp_s = tile("tmp_s", [P, 2, C])
        tmp_a = tile("tmp_a", [P, 2, C])
        ffn_end = at[0]
        x_in, _, _ = place("x_in", [P, 3 * NC, D], offset=pool0)
        rows = place("rows", [P, 3 * P], offset=wd_at)[0]
        st_rows = place("st_rows", [P, NJ * P], offset=wd_at + 4 * 3 * P)[0]
        p_in = place("p_in", [P, 3 * NC, PLE], offset=tmp_at)[0]
        y_stage = place("y_stage", [P, 2, D], offset=rawd_at)[0]

        at[0] = pool0
        y_hi, yh_at, _ = place("y_hi", [P, KT, TOK], F32R)
        y_lo, yl_at, _ = place("y_lo", [P, KT, TOK], F32R)
        gp, g_at, _ = place("gp", [P, NJ, CH + SEQ])
        mix_end = at[0]
        gs, _, e = place("gs", [P, NJ, NB, CH + DEC], offset=norm_at)
        assert e <= sq_at
        assert max(ffn_end, mix_end) <= nc.sbuf_usable_end, (ffn_end, mix_end, nc.sbuf_usable_end)
        row = 4 * TOK
        conv = place("conv", [P, NJ, TOK], offset=yl_at)[0]
        hs = place("hs", [P, NJ, TOK], offset=yl_at + 4 * row)[0]
        cache_in = place("cache_in", [P, 2, NJ * P], offset=yl_at + 4 * row)[0]
        gs_new = place("gs_new", [P, NJ, NB * CH], offset=yl_at + 4 * row)[0]
        gate_raw = place("gate_raw", [P, 2, NJ, P], offset=yl_at + 4 * row + 4096)[0]
        cv_stage = place("cv_stage", [P, 3, NJ * P], offset=yl_at + 6 * row)[0]
        ux_p, _, e = place("ux_p", [P, 2, LH + C], offset=yh_at)
        ux_s, _, e = place("ux_s", [P, 2, NB, LH + DEC], offset=e)
        xc_hi, _, e = place("xc_hi", [P, 2, C], F32R, offset=e)
        xc_lo, _, e = place("xc_lo", [P, 2, C], F32R, offset=e)
        diag, _, e = place("diag", [P, TP, P], offset=e)
        assert e <= yh_at + 4 * row
        gw_hi, _, e = place("gw_hi", [P, 2, NJ, P], F32R, offset=yh_at + 4 * row)
        gw_lo, _, e = place("gw_lo", [P, 2, NJ, P], F32R, offset=e)
        assert e <= yh_at + 6 * row
        xc = place("xc", [P, 2, C], offset=yh_at + 6 * row)[0]
        lru_r = place("lru_r", [P, C], offset=yh_at + 6 * row + 8 * C)[0]
        lru_i = place("lru_i", [P, C], offset=yh_at + 6 * row + 12 * C)[0]
        lru_a = place("lru_a", [P, C], offset=yh_at + 6 * row + 16 * C)[0]
        lru_q = place("lru_q", [P, C], offset=yh_at + 6 * row + 20 * C)[0]
        glu = place("glu", [P, 2, C], offset=yl_at + 6 * row)[0]
        oc, _, e = place("oc", [P, KT, C], offset=g_at)
        st_stage, _, e = place("st_stage", [P, NJ * P], offset=e)
        ge, _, e = place("ge", [P, 2, C], offset=e)
        assert e <= mix_end

        ps = ctx.enter_context(nc.psum_tensor("ps", [P, BANKS, 512], F32))
        ps_aux = ctx.enter_context(nc.psum_tensor("ps_aux", [P, 2, 512], F32))

        def f32(t):
            return t.bitcast(F32)

        def vec(name, k):
            return params[:, ROW[name] + k:ROW[name] + k + 1]

        def conv_w(tap, j):
            n = P + tap * NJ + j
            return params[:, n:n + 1]

        def st_in(j, r0, r1):
            return params[:, 2 * P + 32 * j + r0:2 * P + 32 * j + r1]

        def sem(name):
            return ctx.enter_context(nc.semaphore(name))

        const_ready = sem("const_ready")
        rows_in = sem("rows_in")
        x_read = [sem(f"x_read{c}") for c in range(NC)]
        psum_full = sem("psum_full")
        psum_free = sem("psum_free")
        aux_full = sem("aux_full")
        aux_free = sem("aux_free")
        raw_in = [sem(f"raw_in{h}") for h in range(2)]
        wide_hi = sem("wide_hi")
        wide_lo = sem("wide_lo")
        rawd_in = sem("rawd_in")
        down_hi = sem("down_hi")
        down_lo = sem("down_lo")
        silu_done = sem("silu_done")
        prod_done = sem("prod_done")
        a_hi_done = sem("a_hi_done")
        a_lo_done = sem("a_lo_done")
        sq_done = sem("sq_done")
        add_done = sem("add_done")
        rstd_done = sem("rstd_done")
        x_new = sem("x_new")
        x_hi_done = sem("x_hi_done")
        x_lo_done = sem("x_lo_done")
        half_done = sem("half_done")
        sp_act = sem("sp_act")
        dve_own = sem("dve_own")
        act_own = sem("act_own")
        sig_done = sem("sig_done")
        glu_done = sem("glu_done")
        cache_read = sem("cache_read")
        gate_in = sem("gate_in")
        gate_zero = sem("gate_zero")
        gw_hi_done = sem("gw_hi_done")
        gw_lo_done = sem("gw_lo_done")
        gs_new_done = sem("gs_new_done")
        conv_step = sem("conv_step")
        diag_done = sem("diag_done")
        diag_free = sem("diag_free")
        xc_done = sem("xc_done")
        xc_hi_done = sem("xc_hi_done")
        xc_lo_done = sem("xc_lo_done")
        lru_act = sem("lru_act")
        lru_gain = sem("lru_gain")
        lru_sqrt = sem("lru_sqrt")
        scan_done = sem("scan_done")
        gelu_done = sem("gelu_done")
        yb_done = sem("yb_done")
        yb_hi_done = sem("yb_hi_done")
        yb_lo_done = sem("yb_lo_done")
        cn_done = sem("cn_done")
        cn_silu = sem("cn_silu")
        yc_lo_done = sem("yc_lo_done")
        conv_out = sem("conv_out")
        states_out = sem("states_out")
        p_read = sem("p_read")
        pt_hi = sem("pt_hi")
        gate_sig = sem("gate_sig")
        y_fin = sem("y_fin")
        y_out = [sem(f"y_out{s}") for s in range(2)]

        block = ctx.enter_context(nc.Block())

        gu_src = [a[f"ffn{f}_w_gu"][0].rearrange("(k p) (s i n) -> s i p k n", p=P, s=2, n=WIDE)
                  for f in (1, 2)]
        down_src = [a[f"ffn{f}_w_down"][0].rearrange("(i t p) n -> i p t n", t=G, p=P)
                    for f in (1, 2)]
        win_src = a["w_in"][0].rearrange("(k p) (u n) -> u p k n", p=P, n=WIDE)
        wout_src = a["w_out"][0].rearrange("(k p) (u n) -> u p k n", p=P, n=WIDE)
        pg_src = a["ple_w_gate"][0].rearrange("(k p) (u n) -> u p k n", p=P, n=WIDE)
        IN_UNITS = [0, 2, 1, 3, 4, 5, 6, 7]

        def wide_src(v):
            if v < WIDE0["mix"]:
                return gu_src[0][v % 2, v // 2]
            if v < WIDE0["mix"] + 8:
                return win_src[IN_UNITS[v - WIDE0["mix"]]]
            if v < WIDE0["ffn2"]:
                return wout_src[(v - WIDE0["mix"]) % 4]
            if v < WIDE0["ple"]:
                v -= WIDE0["ffn2"]
                return gu_src[1][v % 2, v // 2]
            return pg_src[(v - WIDE0["ple"]) % 4]

        def wide_gain(v):
            if v < WIDE0["mix"]:
                return "ffn1_pre_g"
            if v < WIDE0["mix"] + 8:
                return "mix_pre_g"
            if v < WIDE0["ffn2"]:
                return None
            return "ffn2_pre_g" if v < WIDE0["ple"] else "ple_norm_g"

        def wide_last_use(v):
            if v < WIDE0["mix"] or WIDE0["ffn2"] <= v < WIDE0["ple"]:
                f = int(v >= WIDE0["ffn2"])
                v -= WIDE0["ffn2"] if f else 0
                return RING["ffn", f] + STEP * (v // 2) + 4 * NC - 2 + 2 * (v % 2)
            if v < WIDE0["mix"] + 8:
                u = v - WIDE0["mix"]
                return RING["vg", 2, 3] + 1 if u < 2 else RING["in", u, 2, 1] + 1
            if v < WIDE0["ffn2"]:
                c, q = divmod(v - WIDE0["mix"] - 8, 4)
                return RING["wout", c, 2 * q + 1] + 1
            c, q = divmod(v - WIDE0["ple"], 4)
            return RING["ple", c, q, 3] + 1

        @block.sync
        def _(sp_eng):
            eng = sp_eng

            def load_wide(v, src=None):
                src = wide_src(v) if src is None else src
                for h in range(2):
                    if not isinstance(v, int) or v > 0:
                        eng.wait_ge(wide_lo, v * 2 + (h - 1))
                    eng.dma_start(raw[:, h * HALF:(h + 1) * HALF].rearrange(
                        "p (k n) -> p k n", n=WIDE), src[:, 4 * h:4 * h + 4]
                        ).then_inc(raw_in[h], 16)

            def load_down(d, src):
                if not isinstance(d, int) or d > 0:
                    eng.wait_ge(down_lo, d)
                eng.dma_start(rawd[:, :].rearrange("p (t n) -> p t n", t=G), src).then_inc(rawd_in, 16)

            def ffn_loads(f):
                v0, d0 = WIDE0[f"ffn{f + 1}"], NI * f
                load_down(d0, down_src[f][0])
                load_wide(v0 + 2)
                load_wide(v0 + 3)
                with eng.Fori(1, NI - 1) as i:
                    load_down(i + d0, down_src[f][i])
                    load_wide(i * 2 + (v0 + 2), gu_src[f][0, i + 1])
                    load_wide(i * 2 + (v0 + 3), gu_src[f][1, i + 1])
                load_down(d0 + NI - 1, down_src[f][NI - 1])
                load_wide(v0 + 2 * NI)
                load_wide(v0 + 2 * NI + 1)

            def store(n):
                c, q = divmod(n, 3)
                w, r0 = min(P, C - P * q), C * c + P * q
                eng.wait_ge(psum_free, RING["yT", c, 2 * q + 1] + 1)
                if n == 8:
                    w = LAST - 2 * P
                    eng.dma_start(out["y_sample"].rearrange("b t n -> (b t) n"),
                                  y_stage[w:w + NB * DEC, n % 2, :]).then_inc(y_out[n % 2], 16)
                eng.dma_start(out["y_prompt"][0, r0:r0 + w, :], y_stage[0:w, n % 2, :]
                              ).then_inc(y_out[n % 2], 16)

            for name, n in VECTORS:
                src = a[name] if name != "lru_conv_w" else a[name][0]
                eng.dma_start(rows[ROW[name]:ROW[name] + n, 0:P],
                              src.rearrange("a (k p) -> (a k) p", p=P)).then_inc(rows_in, 16)
            eng.dma_start(rows[0:CW * NJ, P:2 * P],
                          a["conv_w"][0].rearrange("a (k p) -> (a k) p", p=P)).then_inc(rows_in, 16)
            eng.dma_start(st_rows[0:NB * LH, :],
                          a["state_lru_conv"][0].rearrange("b w n -> (b w) n")).then_inc(rows_in, 16)
            eng.dma_start(st_rows[NB * LH:NB * LH + NB, :], a["state_lru_h"][0]).then_inc(rows_in, 16)
            load_wide(0)
            load_wide(1)
            ffn_loads(0)
            eng.wait_ge(psum_full, RING["ffn", 0] + NI * STEP)
            for s in range(2):
                eng.dma_start(cache_in[0:4 * CH, s, :],
                              a["cache_conv"][0, 4 * s:4 * s + 4].rearrange("b w n -> (b w) n")
                              ).then_inc(cache_read, 16)
            eng.wait_ge(gate_zero, 1)
            for g, name in enumerate(("lru_wa", "lru_wx")):
                w = a[name][0].rearrange("(j two) r n -> two r j n", two=2)
                for half in range(2):
                    eng.dma_start(gate_raw[64 * half:64 * half + 64, g, :, 64 * half:64 * half + 64],
                                  w[half]).then_inc(gate_in, 16)
            for v in range(WIDE0["mix"] + 2, WIDE0["mix"] + 6):
                load_wide(v)
            eng.wait_ge(psum_free, RING["convout", 2] + 1)
            eng.dma_start(out["conv_p"][0, 0], cv_stage[0:CH, 0, :]).then_inc(conv_out, 16)
            for s in range(2):
                eng.dma_start(out["conv_s"][0, 4 * s:4 * s + 4].rearrange("b w n -> (b w) n"),
                              cv_stage[0:4 * CH, 1 + s, :]).then_inc(conv_out, 16)
            for v in range(WIDE0["mix"] + 6, WIDE0["mix"] + 9):
                load_wide(v)
            eng.wait_ge(psum_free, RING["state"] + 1)
            for dst, r in ((out["lconv_p"][0, 0], 0),
                           (out["lconv_s"][0].rearrange("b w n -> (b w) n"), LH),
                           (out["h_p"][0], LH + NB * LH), (out["h_s"][0], LH + NB * LH + 1)):
                eng.dma_start(dst, st_stage[r:r + dst.shape[0], :]).then_inc(states_out, 16)
            for v in range(WIDE0["mix"] + 9, WIDE0["ffn2"] + 2):
                load_wide(v)
            eng.wait_ge(psum_full, RING["ffn", 1])
            eng.wait_ge(x_lo_done, 24 * 2)
            ffn_loads(1)
            load_down(2 * NI, a["ple_w_proj"][0].rearrange("(t p) n -> p t n", p=P))
            eng.wait_ge(a_lo_done, 2 * NI * NC * G)
            for c in range(NC):
                for q in range(3):
                    n, r0 = (P, C * c + P * q) if q < 2 else (C - 2 * P, C * c + 2 * P)
                    if c == 2 and q == 2:
                        n = LAST - 2 * P
                        eng.dma_start(p_in[n:n + NB * DEC, 8, :],
                                      a["p_sample"][0].rearrange("b t n -> (b t) n")
                                      ).then_inc(p_read, 16)
                    eng.dma_start(p_in[0:n, 3 * c + q, :], a["p_prompt"][0, 0, r0:r0 + n, :]
                                  ).then_inc(p_read, 16)
            for v in range(WIDE0["ple"] + 2, N_WIDE - 1):
                load_wide(v)
            for n in range(3):
                store(n)
            load_wide(N_WIDE - 1)
            for n in range(3, 9):
                store(n)
            for s in range(2):
                eng.wait_ge(y_out[s], (96, 64)[s])
            eng.wait_ge(conv_out, 48)
            eng.wait_ge(states_out, 64)

        @block.gpsimd
        def _(eng):
            eng.memset(ident[:, :], 0.0).then_inc(const_ready, 1)
            eng.memset(ones[:, :], 1.0).then_inc(const_ready, 1)
            eng.memset(eps_t[:, :], EPS).then_inc(const_ready, 1)
            eng.wait_ge(const_ready, 3)
            eng.affine_select(out=ident[:, :], in_=ident[:, :], compare_op=ALU.not_equal, fill=1.0,
                              base=0, pattern=[[-1, P]], channel_multiplier=1
                              ).then_inc(const_ready, 1)

        @block.tensor
        def _(eng):
            def bank(n, ncols=C):
                if n >= BANKS:
                    eng.wait_ge(psum_free, n - BANKS + 1)
                return ps[:, n % BANKS, 0:ncols]

            def bank_at(base_n, off):
                eng.wait_ge(psum_free, base_n + (off - BANKS + 1))

            def passes(dst, wh, wl, xh, xl, first, last):
                eng.matmul(dst, wl, xh, start=first, stop=False)
                eng.matmul(dst, wh, xl, start=False, stop=False)
                return eng.matmul(dst, wh, xh, start=False, stop=last)

            def wide(s, k, t):
                sl = slice(k * WIDE + t * P, k * WIDE + t * P + P)
                return w_hi[s][:, sl], w_lo[s][:, sl]

            def tile_product(dst, s, t, c):
                for k in range(KT):
                    wh, wl = wide(s, k, t)
                    mm = passes(dst, wh, wl, x_hi[:, k, cols(c)], x_lo[:, k, cols(c)],
                                k == 0, k == KT - 1)
                mm.then_inc(psum_full, 1)

            def batch_products(n0, specs, c, x0):
                dsts = [bank(n0 + i) for i in range(len(specs))]
                for k in range(KT):
                    if x0 is None:
                        eng.wait_ge(psum_free, RING["xT", c, k] + 1)
                    else:
                        eng.wait_ge(x_lo_done, x0 + 8 * c + k + 1)
                    for dst, (s, t) in zip(dsts, specs):
                        wh, wl = wide(s, k, t)
                        mm = passes(dst, wh, wl, x_hi[:, k, cols(c)], x_lo[:, k, cols(c)],
                                    k == 0, k == KT - 1)
                        if k == KT - 1:
                            mm.then_inc(psum_full, 1)

            def norm_sum(name, c):
                i = NORM[name, c]
                n = AUX["norm", i]
                eng.wait_ge(add_done, ADD0[i + 1])
                if n >= 2:
                    eng.wait_ge(aux_free, n - 1)
                eng.matmul(ps_aux[:, n % 2, 0:C], ones[:, :], ssum[:, :], start=True, stop=True
                           ).then_inc(aux_full, 1)

            def down_products(c, n_of, a_count, wait_bank):
                eng.wait_ge(a_lo_done, a_count)
                for m in range(KT):
                    wait_bank(m)
                    dst = ps[:, n_of(m) % BANKS, 0:C]
                    for t in range(G):
                        sl = slice(t * D + m * P, t * D + m * P + P)
                        mm = passes(dst, wd_hi[:, sl], wd_lo[:, sl], a_hi[:, t, cols(c)],
                                    a_lo[:, t, cols(c)], t == 0, t == G - 1)
                    mm.then_inc(psum_full, 1)

            SPECS = [(0, 0), (0, 1), (1, 0), (1, 1)]

            def ffn_step(f, i, first=False, x0=None, hook=None, mid_down=None):
                R, V, Q, E = (RING["ffn", f], WIDE0[f"ffn{f + 1}"], NI * NC * G * f, NI * f)
                eng.wait_ge(wide_lo, i * 4 + (2 * V + 4))
                for c in range(NC):
                    if first:
                        batch_products(R + 4 * c, SPECS, c, x0)
                        if hook:
                            hook(c)
                        continue
                    for t, (s, h) in enumerate(SPECS):
                        off = 4 * c + t
                        bank_at(i * STEP, R + off)
                        tile_product(ps[:, (R + off) % BANKS, 0:C], s, h, c)
                eng.wait_ge(down_lo, i + (E + 1))
                for c in range(NC):
                    off = 4 * NC + KT * c
                    down_products(c, lambda m: R + off + m, i * (NC * G) + (Q + 2 * c + 2),
                                  lambda m: bank_at(i * STEP, R + off + m))
                    if mid_down:
                        mid_down(c)

            def ffn(f, x0, hook, mid_down):
                ffn_step(f, 0, first=True, x0=x0, hook=hook)
                with eng.Fori(1, NI - 1) as i:
                    ffn_step(f, i)
                ffn_step(f, NI - 1, mid_down=mid_down)

            eng.wait_ge(const_ready, 4)
            eng.wait_ge(rows_in, 16 * (len(VECTORS) + 3))
            dst = bank(0, 512)
            eng.transpose(dst[:, 0:NROWS], rows[0:NROWS, 0:P], ident[0:NROWS, 0:NROWS])
            eng.transpose(dst[:, P:P + CW * NJ], rows[0:CW * NJ, P:2 * P],
                          ident[0:CW * NJ, 0:CW * NJ])
            for j in range(NJ):
                mm = eng.transpose(dst[:, 2 * P + 32 * j:2 * P + 32 * j + 32],
                                   st_rows[0:32, j * P:j * P + P], ident[0:32, 0:32])
            mm.then_inc(psum_full, 1)

            def to_features(src, n, c, k):
                dst = bank(n)
                for q in range(3):
                    w = min(P, C - P * q)
                    mm = eng.transpose(dst[:, P * q:P * q + w],
                                       src[0:w, 3 * c + q, k * P:k * P + P], ident[0:w, 0:w])
                mm.then_inc(psum_full, 1)

            for c in range(NC):
                eng.wait_ge(x_read[c], 48 + 16 * (c == 2))
                for k in range(KT):
                    to_features(x_in, RING["xT", c, k], c, k)
                norm_sum("pre1", c)

            def down_norms(name):
                def mid(c):
                    if c >= 1:
                        norm_sum(name, c - 1)
                return mid

            ffn(0, None, None, down_norms("post1"))

            eng.wait_ge(wide_lo, 2 * (WIDE0["mix"] + 2))
            for c in range(NC):
                batch_products(RING["vg", c, 0], [(0, 0), (0, 1), (1, 0), (1, 1)], c, 0)
                norm_sum("pre2", c)
                if c == 0:
                    norm_sum("post1", 2)
            eng.wait_ge(cache_read, 32)
            for s in range(2):
                dst = bank(RING["cache", s], 4 * 4 * CH)
                for j in range(NJ):
                    mm = eng.transpose(dst[:, j * 4 * CH:(j + 1) * 4 * CH],
                                       cache_in[0:4 * CH, s, j * P:j * P + P],
                                       ident[0:4 * CH, 0:4 * CH])
                mm.then_inc(psum_full, 1)

            def lru_gates(x):
                j, c, t = lru_tile(x)
                eng.wait_ge(xc_lo_done, x + 1)
                for g, which in enumerate("ri"):
                    n = AUX[which, x]
                    eng.wait_ge(aux_free, n - 1)
                    passes(ps_aux[:, n % 2, 0:C], gw_hi[:, g, j, :], gw_lo[:, g, j, :],
                           xc_hi[:, x % 2, :], xc_lo[:, x % 2, :], True, True
                           ).then_inc(aux_full, 1)

            def in_unit(u, behind=None):
                eng.wait_ge(wide_lo, 2 * (WIDE0["mix"] + u + 1))
                for c in range(NC):
                    for t in range(2):
                        tile_product(bank(RING["in", u, c, t]), u % 2, t, c)
                        if behind:
                            behind(2 * c + t)

            def conv_group(j, c):
                dst = bank(RING["conv", j, c])
                w = C if c < 2 else LAST
                eng.wait_ge(glu_done, 6 * (j // 2 + 1))
                for tap in range(TP if c == 2 else 0):
                    eng.matmul(dst[:, w:C].rearrange("p (b t) -> p b t", b=NB), diag[:, tap, :],
                               gs[:, j, :, tap:tap + DEC], start=tap == 0, stop=tap == TP - 1)
                for tap in range(TP):
                    if c == 0:
                        eng.wait_ge(diag_done, TP * j + tap + 1)
                    at0 = C * c + tap
                    mm = eng.matmul(dst[:, 0:w], diag[:, tap, :], gp[:, j, at0:at0 + w],
                                    start=tap == 0, stop=tap == TP - 1)
                    if c == 2 and tap < TP - 1:
                        mm.then_inc(diag_free, 1)
                mm.then_inc(psum_full, 1)

            def conv_states():
                eng.wait_ge(gs_new_done, 1)
                for s in range(3):
                    n = RING["convout", s]
                    eng.wait_ge(psum_free, n - BANKS + 1)
                    for j in range(NJ):
                        src = gp[:, j, SEQ:SEQ + CH] if s == 0 else \
                            gs_new[:, j, (4 * s - 4) * CH:4 * s * CH]
                        w = CH if s == 0 else 4 * CH
                        mm = eng.transpose(ps[0:w, n % BANKS, j * P:j * P + P], src, ident[:, :])
                    mm.then_inc(psum_full, 1)

            in_unit(2)
            in_unit(3)
            for x in range(NJ * NC):
                j, c, t = lru_tile(x)
                u = 4 + x // 6
                if x % 6 == 0:
                    eng.wait_ge(wide_lo, 2 * (WIDE0["mix"] + u + 1))
                tile_product(bank(RING["in", u, c, t]), u % 2, t, c)
                conv_group(x // NC, x % NC)
                if x == 0:
                    conv_states()
                    eng.wait_ge(gw_lo_done, 1)
                lru_gates(x)

            def gelu_hook(n):
                if n in (3, 7, 11):
                    norm_sum("conv", n // 4)

            in_unit(6, gelu_hook)
            eng.wait_ge(scan_done, 12)
            n = RING["state"]
            eng.wait_ge(psum_free, n - BANKS + 1)
            for j in range(NJ):
                mm = eng.transpose(ps[0:36, n % BANKS, j * P:j * P + P], st_out[:, j, :], ident[:, :])
            mm.then_inc(psum_full, 1)
            in_unit(7, lambda n: gelu_hook(n + 6))

            def out_unit(c, q):
                v = WIDE0["mix"] + 8 + 4 * c + q
                eng.wait_ge(wide_lo, 2 * (v + 1))
                if q == 0:
                    eng.wait_ge(yc_lo_done, NJ * (c + 1))
                    eng.wait_ge(yb_lo_done, 12)
                for t in range(2):
                    dst = bank(RING["wout", c, 2 * q + t])
                    for k in range(KT):
                        wh, wl = wide(v % 2, k, t)
                        mm = passes(dst, wh, wl, y_hi[:, k, cols(c)], y_lo[:, k, cols(c)],
                                    k == 0, k == KT - 1)
                    mm.then_inc(psum_full, 1)

            for c in range(NC):
                out_unit(c, 0)
                if c > 0:
                    norm_sum("post2", c - 1)
                out_unit(c, 1)
                if c > 0:
                    norm_sum("pre3", c - 1)
                out_unit(c, 2)
                out_unit(c, 3)
            norm_sum("post2", 2)

            ffn(1, 24, lambda c: c == 0 and norm_sum("pre3", 2), down_norms("post3"))

            eng.wait_ge(p_read, 16 * 10)
            for c in range(NC):
                for k in range(PT):
                    to_features(p_in, RING["pT", c, k], c, k)

            def ple_unit(c, q):
                v = WIDE0["ple"] + 4 * c + q
                eng.wait_ge(wide_lo, 2 * (v + 1))
                if q == 0:
                    batch_products(RING["ple", c, 0, 0], [(v % 2, 0), (v % 2, 1)], c, 48)
                else:
                    for t in range(2):
                        tile_product(bank(RING["ple", c, q, t]), v % 2, t, c)
                if (c, q) == (0, 0):
                    eng.wait_ge(down_lo, 2 * NI + 1)
                    eng.wait_ge(psum_free, RING["pT", 2, 1] + 1)
                for t in range(2):
                    dst = bank(RING["ple", c, q, 2 + t])
                    for k in range(PT):
                        sl = slice(k * D + (2 * q + t) * P, k * D + (2 * q + t) * P + P)
                        mm = passes(dst, wd_hi[:, sl], wd_lo[:, sl], a_hi[:, k, cols(c)],
                                    a_lo[:, k, cols(c)], k == 0, k == PT - 1)
                    mm.then_inc(psum_full, 1)

            def to_tokens(c):
                for q in range(3):
                    w = min(P, C - P * q)
                    for half in range(2):
                        n = RING["yT", c, 2 * q + half]
                        eng.wait_ge(psum_free, n - BANKS + 1)
                        for k in range(4):
                            kk = 4 * half + k
                            eng.wait_ge(y_fin, KT * c + kk + 1)
                            mm = eng.transpose(ps[0:w, n % BANKS, k * P:k * P + P],
                                               acc[:, kk, C * c + P * q:C * c + P * q + w],
                                               ident[:, :])
                        mm.then_inc(psum_full, 1)

            ple_unit(0, 0)
            norm_sum("pre4", 0)
            norm_sum("post3", 2)
            for q in (1, 2, 3):
                ple_unit(0, q)
            ple_unit(1, 0)
            norm_sum("pre4", 1)
            ple_unit(1, 1)
            norm_sum("pre4", 2)
            ple_unit(1, 2)
            norm_sum("post4", 0)
            ple_unit(1, 3)
            to_tokens(0)
            for q in (0, 1):
                ple_unit(2, q)
            norm_sum("post4", 1)
            for q in (2, 3):
                ple_unit(2, q)
            to_tokens(1)
            norm_sum("post4", 2)
            to_tokens(2)

        @block.scalar
        def _(eng):
            own = [0]

            def done(ins):
                own[0] += 1
                ins.then_inc(act_own, 1)
                eng.wait_ge(act_own, own[0])

            def split_half(v, h, s=None, gain=None, last_use=None):
                if s is None:
                    s, gain = v % 2, wide_gain(v)
                if last_use is None and v >= 2:
                    last_use = wide_last_use(v - 2)
                if last_use is not None and h == 0:
                    eng.wait_ge(psum_full, last_use)
                eng.wait_ge(raw_in[h], v * 16 + 16)
                if gain is None:
                    sl = slice(h * HALF, (h + 1) * HALF)
                    eng.activation(w_hi[s][:, sl], raw[:, sl], ACT.Copy).then_inc(wide_hi, 1)
                    return
                for k in range(4 * h, 4 * h + 4):
                    sl = slice(k * WIDE, (k + 1) * WIDE)
                    ins = eng.activation(w_hi[s][:, sl], raw[:, sl], ACT.Copy, scale=vec(gain, k))
                ins.then_inc(wide_hi, 1)

            def split_wide(v):
                for h in range(2):
                    split_half(v, h)

            def split_down(d, last_use=None):
                if last_use is not None:
                    eng.wait_ge(psum_full, last_use)
                eng.wait_ge(rawd_in, d * 16 + 16)
                eng.activation(wd_hi[:, :], rawd[:, :], ACT.Copy).then_inc(down_hi, 1)

            def square(i, m, src, src_sem=None, count=None):
                if src_sem is not None:
                    eng.wait_ge(src_sem, count)
                if m == 0:
                    if i > 0:
                        eng.wait_ge(aux_full, AUX["norm", i - 1] + 1)
                    dst = ssum[:, :]
                else:
                    if ADD0[i] + max(0, m - 2) > 0:
                        eng.wait_ge(add_done, ADD0[i] + max(0, m - 2))
                    dst = sq[:, m % 2, :]
                eng.activation(dst, src, ACT.Square).then_inc(sq_done, 1)

            def root(name, c):
                i = NORM[name, c]
                n = AUX["norm", i]
                width = P * TILES[i]
                eng.wait_ge(aux_full, n + 1)
                if i > 0:
                    eng.wait_ge(rstd_done, i)
                eng.activation(std[:, :], ps_aux[:, n % 2, 0:C], ACT.Sqrt, scale=1.0 / width,
                               bias=eps_t[:, :]).then_inc(aux_free, 1)

            def squares(name, c, src, sem_, count0):
                i = NORM[name, c]
                for m in range(TILES[i]):
                    square(i, m, src(m), sem_, count0 + m + 1)

            def apply(name, c, x0, src):
                i = NORM[name, c]
                for m in range(KT):
                    eng.wait_ge(x_new, x0 + m + 1)
                    eng.activation(x_hi[:, m, cols(c)], src(m), ACT.Copy).then_inc(x_hi_done, 1)
                    square(i, m, src(m))

            def silu(f, i, c, h):
                R, Q = RING["ffn", f], NI * NC * G * f
                q, n = NC * G * i + (Q + 2 * c + h), STEP * i + (R + 4 * c + h)
                eng.wait_ge(psum_free, n + 1)
                if f or not isinstance(i, int) or i or c:
                    eng.wait_ge(prod_done, q - 1)
                eng.activation(tmp_s[:, h, :], tmp_g[:, h, :], ACT.Silu).then_inc(silu_done, 1)

            def hidden_hi(f, i, c, h):
                R, Q = RING["ffn", f], NI * NC * G * f
                eng.wait_ge(prod_done, NC * G * i + (Q + 2 * c + h + 1))
                if not isinstance(i, int) or i:
                    eng.wait_ge(psum_full, STEP * i + (R - STEP + 4 * NC + KT * (c + 1)))
                eng.activation(a_hi[:, h, cols(c)], tmp_a[:, h, :], ACT.Copy).then_inc(a_hi_done, 1)

            def ffn_step(f, i, last=False, root0=None):
                R, V, E = RING["ffn", f], WIDE0[f"ffn{f + 1}"], NI * f
                gain = f"ffn{f + 1}_pre_g"

                def next_half(s, h):
                    if last:
                        split_half(V + 2 * NI + s, h)
                    else:
                        split_half(i * 2 + (V + 2 + s), h, s, gain,
                                   i * STEP + (R + 4 * NC - 2 + 2 * s))

                for c in range(NC):
                    silu(f, i, c, 0)
                    silu(f, i, c, 1)
                    if c == 2:
                        next_half(0, 0)
                    hidden_hi(f, i, c, 0)
                    if c == 2:
                        next_half(0, 1)
                    hidden_hi(f, i, c, 1)
                    if c == 0:
                        if root0:
                            root(*root0)
                        split_down(i + E, None if isinstance(i, int) and i == 0 else i * STEP + R)
                for h in range(2):
                    next_half(1, h)

            def ffn(f):
                ffn_step(f, 0)
                with eng.Fori(1, NI - 1) as i:
                    ffn_step(f, i)
                ffn_step(f, NI - 1, last=True)

            for c in range(NC):
                for q in range(3):
                    n, r0 = (P, C * c + P * q) if q < 2 else (C - 2 * P, C * c + 2 * P)
                    if c == 2 and q == 2:
                        n = LAST - 2 * P
                        eng.dma_start(x_in[n:n + NB * DEC, 8, :],
                                      a["x_sample"].rearrange("b t n -> (b t) n")
                                      ).then_inc(x_read[c], 16)
                    eng.dma_start(x_in[0:n, 3 * c + q, :], a["x_prompt"][0, r0:r0 + n, :]
                                  ).then_inc(x_read[c], 16)
            eng.wait_ge(const_ready, 4)
            eng.wait_ge(half_done, 1)
            eng.activation(sp[:, 1, :], sp[:, 0, :], ACT.Exp).then_inc(sp_act, 1)
            split_wide(0)
            for c in range(NC):
                for k in range(KT):
                    n = RING["xT", c, k]
                    eng.wait_ge(psum_full, n + 1)
                    eng.activation(x_hi[:, k, cols(c)], ps[:, n % BANKS, 0:C], ACT.Copy)
                    square(NORM["pre1", c], k, ps[:, n % BANKS, 0:C])
                root("pre1", c)
                if c == 0:
                    split_wide(1)

            def behind_ffn(f, post, pre, batch):
                n0 = RING["ffn", f] + (NI - 1) * STEP + 4 * NC
                tile_of = lambda c: (lambda m: acc[:, m, cols(c)])
                for c in (0, 1):
                    squares(post, c, tile_of(c), psum_free, n0 + KT * c)
                    root(post, c)
                if f:
                    p_to_features()
                apply(pre, 0, 24 * 2 * f, tile_of(0))
                if f:
                    split_down(2 * NI, RING["ffn", 1] + NI * STEP)
                root(pre, 0)
                batch(0)
                squares(post, 2, tile_of(2), psum_free, n0 + KT * 2)
                root(post, 2)
                apply(pre, 1, 24 * 2 * f + 8, tile_of(1))

            def p_to_features():
                for c in range(NC):
                    for k in range(PT):
                        n = RING["pT", c, k]
                        eng.wait_ge(psum_full, n + 1)
                        eng.activation(a_hi[:, k, cols(c)], ps[:, n % BANKS, 0:C], ACT.Copy
                                       ).then_inc(pt_hi, 1)

            ffn(0)

            def sigmoid_glu(n, ring_n):
                b = n % 2
                eng.wait_ge(psum_free, ring_n + 1)
                eng.activation(glu[:, b, :], glu[:, b, :], ACT.Sigmoid).then_inc(sig_done, 1)

            def glu_batch(c):
                for t in range(2):
                    sigmoid_glu(2 * c + t, RING["vg", c, 2 + t])

            behind_ffn(0, "post1", "pre2", glu_batch)
            root("pre2", 1)
            glu_batch(1)
            apply("pre2", 2, 16, lambda m: acc[:, m, cols(2)])
            root("pre2", 2)
            glu_batch(2)
            split_wide(WIDE0["mix"] + 2)
            eng.wait_ge(gate_in, 64)
            eng.activation(gw_hi[:, :, :, :], gate_raw[:, :, :, :], ACT.Copy).then_inc(gw_hi_done, 1)
            split_wide(WIDE0["mix"] + 3)
            split_wide(WIDE0["mix"] + 4)
            for c in range(NC):
                for t in range(2):
                    sigmoid_glu(6 + 2 * c + t, RING["in", 3, c, t])
            split_wide(WIDE0["mix"] + 5)

            def lru_front(x):
                eng.wait_ge(xc_done, x + 1)
                if x >= 2:
                    eng.wait_ge(aux_full, AUX["i", x - 2] + 1)
                eng.activation(xc_hi[:, x % 2, :], xc[:, x % 2, :], ACT.Copy).then_inc(xc_hi_done, 1)

            def lru_gates(x):
                j, c, t = lru_tile(x)
                nr, ni = AUX["r", x], AUX["i", x]
                if x > 0:
                    eng.wait_ge(scan_done, x)
                eng.wait_ge(aux_full, nr + 1)
                eng.activation(lru_r[:, :], ps_aux[:, nr % 2, 0:C], ACT.Sigmoid,
                               bias=vec("lru_ba", j)).then_inc(aux_free, 1)
                eng.wait_ge(aux_full, ni + 1)
                eng.activation(lru_i[:, :], ps_aux[:, ni % 2, 0:C], ACT.Sigmoid,
                               bias=vec("lru_bx", j)).then_inc(aux_free, 1)
                eng.wait_ge(aux_free, nr + 1)
                eng.activation(lru_a[:, :], lru_r[:, :], ACT.Exp, scale=sp[:, 6, j:j + 1]
                               ).then_inc(lru_act, 1)
                eng.wait_ge(lru_act, 3 * x + 1)
                eng.activation(lru_r[:, :], lru_r[:, :], ACT.Tanh, scale=sp[:, 7, j:j + 1]
                               ).then_inc(lru_act, 1)
                eng.activation(lru_q[:, :], lru_a[:, :], ACT.Square).then_inc(lru_act, 1)

            def lru_root(x):
                eng.wait_ge(lru_gain, x + 1)
                eng.activation(lru_q[:, :], lru_q[:, :], ACT.Sqrt).then_inc(lru_sqrt, 1)

            def diagonals(j):
                for tap in range(TP):
                    if j and tap < TP - 1:
                        eng.wait_ge(diag_free, (TP - 1) * (j - 1) + tap + 1)
                    elif j:
                        eng.wait_ge(psum_full, RING["conv", j - 1, 2] + 1)
                    eng.activation(diag[:, tap, :], ident[:, :], ACT.Copy, scale=conv_w(tap, j)
                                   ).then_inc(diag_done, 1)

            diagonals(0)
            for x in range(12):
                lru_front(x)
                if x > 0:
                    lru_root(x - 1)
                if x % 3 == 2 and x < 11:
                    diagonals(x // 3 + 1)
                lru_gates(x)
                if x == 5:
                    split_wide(WIDE0["mix"] + 6)

            def gelu(n):
                j, c, t = lru_tile(n)
                eng.wait_ge(psum_free, RING["in", 6 + n // 6, c, t] + 1)
                eng.activation(ge[:, n % 2, :], ge[:, n % 2, :], ACT.Gelu_apprx_tanh
                               ).then_inc(gelu_done, 1)

            def yb_hi(n):
                j, c, t = lru_tile(n)
                eng.wait_ge(yb_done, n + 1)
                if n == 0:
                    eng.wait_ge(aux_full, AUX["i", 11] + 1)
                eng.activation(y_hi[:, NJ + j, cols(c)], ge[:, n % 2, :], ACT.Copy
                               ).then_inc(yb_hi_done, 1)

            def conv_squares(c):
                for j in range(NJ):
                    square(NORM["conv", c], j, conv[:, j, cols(c)], psum_free,
                           RING["conv", 3, c] + 1)

            def conv_silu(c):
                for j in range(NJ):
                    eng.wait_ge(cn_done, NJ * c + j + 1)
                    done(eng.activation(conv[:, j, cols(c)], conv[:, j, cols(c)], ACT.Silu,
                                        scale=vec("conv_norm_g", j)))
                    eng.activation(y_hi[:, j, cols(c)], conv[:, j, cols(c)], ACT.Copy
                                   ).then_inc(cn_silu, 1)

            lru_root(11)
            for n in range(12):
                c, part = divmod(n, 4)
                if n == 1:
                    split_wide(WIDE0["mix"] + 7)
                if n == 6:
                    split_wide(WIDE0["mix"] + 8)
                gelu(n)
                if n:
                    yb_hi(n - 1)
                if part == 1:
                    conv_squares(c)
                if part == 2:
                    root("conv", c)
                if part == 3:
                    conv_silu(c)
            yb_hi(11)
            split_wide(WIDE0["mix"] + 9)

            for c in range(NC):
                i = NORM["post2", c]
                for m in range(KT):
                    square(i, m, oc[:, m, :], psum_free, RING["wout", c, m] + 1)
                    if m % 2:
                        v = WIDE0["mix"] + 8 + 4 * c + m // 2 + 2
                        split_wide(v)
                root("post2", c)
                apply("pre3", c, 24 + 8 * c, lambda m: oc[:, m, :])
                if c < 2:
                    root("pre3", c)

            ffn_step(1, 0, root0=("pre3", 2))
            with eng.Fori(1, NI - 1) as i:
                ffn_step(1, i)
            ffn_step(1, NI - 1, last=True)

            def gate_unit(c, q):
                for t in range(2):
                    n = 8 * c + 2 * q + t
                    eng.wait_ge(psum_free, RING["ple", c, q, t] + 1)
                    if n >= 2:
                        c0, q0 = divmod(n - 2, 8)
                        eng.wait_ge(psum_free, RING["ple", c0, q0 // 2, 2 + t] + 1)
                    eng.activation(tmp_s[:, t, :], tmp_g[:, t, :], ACT.Sigmoid
                                   ).then_inc(gate_sig, 1)
                v = WIDE0["ple"] + 4 * c + q + 2
                if v < N_WIDE:
                    split_wide(v)

            def z_squares(c):
                i = NORM["post4", c]
                for m in range(KT):
                    square(i, m, acc[:, m, cols(c)], psum_free,
                           RING["ple", c, m // 2, 2 + m % 2] + 1)

            behind_ffn(1, "post3", "pre4", lambda c: gate_unit(0, 0))
            for q in (1, 2, 3):
                gate_unit(0, q)
            root("pre4", 1)
            gate_unit(1, 0)
            apply("pre4", 2, 48 + 16, lambda m: acc[:, m, cols(2)])
            gate_unit(1, 1)
            root("pre4", 2)
            z_squares(0)
            gate_unit(1, 2)
            root("post4", 0)
            gate_unit(1, 3)
            gate_unit(2, 0)
            z_squares(1)
            gate_unit(2, 1)
            root("post4", 1)
            gate_unit(2, 2)
            gate_unit(2, 3)
            z_squares(2)
            root("post4", 2)

        @block.vector
        def _(eng):
            own = [0]

            def mark(ins):
                own[0] += 1
                ins.then_inc(dve_own, 1)
                return own[0]

            def done(ins):
                mark(ins)
                eng.wait_ge(dve_own, own[0])

            def bank(n):
                eng.wait_ge(psum_full, n + 1)
                return ps[:, n % BANKS, 0:C]

            def bank_at(reg, n):
                eng.wait_ge(psum_full, reg + (n + 1))
                return ps[:, n % BANKS, 0:C]

            def split_tile(v, k, s=None, gain=None):
                if s is None:
                    s, gain = v % 2, wide_gain(v)
                h = k // 4
                if k % 4 == 0:
                    eng.wait_ge(wide_hi, v * 2 + (h + 1))
                    if gain is None:
                        sl = slice(h * HALF, (h + 1) * HALF)
                        eng.tensor_tensor(w_lo[s][:, sl], raw[:, sl], f32(w_hi[s][:, sl]),
                                          ALU.subtract).then_inc(wide_lo, 1)
                if gain is None:
                    return
                sl = slice(k * WIDE, (k + 1) * WIDE)
                ins = eng.scalar_tensor_tensor(w_lo[s][:, sl], raw[:, sl], vec(gain, k),
                                               f32(w_hi[s][:, sl]), ALU.mult, ALU.subtract)
                if k % 4 == 3:
                    ins.then_inc(wide_lo, 1)

            def split_half(v, h):
                for k in range(4 * h, 4 * h + 4):
                    split_tile(v, k)

            def split_wide(v):
                for h in range(2):
                    split_half(v, h)

            def split_down(d):
                eng.wait_ge(down_hi, d + 1)
                eng.tensor_tensor(wd_lo[:, :], rawd[:, :], f32(wd_hi[:, :]), ALU.subtract
                                  ).then_inc(down_lo, 1)

            def add_square(i, m):
                eng.wait_ge(sq_done, SQ0[i] + m + 1)
                if ADD0[i] + m - 1 > 0:
                    eng.wait_ge(add_done, ADD0[i] + m - 1)
                eng.tensor_tensor(ssum[:, :], ssum[:, :], sq[:, m % 2, :], ALU.add
                                  ).then_inc(add_done, 1)

            post_buf = {}

            def invert(name, c):
                i = NORM[name, c]
                eng.wait_ge(aux_free, AUX["norm", i] + 1)
                if name.startswith("pre"):
                    dst = rstd_pre[:, cols(c)]
                else:
                    post_buf[name, c] = len(post_buf) % 2
                    dst = rstd_post[:, post_buf[name, c], :]
                eng.reciprocal(dst, std[:, :]).then_inc(rstd_done, 1)

            def rstd(name, c):
                eng.wait_ge(rstd_done, NORM[name, c] + 1)
                return rstd_pre[:, cols(c)] if name.startswith("pre") else \
                    rstd_post[:, post_buf[name, c], :]

            def apply(post, c, x0, src, gain, pre, after=None):
                r = rstd(post, c)
                n = own[0]
                for m0 in range(0, KT, 2):
                    for m in (m0, m0 + 1):
                        n1 = mark(eng.tensor_tensor(src(m), src(m), r, ALU.mult))
                    for m in (m0, m0 + 1):
                        eng.wait_ge(dve_own, n1 - 1 + (m - m0))
                        n2 = mark(eng.scalar_tensor_tensor(src(m), src(m), gain(m),
                                                           f32(x_hi[:, m, cols(c)]),
                                                           ALU.mult, ALU.add))
                    for m in (m0, m0 + 1):
                        eng.wait_ge(dve_own, n2 - 1 + (m - m0))
                        eng.tensor_tensor(src(m), src(m), f32(x_lo[:, m, cols(c)]), ALU.add
                                          ).then_inc(x_new if pre else y_fin, 1)
                    if pre:
                        for m in (m0 - 2, m0 - 1) if m0 else ():
                            apply_tail(c, m, x0, src, pre)
                if pre:
                    for m in (KT - 2, KT - 1):
                        apply_tail(c, m, x0, src, pre)

            def apply_tail(c, m, x0, src, pre):
                eng.wait_ge(x_hi_done, x0 + m + 1)
                eng.tensor_tensor(x_lo[:, m, cols(c)], src(m), f32(x_hi[:, m, cols(c)]),
                                  ALU.subtract).then_inc(x_lo_done, 1)
                if m:
                    add_square(NORM[pre, c], m)

            def scaled(f, i, c, h, up):
                R, Q = RING["ffn", f], NI * NC * G * f
                q, off = NC * G * i + (Q + 2 * c + h), R + 4 * c + 2 * up + h
                src = bank_at(i * STEP, off)
                if f or not isinstance(i, int) or i or c:
                    eng.wait_ge(prod_done if up else silu_done, q - 1)
                eng.tensor_tensor((tmp_u if up else tmp_g)[:, h, :], src, rstd_pre[:, cols(c)],
                                  ALU.mult).then_inc(psum_free, 1)

            def hidden(f, i, c, h):
                R, Q = RING["ffn", f], NI * NC * G * f
                q, n = NC * G * i + (Q + 2 * c + h), STEP * i + (R + 4 * c + 2 + h)
                eng.wait_ge(silu_done, q + 1)
                eng.wait_ge(psum_free, n + 1)
                if f or not isinstance(i, int) or i or c:
                    eng.wait_ge(a_lo_done, q - 1)
                eng.tensor_tensor(tmp_a[:, h, :], tmp_s[:, h, :], tmp_u[:, h, :], ALU.mult
                                  ).then_inc(prod_done, 1)

            def hidden_lo(f, i, c, h):
                q = NC * G * i + (NI * NC * G * f + 2 * c + h)
                eng.wait_ge(a_hi_done, q + 1)
                eng.tensor_tensor(a_lo[:, h, cols(c)], tmp_a[:, h, :], f32(a_hi[:, h, cols(c)]),
                                  ALU.subtract).then_inc(a_lo_done, 1)

            def hidden_chunks(f, i, next_tile, invert_pre=None):
                for c in range(NC):
                    scaled(f, i, c, 0, 0)
                    scaled(f, i, c, 1, 0)
                    scaled(f, i, c, 0, 1)
                    if c == 2:
                        for k in range(4):
                            next_tile(0, k)
                    scaled(f, i, c, 1, 1)
                    hidden(f, i, c, 0)
                    hidden(f, i, c, 1)
                    if c == 2:
                        for k in range(4, 8):
                            next_tile(0, k)
                    hidden_lo(f, i, c, 0)
                    hidden_lo(f, i, c, 1)
                    if c == 0:
                        if invert_pre:
                            invert(*invert_pre)
                            eng.wait_ge(rstd_done, NORM[invert_pre] + 1)
                        split_down(i + NI * f)

            def down(f, i, c, m):
                off = RING["ffn", f] + 4 * NC + KT * c + m
                src = bank_at(i * STEP, off)
                if isinstance(i, int) and i == 0:
                    eng.tensor_copy(acc[:, m, cols(c)], src).then_inc(psum_free, 1)
                    return
                eng.wait_ge(psum_free, STEP * i + (off - STEP + 1))
                eng.tensor_tensor(acc[:, m, cols(c)], src, acc[:, m, cols(c)], ALU.add
                                  ).then_inc(psum_free, 1)

            def ffn_step(f, i, invert_pre=None):
                V, gain = WIDE0[f"ffn{f + 1}"], f"ffn{f + 1}_pre_g"

                def next_tile(s, k):
                    split_tile(i * 2 + (V + 2 + s), k, s, gain)

                hidden_chunks(f, i, next_tile, invert_pre)
                for c in range(NC):
                    for m in range(KT):
                        down(f, i, c, m)
                        if c < 2 and m >= 4:
                            next_tile(1, 4 * c + m - 4)

            def ffn_last(f, post):
                i, V = NI - 1, WIDE0[f"ffn{f + 1}"]

                def next_tile(s, k):
                    split_tile(V + 2 * NI + s, k)

                hidden_chunks(f, i, next_tile)
                for c in range(NC):
                    for m in range(KT):
                        down(f, i, c, m)
                        if c and m > 1:
                            add_square(NORM[post, c - 1], m - 1)
                        if c < 2 and m >= 4:
                            next_tile(1, 4 * c + m - 4)
                    if c:
                        add_square(NORM[post, c - 1], KT - 1)
                    if c == 1:
                        invert(post, 0)

            acc_tile = lambda c: (lambda m: acc[:, m, cols(c)])

            def behind_ffn(f, post, pre, batch, middle=None):
                x0 = 24 * 2 * f
                gain = lambda m: half_g[:, KT * f + m:KT * f + m + 1]
                if f:
                    p_to_features()
                apply(post, 0, x0, acc_tile(0), gain, pre)
                if f:
                    split_down(2 * NI)
                invert(post, 1)
                invert(pre, 0)
                batch(0)
                for m in range(1, KT):
                    add_square(NORM[post, 2], m)
                apply(post, 1, x0 + 8, acc_tile(1), gain, pre)
                invert(post, 2)
                return gain

            def p_to_features():
                for c in range(NC):
                    for k in range(PT):
                        n = RING["pT", c, k]
                        eng.wait_ge(pt_hi, PT * c + k + 1)
                        eng.tensor_tensor(a_lo[:, k, cols(c)], ps[:, n % BANKS, 0:C],
                                          f32(a_hi[:, k, cols(c)]), ALU.subtract
                                          ).then_inc(psum_free, 1)

            eng.wait_ge(psum_full, 1)
            width = 2 * P
            n = mark(eng.tensor_copy(params[:, 0:NROWS], ps[:, 0, 0:NROWS]))
            n = mark(eng.tensor_copy(params[:, P:P + CW * NJ], ps[:, 0, P:P + CW * NJ]))
            eng.tensor_copy(params[:, width:3 * P], ps[:, 0, width:3 * P]).then_inc(psum_free, 1)
            eng.wait_ge(dve_own, n)
            lam = params[:, ROW["lru_lambda"]:ROW["lru_lambda"] + NJ]
            done(eng.tensor_scalar(sp[:, 2, :], lam, -1.0, None, ALU.mult))
            eng.tensor_tensor(sp[:, 0, :], sp[:, 2, :], lam, ALU.min).then_inc(half_done, 1)
            for f in range(2):
                g0 = ROW[f"ffn{f + 1}_post_g"]
                done(eng.tensor_scalar(half_g[:, KT * f:KT * f + KT], params[:, g0:g0 + KT], 0.5,
                                       None, ALU.mult))
            eng.wait_ge(sp_act, 1)
            done(eng.tensor_scalar(sp[:, 3, :], sp[:, 1, :], 2.0, None, ALU.add))
            done(eng.reciprocal(sp[:, 4, :], sp[:, 3, :]))
            done(eng.tensor_tensor(sp[:, 3, :], sp[:, 1, :], sp[:, 4, :], ALU.mult))
            done(eng.tensor_tensor(sp[:, 4, :], sp[:, 3, :], sp[:, 3, :], ALU.mult))
            done(eng.tensor_scalar(sp[:, 5, :], sp[:, 4, :], 1.0 / 17, 1.0 / 15, ALU.mult, ALU.add))
            for d in (13, 11, 9, 7, 5, 3, 1):
                done(eng.tensor_tensor(sp[:, 5, :], sp[:, 5, :], sp[:, 4, :], ALU.mult))
                done(eng.tensor_scalar(sp[:, 5, :], sp[:, 5, :], 1.0 / d, None, ALU.add))
            done(eng.tensor_tensor(sp[:, 5, :], sp[:, 5, :], sp[:, 3, :], ALU.mult))
            done(eng.tensor_scalar(sp[:, 2, :], sp[:, 2, :], 0.0, None, ALU.max))
            done(eng.scalar_tensor_tensor(sp[:, 5, :], sp[:, 5, :], 2.0, sp[:, 2, :], ALU.mult,
                                          ALU.add))
            done(eng.tensor_scalar(sp[:, 6, :], sp[:, 5, :], -8.0, None, ALU.mult))
            done(eng.tensor_scalar(sp[:, 7, :], sp[:, 5, :], 8.0, None, ALU.mult))
            split_wide(0)

            for c in range(NC):
                i = NORM["pre1", c]
                for k in range(KT):
                    n = RING["xT", c, k]
                    eng.wait_ge(sq_done, SQ0[i] + k + 1)
                    eng.tensor_tensor(x_lo[:, k, cols(c)], ps[:, n % BANKS, 0:C],
                                      f32(x_hi[:, k, cols(c)]), ALU.subtract
                                      ).then_inc(psum_free, 1)
                    eng.wait_ge(psum_free, n + 1)
                    if k:
                        add_square(i, k)
                invert("pre1", c)
                if c == 0:
                    split_wide(1)

            eng.wait_ge(rstd_done, NC)
            ffn_step(0, 0)
            with eng.Fori(1, NI - 1) as i:
                ffn_step(0, i)
            ffn_last(0, "post1")

            glu_n = [0]

            def parts(c):
                return C if c < 2 else LAST

            def put_g(c, j, src, r, op_in1=None):
                w = parts(c)
                ins = eng.tensor_tensor(gp[:, j, CH + C * c:CH + C * c + w], src[:, 0:w],
                                        r[:, 0:w], ALU.mult)
                if c == 2:
                    ins = eng.tensor_tensor(
                        gs[:, j, :, CH:CH + DEC],
                        src[:, w:C].rearrange("p (b t) -> p b t", b=NB),
                        r[:, w:C].rearrange("p (b t) -> p b t", b=NB), ALU.mult)
                ins.then_inc(psum_free, 1)

            def value(n, c, j):
                put_g(c, j, bank(n), rstd("pre2", c))

            def glu_gate(n, c, j):
                b = glu_n[0] % 2
                src = bank(n)
                if glu_n[0] >= 2:
                    eng.wait_ge(glu_done, glu_n[0] - 1)
                eng.tensor_tensor(glu[:, b, :], src, rstd("pre2", c), ALU.mult
                                  ).then_inc(psum_free, 1)
                glu_n[0] += 1

            def glu_mult(k, c, j):
                eng.wait_ge(sig_done, k + 1)
                w = parts(c)
                dst = gp[:, j, CH + C * c:CH + C * c + w]
                ins = eng.tensor_tensor(dst, dst, glu[:, k % 2, 0:w], ALU.mult)
                if c == 2:
                    dst = gs[:, j, :, CH:CH + DEC]
                    ins = eng.tensor_tensor(
                        dst, dst, glu[:, k % 2, w:C].rearrange("p (b t) -> p b t", b=NB), ALU.mult)
                ins.then_inc(glu_done, 1)

            def vg_batch(c):
                for j in range(2):
                    value(RING["vg", c, j], c, j)
                for j in range(2):
                    glu_gate(RING["vg", c, 2 + j], c, j)
                for j in range(2):
                    eng.wait_ge(psum_free, RING["vg", c, j] + 1)
                    glu_mult(2 * c + j, c, j)

            gain1 = behind_ffn(0, "post1", "pre2", vg_batch)
            invert("pre2", 1)
            vg_batch(1)
            apply("post1", 2, 16, acc_tile(2), gain1, "pre2")
            invert("pre2", 2)
            vg_batch(2)
            eng.wait_ge(psum_full, RING["ffn", 0] + NI * STEP)
            eng.memset(gate_raw[:, :, :, :], 0.0).then_inc(gate_zero, 1)
            n_hist = mark(eng.memset(gp[:, :, 0:CH], 0.0))
            for s in range(2):
                n = RING["cache", s]
                eng.wait_ge(psum_full, n + 1)
                for j in range(NJ):
                    ins = eng.tensor_copy(
                        gs[:, j, 4 * s:4 * s + 4, 0:CH],
                        ps[:, n % BANKS, j * 4 * CH:(j + 1) * 4 * CH].rearrange(
                            "p (b w) -> p b w", b=4))
                ins.then_inc(psum_free, 1)
            eng.wait_ge(psum_free, RING["cache", 1] + 1)
            eng.wait_ge(dve_own, n_hist)
            split_wide(WIDE0["mix"] + 2)
            eng.wait_ge(gw_hi_done, 1)
            eng.tensor_tensor(gw_lo[:, :, :, :], gate_raw[:, :, :, :], f32(gw_hi[:, :, :, :]),
                              ALU.subtract).then_inc(gw_lo_done, 1)
            split_wide(WIDE0["mix"] + 3)

            conv_n = [0]

            def conv_taps(count):
                own_taps = CW - TP
                for n in range(conv_n[0], min(conv_n[0] + count, own_taps * NJ)):
                    j, tap = divmod(n, own_taps)
                    tap += TP
                    if tap == TP:
                        eng.wait_ge(glu_done, 6 * (j // 2 + 1))
                    dst_p, src_p = conv[:, j, 0:SEQ], gp[:, j, tap:tap + SEQ]
                    dst_s = conv[:, j, SEQ:TOK].rearrange("p (b t) -> p b t", b=NB)
                    src_s = gs[:, j, :, tap:tap + DEC]
                    for part, (dst, src) in enumerate(((dst_p, src_p), (dst_s, src_s))):
                        if tap == TP:
                            ins = eng.tensor_scalar(dst, src, conv_w(tap, j), vec("conv_b", j),
                                                    ALU.mult, ALU.add)
                        else:
                            eng.wait_ge(conv_step, 2 * n - 1 + part)
                            ins = eng.scalar_tensor_tensor(dst, src, conv_w(tap, j), dst,
                                                           ALU.mult, ALU.add)
                        ins.then_inc(conv_step, 1)
                    conv_n[0] = n + 1

            def conv_join(j, c):
                assert conv_n[0] >= (CW - TP) * (j + 1)
                eng.wait_ge(conv_step, 2 * (CW - TP) * (j + 1))
                src = bank(RING["conv", j, c])
                eng.tensor_tensor(conv[:, j, cols(c)], src, conv[:, j, cols(c)], ALU.add
                                  ).then_inc(psum_free, 1)

            for c in range(NC):
                for t in range(2):
                    value(RING["in", 2, c, t], c, 2 + t)
                    conv_taps(2)
            split_wide(WIDE0["mix"] + 4)
            for c in range(NC):
                for t in range(2):
                    glu_gate(RING["in", 3, c, t], c, 2 + t)
                    conv_taps(2)
                    eng.wait_ge(psum_free, RING["in", 2, c, t] + 1)
                    glu_mult(6 + 2 * c + t, c, 2 + t)
            split_wide(WIDE0["mix"] + 5)
            def conv_states():
                for s in range(3):
                    n = RING["convout", s]
                    w = CH if s == 0 else 4 * CH
                    eng.wait_ge(psum_full, n + 1)
                    eng.tensor_copy(cv_stage[0:w, s, :], ps[0:w, n % BANKS, :]
                                    ).then_inc(psum_free, 1)

            eng.wait_ge(glu_done, 4 * NC)
            eng.tensor_copy(gs_new[:, :, :].rearrange("p j (b w) -> p (j b) w", w=CH),
                            gs[:, :, :, DEC:DEC + CH].rearrange("p j b w -> p (j b) w")
                            ).then_inc(gs_new_done, 1)

            def lru_front(x):
                j, c, t = lru_tile(x)
                if x >= 2:
                    eng.wait_ge(xc_done, x - 1)
                if c == 0:
                    mark(eng.memset(ux_p[:, t, 0:LH], 0.0))
                    mark(eng.tensor_copy(
                        ux_s[:, t, :, 0:LH],
                        st_in(j, 0, NB * LH).rearrange("p (b w) -> p b w", b=NB)))
                else:
                    done(eng.tensor_copy(ux_p[:, t, 0:LH], ux_p[:, t, C:C + LH]))
                src = bank(RING["in", 4 + x // 6, c, t])
                r = rstd("pre2", c)
                w = parts(c)
                ins = eng.tensor_tensor(ux_p[:, t, LH:LH + w], src[:, 0:w], r[:, 0:w], ALU.mult)
                if c == 2:
                    ins = eng.tensor_tensor(
                        ux_s[:, t, :, LH:LH + DEC], src[:, w:C].rearrange("p (b t) -> p b t", b=NB),
                        r[:, w:C].rearrange("p (b t) -> p b t", b=NB), ALU.mult)
                ins.then_inc(psum_free, 1)
                eng.wait_ge(psum_free, RING["in", 4 + x // 6, c, t] + 1)
                if x >= 2:
                    eng.wait_ge(scan_done, x - 1)
                eng.wait_ge(dve_own, own[0])
                b = x % 2
                for tap in range(LW):
                    wt = params[:, ROW["lru_conv_w"] + tap * NJ + j:][:, 0:1]
                    pieces = [(xc[:, b, 0:w], ux_p[:, t, tap:tap + w])]
                    if c == 2:
                        pieces.append((xc[:, b, w:C].rearrange("p (b t) -> p b t", b=NB),
                                       ux_s[:, t, :, tap:tap + DEC]))
                    if tap:
                        eng.wait_ge(dve_own, own[0])
                    for dst, s_ in pieces:
                        if tap == 0:
                            ins = eng.tensor_scalar(dst, s_, wt, vec("lru_conv_b", j), ALU.mult,
                                                    ALU.add)
                        else:
                            ins = eng.scalar_tensor_tensor(dst, s_, wt, dst, ALU.mult, ALU.add)
                        if tap < LW - 1:
                            mark(ins)
                ins.then_inc(xc_done, 1)
                if c == 2:
                    eng.tensor_copy(st_out[:, j, 0:LH], ux_p[:, t, LAST:LAST + LH])
                    done(eng.tensor_copy(
                        st_out[:, j, LH:LH + NB * LH].rearrange("p (b w) -> p b w", b=NB),
                        ux_s[:, t, :, DEC:DEC + LH]))
                eng.wait_ge(xc_hi_done, x + 1)
                eng.tensor_tensor(xc_lo[:, b, :], xc[:, b, :], f32(xc_hi[:, b, :]), ALU.subtract
                                  ).then_inc(xc_lo_done, 1)

            def lru_one_minus(x):
                eng.wait_ge(lru_act, 3 * x + 3)
                eng.scalar_tensor_tensor(lru_q[:, :], lru_q[:, :], 1.0, lru_r[:, :], ALU.add,
                                         ALU.mult).then_inc(lru_gain, 1)

            def lru_scan(x):
                j, c, t = lru_tile(x)
                if x == 0:
                    eng.wait_ge(gw_lo_done, 1)
                if x == 6:
                    eng.wait_ge(conv_out, 48)
                done(eng.tensor_tensor(lru_i[:, :], lru_i[:, :], xc[:, x % 2, :], ALU.mult))
                eng.wait_ge(lru_sqrt, x + 1)
                done(eng.tensor_tensor(lru_i[:, :], lru_i[:, :], lru_q[:, :], ALU.mult))
                w = parts(c)
                first = 0.0 if c == 0 else hs[:, j, C * c - 1:C * c]
                if c:
                    eng.wait_ge(scan_done, x - 1)
                ins = eng.tensor_tensor_scan(hs[:, j, C * c:C * c + w], lru_a[:, 0:w],
                                             lru_i[:, 0:w], first, ALU.mult, ALU.add)
                if c == 2:
                    mark(ins)
                    for b in range(NB):
                        o = LAST + DEC * b
                        ins = eng.tensor_tensor_scan(
                            hs[:, j, C * c + o:C * c + o + DEC], lru_a[:, o:o + DEC],
                            lru_i[:, o:o + DEC], st_in(j, 24 + b, 25 + b), ALU.mult, ALU.add)
                    done(ins)
                    n_st = LH + NB * LH
                    eng.tensor_copy(st_out[:, j, n_st:n_st + 1], hs[:, j, SEQ - 1:SEQ])
                    ins = eng.tensor_copy(
                        st_out[:, j, n_st + 1:n_st + 1 + NB],
                        hs[:, j, SEQ:TOK].rearrange("p (b t) -> p b t", b=NB)[:, :, DEC - 1])
                ins.then_inc(scan_done, 1)

            for x in range(12):
                lru_front(x)
                if x:
                    lru_one_minus(x - 1)
                conv_taps(4)
                if x == 0:
                    conv_join(0, 0)
                    conv_states()
                    continue
                lru_scan(x - 1)
                conv_join(x // NC, x % NC)
                if x == 5:
                    split_wide(WIDE0["mix"] + 6)

            def gelu_in(n):
                j, c, t = lru_tile(n)
                src = bank(RING["in", 6 + n // 6, c, t])
                if n >= 2:
                    eng.wait_ge(yb_lo_done, n - 1)
                eng.tensor_tensor(ge[:, n % 2, :], src, rstd("pre2", c), ALU.mult
                                  ).then_inc(psum_free, 1)

            def yb(n):
                j, c, t = lru_tile(n)
                eng.wait_ge(gelu_done, n + 1)
                eng.wait_ge(scan_done, n + 1)
                eng.tensor_tensor(ge[:, n % 2, :], ge[:, n % 2, :], hs[:, j, cols(c)], ALU.mult
                                  ).then_inc(yb_done, 1)

            def yb_lo(n):
                j, c, t = lru_tile(n)
                eng.wait_ge(yb_hi_done, n + 1)
                eng.tensor_tensor(y_lo[:, NJ + j, cols(c)], ge[:, n % 2, :],
                                  f32(y_hi[:, NJ + j, cols(c)]), ALU.subtract
                                  ).then_inc(yb_lo_done, 1)

            def conv_scale(c):
                invert("conv", c)
                r = rstd("conv", c)
                for j in range(NJ):
                    eng.tensor_tensor(conv[:, j, cols(c)], conv[:, j, cols(c)], r, ALU.mult
                                      ).then_inc(cn_done, 1)

            def conv_lo(c):
                for j in range(NJ):
                    eng.wait_ge(cn_silu, NJ * c + j + 1)
                    eng.tensor_tensor(y_lo[:, j, cols(c)], conv[:, j, cols(c)],
                                      f32(y_hi[:, j, cols(c)]), ALU.subtract
                                      ).then_inc(yc_lo_done, 1)

            lru_one_minus(11)
            lru_scan(11)
            for n in range(12):
                c, part = divmod(n, 4)
                if n == 1:
                    split_wide(WIDE0["mix"] + 7)
                if n == 6:
                    split_wide(WIDE0["mix"] + 8)
                    k = RING["state"]
                    eng.wait_ge(psum_full, k + 1)
                    eng.tensor_copy(st_stage[0:36, :], ps[0:36, k % BANKS, :]).then_inc(psum_free, 1)
                if n >= 2:
                    yb_lo(n - 2)
                gelu_in(n)
                if n:
                    yb(n - 1)
                if part == 1:
                    for j in range(1, NJ):
                        add_square(NORM["conv", c], j)
                if part == 3:
                    conv_scale(c)
                if part == 0 and c:
                    conv_lo(c - 1)
            yb_lo(10)
            yb(11)
            yb_lo(11)
            conv_lo(2)
            split_wide(WIDE0["mix"] + 9)

            oc_tile = lambda m: oc[:, m, :]
            for c in range(NC):
                for m in range(KT):
                    n = RING["wout", c, m]
                    src = bank(n)
                    if c:
                        eng.wait_ge(x_lo_done, 24 + 8 * c)
                        eng.wait_ge(add_done, ADD0[NORM["pre3", c - 1] + 1])
                    eng.tensor_copy(oc[:, m, :], src).then_inc(psum_free, 1)
                    if m > 1:
                        add_square(NORM["post2", c], m - 1)
                    if m % 2:
                        v = WIDE0["mix"] + 8 + 4 * c + m // 2 + 2
                        split_wide(v)
                add_square(NORM["post2", c], KT - 1)
                invert("post2", c)
                apply("post2", c, 24 + 8 * c, oc_tile, lambda m: vec("mix_post_g", m), "pre3")
                if c < 2:
                    invert("pre3", c)

            eng.wait_ge(x_lo_done, 48)
            ffn_step(1, 0, invert_pre=("pre3", 2))
            with eng.Fori(1, NI - 1) as i:
                ffn_step(1, i)
            ffn_last(1, "post3")

            def ple_unit(c, q):
                for t in range(2):
                    n = 8 * c + 2 * q + t
                    src = bank(RING["ple", c, q, t])
                    if n >= 2:
                        eng.wait_ge(gate_sig, n - 1)
                    eng.tensor_tensor(tmp_g[:, t, :], src, rstd("pre4", c), ALU.mult
                                      ).then_inc(psum_free, 1)
                for t in range(2):
                    n = 8 * c + 2 * q + t
                    src = bank(RING["ple", c, q, 2 + t])
                    eng.wait_ge(gate_sig, n + 1)
                    eng.tensor_tensor(acc[:, 2 * q + t, cols(c)], src, tmp_s[:, t, :], ALU.mult
                                      ).then_inc(psum_free, 1)
                v = WIDE0["ple"] + 4 * c + q + 2
                if v < N_WIDE:
                    split_wide(v)

            def z_adds(c):
                for m in range(1, KT):
                    add_square(NORM["post4", c], m)

            def finish(c):
                invert("post4", c)
                apply("post4", c, None, acc_tile(c), lambda m: vec("ple_post_g", m), None)

            def stage_out(c):
                for q in range(3):
                    w, n = min(P, C - P * q), 3 * c + q
                    if n >= 2:
                        eng.wait_ge(y_out[n % 2], 16 * (n // 2))
                    for half in range(2):
                        k = RING["yT", c, 2 * q + half]
                        eng.wait_ge(psum_full, k + 1)
                        eng.tensor_copy(y_stage[0:w, n % 2, 512 * half:512 * half + 512],
                                        ps[0:w, k % BANKS, :]).then_inc(psum_free, 1)

            gain3 = behind_ffn(1, "post3", "pre4", lambda c: ple_unit(0, 0))
            for q in (1, 2, 3):
                ple_unit(0, q)
            invert("pre4", 1)
            ple_unit(1, 0)
            apply("post3", 2, 48 + 16, acc_tile(2), gain3, "pre4")
            ple_unit(1, 1)
            invert("pre4", 2)
            z_adds(0)
            ple_unit(1, 2)
            finish(0)
            ple_unit(1, 3)
            stage_out(0)
            ple_unit(2, 0)
            z_adds(1)
            ple_unit(2, 1)
            finish(1)
            ple_unit(2, 2)
            ple_unit(2, 3)
            stage_out(1)
            z_adds(2)
            finish(2)
            stage_out(2)


def lru_tile(x):
    u, r = divmod(x, 6)
    c, t = divmod(r, 2)
    return 2 * u + t, c, t


_INS = ["x_prompt", "x_sample", "cache_conv", "state_lru_conv", "state_lru_h", "p_prompt",
        "p_sample", "ffn1_pre_g", "ffn1_post_g", "ffn1_w_gu", "ffn1_w_down", "mix_pre_g",
        "mix_post_g", "w_in", "conv_w", "conv_b", "conv_norm_g", "lru_conv_w", "lru_conv_b",
        "lru_wa", "lru_ba", "lru_wx", "lru_bx", "lru_lambda", "w_out", "ffn2_pre_g",
        "ffn2_post_g", "ffn2_w_gu", "ffn2_w_down", "ple_norm_g", "ple_w_gate", "ple_w_proj",
        "ple_post_g"]
_OUTS = [("y_prompt", (1, SEQ, D)), ("y_sample", (NB, DEC, D)), ("conv_p", (1, 1, CH, NJ * P)),
         ("lconv_p", (1, 1, LH, NJ * P)), ("h_p", (1, 1, NJ * P)),
         ("conv_s", (1, NB, CH, NJ * P)), ("lconv_s", (1, NB, LH, NJ * P)),
         ("h_s", (1, NB, NJ * P))]


def kernel(**inputs):
    import numpy as _np
    import concourse.bacc as _bacc
    from concourse.bass_utils import run_bass_kernel_spmd as _run

    nc = _bacc.Bacc("TRN2", target_bir_lowering=False, num_devices=1)
    arrays, ins, outs = {}, {}, {}
    for name in _INS:
        arr = _np.ascontiguousarray(inputs[name])
        arrays[f"in_{name}_dram"] = arr
        ins[name] = nc.dram_tensor(f"in_{name}_dram", arr.shape, mybir.dt.from_np(arr.dtype),
                                   kind="ExternalInput").ap()
    for i, (name, shape) in enumerate(_OUTS):
        outs[name] = nc.dram_tensor(f"out_{i}_dram", shape, F32, kind="ExternalOutput").ap()
    build(nc, ins, outs)
    r = _run(nc, [arrays], core_ids=[0])
    return tuple(r.results[0][f"out_{i}_dram"] for i in range(len(_OUTS)))
```

```python
from contextlib import ExitStack

import concourse.bass as bass
from concourse import mybir

F32 = mybir.dt.float32
F32R = mybir.dt.float32r
ALU = mybir.AluOpType
ACT = mybir.ActivationFunctionType

P = 128
D = 1024
KT = D // P
FF = 2816
NJ = 4
PLE = 256
PT = PLE // P
SEQ, NB, DEC = 1024, 8, 4
TOK = SEQ + NB * DEC
NC = 3
C = TOK // NC
LAST = SEQ - 2 * C
CW, LW = 31, 4
CH, LH = CW - 1, LW - 1
TP = 15
EPS = 1e-6
G = 2
NI = FF // P // G
WIDE = 256
HALF = KT * WIDE // 2
PAIRS = KT // 2
SQ = 3
BANKS = 6
STEP = NC * (2 * G + KT)

VECTORS = [("ffn1_pre_g", 8), ("ffn1_post_g", 8), ("mix_pre_g", 8), ("mix_post_g", 8),
           ("ffn2_pre_g", 8), ("ffn2_post_g", 8), ("ple_norm_g", 8), ("ple_post_g", 8),
           ("conv_b", 4), ("conv_norm_g", 4), ("lru_conv_b", 4), ("lru_ba", 4), ("lru_bx", 4),
           ("lru_lambda", 4), ("lru_conv_w", 16)]
ROW = {}
for _name, _n in VECTORS:
    ROW[_name] = sum(n for _, n in VECTORS[:len(ROW)])
NROWS = sum(n for _, n in VECTORS)


def ring_plan():
    at, n = {}, 0

    def put(*key):
        nonlocal n
        at[key if len(key) > 1 else key[0]] = n
        n += 1

    for c in range(NC):
        for k in range(KT):
            put("xT", c, k)
        if c == 0:
            put("params")
        n += 4
    at["ffn", 0] = n - 4 * NC
    assert n == at["ffn", 0] + 4 * NC
    n = at["ffn", 0] + NI * STEP
    for c in range(NC):
        for t in range(4):
            put("vg", c, t)
    for s in range(2):
        put("cache", s)
    for u in (2, 3):
        for c in range(NC):
            for t in range(2):
                put("in", u, c, t)
    for x in range(NJ * NC):
        put("in", 4 + x // 6, x % 6 // 2, x % 2)
        put("conv", x // NC, x % NC)
        if x == 0:
            for s in range(3):
                put("convout", s)
    for c in range(NC):
        for t in range(2):
            put("in", 6, c, t)
    put("state")
    for c in range(NC):
        for t in range(2):
            put("in", 7, c, t)
    for c in range(NC):
        for m in range(KT):
            put("wout", c, m)
    at["ffn", 1] = n
    n += NI * STEP
    for c in range(NC):
        for q in range(4):
            for t in range(4):
                if (c, q, t) == (0, 0, 2):
                    for cc in range(NC):
                        for k in range(PT):
                            put("pT", cc, k)
                put("ple", c, q, t)
            if (c, q) in ((2, 2), (2, 3)):
                for s in range(6):
                    put("yT", int(q == 3), s)
    for s in range(6):
        put("yT", 2, s)
    return at, n


NORMS = ([("pre1", c, KT) for c in range(NC)]
         + [(n, c, KT) for c in range(NC) for n in ("post1", "pre2")]
         + [("conv", c, NJ) for c in range(NC)]
         + [(n, c, KT) for c in range(NC) for n in ("post2", "pre3")]
         + [(n, c, KT) for c in range(NC) for n in ("post3", "pre4")]
         + [("post4", c, KT) for c in range(NC)])
NORM = {(n, c): i for i, (n, c, _) in enumerate(NORMS)}
TILES = [t for _, _, t in NORMS]
BEHIND = [i for i, (n, _, _) in enumerate(NORMS) if not n.startswith("pre")]
SQ0 = [sum(TILES[:i]) for i in range(len(TILES) + 1)]
ADD0 = [sum(t - 1 for t in TILES[:i]) for i in range(len(TILES) + 1)]


def aux_plan():
    at, n = {}, 0
    first = NORM["conv", 0]

    def norm(i):
        nonlocal n
        at["norm", i], at["spread", i] = n, n + 1
        n += 2

    for i in range(first):
        norm(i)
    for x in range(4 * NC):
        for which in "ri":
            at[which, x] = n
            n += 1
    for i in range(first, len(NORMS)):
        norm(i)
    return at


RING, RING_N = ring_plan()
AUX = aux_plan()
WIDE0 = {"ffn1": 0, "mix": 2 * NI, "ffn2": 2 * NI + 8 + 4 * NC, "ple": 4 * NI + 8 + 4 * NC}
N_WIDE = WIDE0["ple"] + 4 * NC


def gate_at(f, i, c):
    if isinstance(i, int) and i == NI - 1:
        return RING["ffn", f] + (4 + KT) * c
    if isinstance(i, int) and i == 0 and f == 0:
        return RING["ffn", f] + 4 * c - KT * (NC - 1 - c)
    if isinstance(i, int) and i == 0 and c == NC - 1:
        return RING["ffn", f] + (4 + KT) * c
    return RING["ffn", f] + 4 * c


def down_at(f, i, c):
    if isinstance(i, int) and i == NI - 1:
        return RING["ffn", f] + (4 + KT) * c + 4
    if isinstance(i, int) and i == 0 and f == 1 and c < NC - 1:
        return RING["ffn", f] + 4 * (NC - 1) + KT * c
    return RING["ffn", f] + 4 * NC + KT * c


def cols(c):
    return slice(C * c, C * c + C)


def build(nc, a, out):
    ctx = ExitStack()
    with ctx:
        base = (nc.sbuf_base + 63) // 64 * 64
        at = [base]

        def place(name, shape, dt=F32, offset=None):
            size = 4
            for s in shape[1:]:
                size *= s
            if offset is None:
                offset = at[0]
                at[0] += (size + 31) // 32 * 32
            t = nc.alloc_sbuf_tensor_at(name, [P] + list(shape[1:]), dt, offset=offset)
            return t, offset, offset + (size + 31) // 32 * 32

        def tile(name, shape, dt=F32):
            return place(name, shape, dt)[0]

        x_hi = tile("x_hi", [P, KT, TOK], F32R)
        x_lo = tile("x_lo", [P, KT, TOK], F32R)
        w_hi = [tile(f"w_hi{s}", [P, KT * WIDE], F32R) for s in range(2)]
        w_lo = [tile(f"w_lo{s}", [P, KT * WIDE], F32R) for s in range(2)]
        raw = tile("raw", [P, KT * WIDE])
        rstd_pre = tile("rstd_pre", [P, TOK])
        rstd_post, norm_at, _ = place("rstd_post", [P, 2, C])
        ssum = tile("ssum", [P, 2, C])
        std = tile("std", [P, 8])
        sq, sq_at, _ = place("sq", [P, SQ, C])
        ident = tile("ident", [P, P])
        ones = tile("ones", [P, P])
        params = tile("params", [P, 3 * P])
        half_g = tile("half_g", [P, 2 * KT])
        eps_t = tile("eps_t", [P, 1])
        sp = tile("sp", [P, 8, NJ])
        st_out = tile("st_out", [P, NJ, 36])
        pool0 = at[0]

        acc = tile("acc", [P, KT, TOK])
        a_hi = tile("a_hi", [P, G, TOK], F32R)
        a_lo = tile("a_lo", [P, G, TOK], F32R)
        wd_hi, wd_at, _ = place("wd_hi", [P, G * D], F32R)
        wd_lo = tile("wd_lo", [P, G * D], F32R)
        tmp_g, tmp_at, _ = place("tmp_g", [P, 2, C])
        tmp_u = tile("tmp_u", [P, 2, C])
        tmp_s = tile("tmp_s", [P, 2, C])
        tmp_a = tile("tmp_a", [P, 2, C])
        rawd, rawd_at, _ = place("rawd", [P, G * D])
        ffn_end = at[0]
        x_in = place("x_in", [P, 3 * NC - 1, D], offset=pool0)[0]
        x_in8 = place("x_in8", [P, 1, D], offset=wd_at + 4096)[0]
        rows = place("rows", [P, 3 * P], offset=wd_at)[0]
        st_rows = place("st_rows", [P, NJ * P], offset=wd_at + 4 * 3 * P)[0]
        p_in = place("p_in", [P, 3 * NC, PLE], offset=tmp_at)[0]
        y_stage = place("y_stage", [P, 2, D], offset=rawd_at)[0]

        at[0] = pool0
        y_hi, yh_at, _ = place("y_hi", [P, KT, TOK], F32R)
        y_lo, yl_at, _ = place("y_lo", [P, KT, TOK], F32R)
        gp, g_at, _ = place("gp", [P, NJ, CH + SEQ])
        mix_end = at[0]
        gs, _, e = place("gs", [P, NJ, NB, CH + DEC], offset=norm_at)
        assert e <= sq_at
        assert max(ffn_end, mix_end) <= nc.sbuf_usable_end, (ffn_end, mix_end, nc.sbuf_usable_end)
        row = 4 * TOK
        conv = place("conv", [P, NJ, TOK], offset=yl_at)[0]
        hs = place("hs", [P, NJ, TOK], offset=yl_at + 4 * row)[0]
        cache_in = place("cache_in", [P, 2, NJ * P], offset=yl_at + 4 * row)[0]
        gs_new = place("gs_new", [P, NJ, NB * CH], offset=yl_at + 4 * row)[0]
        gate_raw = place("gate_raw", [P, 2, NJ, P], offset=yl_at + 4 * row + 4096)[0]
        cv_stage = place("cv_stage", [P, 3, NJ * P], offset=yl_at + 6 * row)[0]
        ux_p, _, e = place("ux_p", [P, 2, LH + C], offset=yh_at)
        ux_s, _, e = place("ux_s", [P, 2, NB, LH + DEC], offset=e)
        xc_hi, _, e = place("xc_hi", [P, 2, C], F32R, offset=e)
        xc_lo, _, e = place("xc_lo", [P, 2, C], F32R, offset=e)
        diag, _, e = place("diag", [P, TP, P], offset=e)
        assert e <= yh_at + 4 * row
        gw_hi, _, e = place("gw_hi", [P, 2, NJ, P], F32R, offset=yh_at + 4 * row)
        gw_lo, _, e = place("gw_lo", [P, 2, NJ, P], F32R, offset=e)
        assert e <= yh_at + 6 * row
        xc = place("xc", [P, 2, C], offset=yh_at + 6 * row)[0]
        lru_r = place("lru_r", [P, C], offset=yh_at + 6 * row + 8 * C)[0]
        lru_i = place("lru_i", [P, C], offset=yh_at + 6 * row + 12 * C)[0]
        lru_a = place("lru_a", [P, C], offset=yh_at + 6 * row + 16 * C)[0]
        lru_q = place("lru_q", [P, C], offset=yh_at + 6 * row + 20 * C)[0]
        glu = place("glu", [P, 2, C], offset=yl_at + 6 * row)[0]
        oc, _, e = place("oc", [P, KT, C], offset=g_at)
        st_stage, _, e = place("st_stage", [P, NJ * P], offset=e)
        ge, _, e = place("ge", [P, 2, C], offset=e)
        assert e <= mix_end

        ps = ctx.enter_context(nc.psum_tensor("ps", [P, BANKS, 512], F32))
        ps_aux = ctx.enter_context(nc.psum_tensor("ps_aux", [P, 2, 512], F32))

        def f32(t):
            return t.bitcast(F32)

        def oc_tile(c, m, n=1):
            return oc[:, m:m + n, :] if c == 0 else acc[:, m:m + n, cols(c - 1)]

        def acc_tile(c, m, n=1):
            return acc[:, m:m + n, cols(c)]

        def piece(i):
            return x_in[:, i, :] if i < 3 * NC - 1 else x_in8[:, 0, :]

        def rstd_tile(i):
            name, c, _ = NORMS[i]
            if name.startswith("pre"):
                return rstd_pre[:, cols(c)]
            return rstd_post[:, BEHIND.index(i) % 2, :]

        def vec(name, k):
            return params[:, ROW[name] + k:ROW[name] + k + 1]

        def conv_w(tap, j):
            n = P + tap * NJ + j
            return params[:, n:n + 1]

        def st_in(j, r0, r1):
            return params[:, 2 * P + 32 * j + r0:2 * P + 32 * j + r1]

        def sem(name):
            return ctx.enter_context(nc.semaphore(name))

        const_ready = sem("const_ready")
        rows_in = sem("rows_in")
        x_read = [sem(f"x_read{c}") for c in range(NC)]
        psum_full = sem("psum_full")
        psum_free = sem("psum_free")
        aux_full = sem("aux_full")
        aux_free = sem("aux_free")
        raw_in = [sem(f"raw_in{h}") for h in range(2)]
        wide_hi = sem("wide_hi")
        wide_lo = sem("wide_lo")
        rawd_in = sem("rawd_in")
        down_hi = sem("down_hi")
        down_lo = sem("down_lo")
        silu_done = sem("silu_done")
        prod_done = sem("prod_done")
        a_hi_done = sem("a_hi_done")
        a_lo_done = sem("a_lo_done")
        sq_done = sem("sq_done")
        add_done = sem("add_done")
        inv_done = sem("inv_done")
        x_new = sem("x_new")
        x_hi_done = sem("x_hi_done")
        x_lo_done = sem("x_lo_done")
        half_done = sem("half_done")
        sp_act = sem("sp_act")
        dve_own = sem("dve_own")
        act_own = sem("act_own")
        sig_done = sem("sig_done")
        glu_done = sem("glu_done")
        cache_read = sem("cache_read")
        gate_in = sem("gate_in")
        gate_zero = sem("gate_zero")
        gw_hi_done = sem("gw_hi_done")
        gw_lo_done = sem("gw_lo_done")
        gs_new_done = sem("gs_new_done")
        conv_step = sem("conv_step")
        diag_done = sem("diag_done")
        diag_free = sem("diag_free")
        xc_done = sem("xc_done")
        xc_hi_done = sem("xc_hi_done")
        xc_lo_done = sem("xc_lo_done")
        lru_act = sem("lru_act")
        lru_gain = sem("lru_gain")
        lru_sqrt = sem("lru_sqrt")
        scan_done = sem("scan_done")
        gelu_done = sem("gelu_done")
        yb_done = sem("yb_done")
        yb_hi_done = sem("yb_hi_done")
        yb_lo_done = sem("yb_lo_done")
        cn_done = sem("cn_done")
        cn_silu = sem("cn_silu")
        yc_lo_done = sem("yc_lo_done")
        conv_out = sem("conv_out")
        states_out = sem("states_out")
        p_read = sem("p_read")
        pt_hi = sem("pt_hi")
        gate_sig = sem("gate_sig")
        y_fin = sem("y_fin")
        y_out = [sem(f"y_out{s}") for s in range(2)]

        block = ctx.enter_context(nc.Block())

        gu_src = [a[f"ffn{f}_w_gu"][0].rearrange("(k p) (s i n) -> s i p k n", p=P, s=2, n=WIDE)
                  for f in (1, 2)]
        down_src = [a[f"ffn{f}_w_down"][0].rearrange("(i t p) n -> i p t n", t=G, p=P)
                    for f in (1, 2)]
        win_src = a["w_in"][0].rearrange("(k p) (u n) -> u p k n", p=P, n=WIDE)
        wout_src = a["w_out"][0].rearrange("(k p) (u n) -> u p k n", p=P, n=WIDE)
        pg_src = a["ple_w_gate"][0].rearrange("(k p) (u n) -> u p k n", p=P, n=WIDE)
        IN_UNITS = [0, 2, 1, 3, 4, 5, 6, 7]

        def wide_src(v):
            if v < WIDE0["mix"]:
                return gu_src[0][v % 2, v // 2]
            if v < WIDE0["mix"] + 8:
                return win_src[IN_UNITS[v - WIDE0["mix"]]]
            if v < WIDE0["ffn2"]:
                return wout_src[(v - WIDE0["mix"]) % 4]
            if v < WIDE0["ple"]:
                v -= WIDE0["ffn2"]
                return gu_src[1][v % 2, v // 2]
            return pg_src[(v - WIDE0["ple"]) % 4]

        def wide_gain(v):
            if v < WIDE0["mix"]:
                return "ffn1_pre_g"
            if v < WIDE0["mix"] + 8:
                return "mix_pre_g"
            if v < WIDE0["ffn2"]:
                return None
            return "ffn2_pre_g" if v < WIDE0["ple"] else "ple_norm_g"

        def wide_last_use(v):
            if v < WIDE0["mix"] or WIDE0["ffn2"] <= v < WIDE0["ple"]:
                f = int(v >= WIDE0["ffn2"])
                v -= WIDE0["ffn2"] if f else 0
                i = v // 2
                return STEP * i + gate_at(f, i, 2) + 2 + 2 * (v % 2)
            if v < WIDE0["mix"] + 8:
                u = v - WIDE0["mix"]
                return RING["vg", 2, 1 + 2 * u] + 1 if u < 2 else RING["in", u, 2, 1] + 1
            if v < WIDE0["ffn2"]:
                c, q = divmod(v - WIDE0["mix"] - 8, 4)
                return RING["wout", c, 2 * q + 1] + 1
            c, q = divmod(v - WIDE0["ple"], 4)
            return RING["ple", c, q, 3] + 1

        @block.sync
        def _(sp_eng):
            eng = sp_eng

            def load_wide(v, src=None):
                src = wide_src(v) if src is None else src
                for h in range(2):
                    if not isinstance(v, int) or v > 0:
                        eng.wait_ge(wide_lo, v * 2 + (h - 1))
                    eng.dma_start(raw[:, h * HALF:(h + 1) * HALF].rearrange(
                        "p (k n) -> p k n", n=WIDE), src[:, 4 * h:4 * h + 4]
                        ).then_inc(raw_in[h], 16)

            def load_down(d, src):
                if not isinstance(d, int) or d > 0:
                    eng.wait_ge(down_lo, d)
                eng.dma_start(rawd[:, :].rearrange("p (t n) -> p t n", t=G), src).then_inc(rawd_in, 16)

            def ffn_loads(f):
                v0, d0 = WIDE0[f"ffn{f + 1}"], NI * f
                load_down(d0, down_src[f][0])
                load_wide(v0 + 2)
                load_wide(v0 + 3)
                with eng.Fori(1, NI - 1) as i:
                    load_down(i + d0, down_src[f][i])
                    load_wide(i * 2 + (v0 + 2), gu_src[f][0, i + 1])
                    load_wide(i * 2 + (v0 + 3), gu_src[f][1, i + 1])
                load_down(d0 + NI - 1, down_src[f][NI - 1])
                load_wide(v0 + 2 * NI)
                load_wide(v0 + 2 * NI + 1)

            def store(n):
                c, q = divmod(n, 3)
                w, r0 = min(P, C - P * q), C * c + P * q
                eng.wait_ge(psum_free, RING["yT", c, 2 * q + 1] + 1)
                if n == 8:
                    w = LAST - 2 * P
                    eng.dma_start(out["y_sample"].rearrange("b t n -> (b t) n"),
                                  y_stage[w:w + NB * DEC, n % 2, :]).then_inc(y_out[n % 2], 16)
                eng.dma_start(out["y_prompt"][0, r0:r0 + w, :], y_stage[0:w, n % 2, :]
                              ).then_inc(y_out[n % 2], 16)

            for name, n in VECTORS:
                src = a[name] if name != "lru_conv_w" else a[name][0]
                eng.dma_start(rows[ROW[name]:ROW[name] + n, 0:P],
                              src.rearrange("a (k p) -> (a k) p", p=P)).then_inc(rows_in, 16)
            eng.dma_start(rows[0:CW * NJ, P:2 * P],
                          a["conv_w"][0].rearrange("a (k p) -> (a k) p", p=P)).then_inc(rows_in, 16)
            eng.dma_start(st_rows[0:NB * LH, :],
                          a["state_lru_conv"][0].rearrange("b w n -> (b w) n")).then_inc(rows_in, 16)
            eng.dma_start(st_rows[NB * LH:NB * LH + NB, :], a["state_lru_h"][0]).then_inc(rows_in, 16)
            load_wide(0)
            load_wide(1)
            ffn_loads(0)
            eng.wait_ge(psum_full, RING["ffn", 0] + NI * STEP)
            for s in range(2):
                eng.dma_start(cache_in[0:4 * CH, s, :],
                              a["cache_conv"][0, 4 * s:4 * s + 4].rearrange("b w n -> (b w) n")
                              ).then_inc(cache_read, 16)
            load_wide(WIDE0["mix"] + 2)
            eng.wait_ge(gate_zero, 1)
            for g, name in enumerate(("lru_wa", "lru_wx")):
                w = a[name][0].rearrange("(j two) r n -> two r j n", two=2)
                for half in range(2):
                    eng.dma_start(gate_raw[64 * half:64 * half + 64, g, :, 64 * half:64 * half + 64],
                                  w[half]).then_inc(gate_in, 16)
            for v in range(WIDE0["mix"] + 3, WIDE0["mix"] + 6):
                load_wide(v)
            eng.wait_ge(psum_free, RING["convout", 2] + 1)
            eng.dma_start(out["conv_p"][0, 0], cv_stage[0:CH, 0, :]).then_inc(conv_out, 16)
            for s in range(2):
                eng.dma_start(out["conv_s"][0, 4 * s:4 * s + 4].rearrange("b w n -> (b w) n"),
                              cv_stage[0:4 * CH, 1 + s, :]).then_inc(conv_out, 16)
            for v in range(WIDE0["mix"] + 6, WIDE0["mix"] + 9):
                load_wide(v)
            eng.wait_ge(psum_free, RING["state"] + 1)
            for dst, r in ((out["lconv_p"][0, 0], 0),
                           (out["lconv_s"][0].rearrange("b w n -> (b w) n"), LH),
                           (out["h_p"][0], LH + NB * LH), (out["h_s"][0], LH + NB * LH + 1)):
                eng.dma_start(dst, st_stage[r:r + dst.shape[0], :]).then_inc(states_out, 16)
            for v in range(WIDE0["mix"] + 9, WIDE0["ffn2"] + 2):
                load_wide(v)
            eng.wait_ge(yb_lo_done, 12)
            eng.wait_ge(states_out, 64)
            eng.wait_ge(x_lo_done, 3 * PAIRS + PAIRS)
            ffn_loads(1)
            load_down(2 * NI, a["ple_w_proj"][0].rearrange("(t p) n -> p t n", p=P))
            eng.wait_ge(a_lo_done, 2 * NI * NC * G)
            for c in range(NC):
                for q in range(3):
                    n, r0 = (P, C * c + P * q) if q < 2 else (C - 2 * P, C * c + 2 * P)
                    if c == 2 and q == 2:
                        n = LAST - 2 * P
                        eng.dma_start(p_in[n:n + NB * DEC, 8, :],
                                      a["p_sample"][0].rearrange("b t n -> (b t) n")
                                      ).then_inc(p_read, 16)
                    eng.dma_start(p_in[0:n, 3 * c + q, :], a["p_prompt"][0, 0, r0:r0 + n, :]
                                  ).then_inc(p_read, 16)
            for v in range(WIDE0["ple"] + 2, N_WIDE):
                load_wide(v)
            for n in range(9):
                store(n)
            for s in range(2):
                eng.wait_ge(y_out[s], (96, 64)[s])
            eng.wait_ge(conv_out, 48)
            eng.wait_ge(states_out, 64)

        @block.gpsimd
        def _(eng):
            eng.memset(ident[:, :], 0.0).then_inc(const_ready, 1)
            eng.memset(ones[:, :], 1.0).then_inc(const_ready, 1)
            eng.memset(eps_t[:, :], EPS).then_inc(const_ready, 1)
            eng.wait_ge(const_ready, 3)
            eng.affine_select(out=ident[:, :], in_=ident[:, :], compare_op=ALU.not_equal, fill=1.0,
                              base=0, pattern=[[-1, P]], channel_multiplier=1
                              ).then_inc(const_ready, 1)

        @block.tensor
        def _(eng):
            def bank(n, ncols=C):
                if n >= BANKS:
                    eng.wait_ge(psum_free, n - BANKS + 1)
                return ps[:, n % BANKS, 0:ncols]

            def bank_at(base_n, off):
                eng.wait_ge(psum_free, base_n + (off - BANKS + 1))

            def passes(dst, wh, wl, xh, xl, first, last):
                eng.matmul(dst, wl, xh, start=first, stop=False)
                eng.matmul(dst, wh, xl, start=False, stop=False)
                return eng.matmul(dst, wh, xh, start=False, stop=last)

            def wide(s, k, t):
                sl = slice(k * WIDE + t * P, k * WIDE + t * P + P)
                return w_hi[s][:, sl], w_lo[s][:, sl]

            def tile_product(dst, s, t, c):
                for k in range(KT):
                    wh, wl = wide(s, k, t)
                    mm = passes(dst, wh, wl, x_hi[:, k, cols(c)], x_lo[:, k, cols(c)],
                                k == 0, k == KT - 1)
                mm.then_inc(psum_full, 1)

            def start_products(n0, specs, c):
                dsts = [bank(n0 + i) for i in range(len(specs))]
                for k in range(KT):
                    eng.wait_ge(psum_free, RING["xT", c, k] + 1)
                    for dst, (s, t) in zip(dsts, specs):
                        wh, wl = wide(s, k, t)
                        mm = passes(dst, wh, wl, x_hi[:, k, cols(c)], x_lo[:, k, cols(c)],
                                    k == 0, k == KT - 1)
                        if k == KT - 1:
                            mm.then_inc(psum_full, 1)

            def norm_sum(name, c):
                i = NORM[name, c]
                n = AUX["norm", i]
                eng.wait_ge(add_done, ADD0[i + 1])
                if n >= 2:
                    eng.wait_ge(aux_free, n - 1)
                for q in range(3):
                    t0 = min(P * q, C - P)
                    mm = eng.matmul(ps_aux[:, n % 2, q:q + 1], ssum[:, i % 2, t0:t0 + P],
                                    ones[:, 0:1], start=True, stop=True)
                mm.then_inc(aux_full, 1)

            def norm_spread(name, c):
                i = NORM[name, c]
                n = AUX["spread", i]
                eng.wait_ge(inv_done, i + 1)
                eng.wait_ge(aux_free, n - 1)
                for q in range(3):
                    w = min(P, C - P * q)
                    mm = eng.matmul(ps_aux[:, n % 2, P * q:P * q + w],
                                    std[:, 4 + q:5 + q].broadcast_to([P, P]), ident[:, P - w:P],
                                    start=True, stop=True)
                mm.then_inc(aux_full, 1)

            def down_products(f, i, c):
                Q, off = NI * NC * G * f, down_at(f, i, c)
                eng.wait_ge(a_lo_done, i * (NC * G) + (Q + 2 * c + 2))
                for m in range(KT):
                    bank_at(i * STEP, off + m)
                    dst = ps[:, (off + m) % BANKS, 0:C]
                    for t in range(G):
                        sl = slice(t * D + m * P, t * D + m * P + P)
                        mm = passes(dst, wd_hi[:, sl], wd_lo[:, sl], a_hi[:, t, cols(c)],
                                    a_lo[:, t, cols(c)], t == 0, t == G - 1)
                    mm.then_inc(psum_full, 1)

            SPECS = [(0, 0), (0, 1), (1, 0), (1, 1)]

            def gate_products(f, i, c, hook=None):
                for t, (s, h) in enumerate(SPECS):
                    if c == 0 and h == 0:
                        wide_ready(f, i, s)
                    off = gate_at(f, i, c) + t
                    bank_at(i * STEP, off)
                    tile_product(ps[:, off % BANKS, 0:C], s, h, c)
                    if hook:
                        hook(c, t)

            def wide_ready(f, i, s):
                eng.wait_ge(wide_lo, i * 4 + (2 * WIDE0[f"ffn{f + 1}"] + 2 * (s + 1)))

            def down_ready(f, i):
                eng.wait_ge(down_lo, i + (NI * f + 1))

            def ffn_step(f, i):
                for c in range(NC):
                    gate_products(f, i, c)
                down_ready(f, i)
                for c in range(NC):
                    down_products(f, i, c)

            def ffn_first(f, x0, hook):
                for c in range(NC):
                    eng.wait_ge(x_lo_done, x0 + PAIRS * (c + 1))
                    gate_products(f, 0, c, hook)
                    if c == 1:
                        down_ready(f, 0)
                        down_products(f, 0, 0)
                        norm_sum("pre3", 2)
                        down_products(f, 0, 1)
                        norm_spread("pre3", 2)
                down_products(f, 0, 2)

            def ffn_last(f, post, pre):
                i = NI - 1
                for c in range(NC):
                    def hook(c, t):
                        if c == 1:
                            if t == 1:
                                norm_sum(post, 0)
                            if t == 2:
                                norm_spread(post, 0)
                        if c == 2:
                            if t == 1:
                                norm_sum(pre, 0)
                            if t == 2:
                                norm_spread(pre, 0)
                                norm_sum(post, 1)
                            if t == 3:
                                norm_spread(post, 1)
                    gate_products(f, i, c, hook)
                    if c == 0:
                        down_ready(f, i)
                    down_products(f, i, c)

            def norms_behind(post, pre):
                def hook(n):
                    if n == 1:
                        norm_sum(pre, 1)
                    if n == 2:
                        norm_spread(pre, 1)
                        norm_sum(post, 2)
                    if n == 3:
                        norm_spread(post, 2)
                return hook

            def to_features(src, n, c, k):
                dst = bank(n)
                for q in range(3):
                    w = min(P, C - P * q)
                    mm = eng.transpose(dst[:, P * q:P * q + w],
                                       src(3 * c + q)[0:w, k * P:k * P + P], ident[0:w, 0:w])
                mm.then_inc(psum_full, 1)

            eng.wait_ge(const_ready, 4)
            for c in range(NC):
                eng.wait_ge(x_read[c], 48 + 16 * (c == 2))
                for k in range(KT):
                    to_features(piece, RING["xT", c, k], c, k)
                if c == 0:
                    eng.wait_ge(rows_in, 16 * (len(VECTORS) + 3))
                    dst = bank(RING["params"], 512)
                    eng.transpose(dst[:, 0:NROWS], rows[0:NROWS, 0:P], ident[0:NROWS, 0:NROWS])
                    eng.transpose(dst[:, P:P + CW * NJ], rows[0:CW * NJ, P:2 * P],
                                  ident[0:CW * NJ, 0:CW * NJ])
                    for j in range(NJ):
                        mm = eng.transpose(dst[:, 2 * P + 32 * j:2 * P + 32 * j + 32],
                                           st_rows[0:32, j * P:j * P + P], ident[0:32, 0:32])
                    mm.then_inc(psum_full, 1)
                    eng.wait_ge(wide_lo, 2)
                start_products(gate_at(0, 0, c), SPECS[:2], c)
                norm_sum("pre1", c)
                if c == 0:
                    eng.wait_ge(wide_lo, 4)
                start_products(gate_at(0, 0, c) + 2, SPECS[2:3], c)
                norm_spread("pre1", c)
                start_products(gate_at(0, 0, c) + 3, SPECS[3:], c)
            down_ready(0, 0)
            for c in range(NC):
                down_products(0, 0, c)
            with eng.Fori(1, NI - 1) as i:
                ffn_step(0, i)
            ffn_last(0, "post1", "pre2")

            eng.wait_ge(wide_lo, 2 * (WIDE0["mix"] + 1))
            behind = norms_behind("post1", "pre2")
            for c in range(NC):
                eng.wait_ge(x_lo_done, PAIRS * (c + 1))
                for n in range(4):
                    if (c, n) == (0, 2):
                        eng.wait_ge(wide_lo, 2 * (WIDE0["mix"] + 2))
                    tile_product(bank(RING["vg", c, n]), n // 2, n % 2, c)
                    behind(4 * c + n)
                    if (c, n) == (2, 1):
                        norm_sum("pre2", 2)
                    if (c, n) == (2, 2):
                        norm_spread("pre2", 2)
            eng.wait_ge(cache_read, 32)
            for s in range(2):
                dst = bank(RING["cache", s], 4 * 4 * CH)
                for j in range(NJ):
                    mm = eng.transpose(dst[:, j * 4 * CH:(j + 1) * 4 * CH],
                                       cache_in[0:4 * CH, s, j * P:j * P + P],
                                       ident[0:4 * CH, 0:4 * CH])
                mm.then_inc(psum_full, 1)

            def lru_gates(x):
                j, c, t = lru_tile(x)
                eng.wait_ge(xc_lo_done, x + 1)
                for g, which in enumerate("ri"):
                    n = AUX[which, x]
                    eng.wait_ge(aux_free, n - 1)
                    passes(ps_aux[:, n % 2, 0:C], gw_hi[:, g, j, :], gw_lo[:, g, j, :],
                           xc_hi[:, x % 2, :], xc_lo[:, x % 2, :], True, True
                           ).then_inc(aux_full, 1)

            def in_unit(u, behind=None):
                eng.wait_ge(wide_lo, 2 * (WIDE0["mix"] + u + 1))
                for c in range(NC):
                    for t in range(2):
                        tile_product(bank(RING["in", u, c, t]), u % 2, t, c)
                        if behind:
                            behind(2 * c + t)

            def conv_group(j, c):
                dst = bank(RING["conv", j, c])
                w = C if c < 2 else LAST
                eng.wait_ge(glu_done, 6 * (j // 2 + 1))
                for tap in range(TP if c == 2 else 0):
                    eng.matmul(dst[:, w:C].rearrange("p (b t) -> p b t", b=NB), diag[:, tap, :],
                               gs[:, j, :, tap:tap + DEC], start=tap == 0, stop=tap == TP - 1)
                for tap in range(TP):
                    if c == 0:
                        eng.wait_ge(diag_done, TP * j + tap + 1)
                    at0 = C * c + tap
                    mm = eng.matmul(dst[:, 0:w], diag[:, tap, :], gp[:, j, at0:at0 + w],
                                    start=tap == 0, stop=tap == TP - 1)
                    if c == 2 and tap < TP - 1:
                        mm.then_inc(diag_free, 1)
                mm.then_inc(psum_full, 1)

            def conv_states():
                eng.wait_ge(gs_new_done, 1)
                for s in range(3):
                    n = RING["convout", s]
                    eng.wait_ge(psum_free, n - BANKS + 1)
                    for j in range(NJ):
                        src = gp[:, j, SEQ:SEQ + CH] if s == 0 else \
                            gs_new[:, j, (4 * s - 4) * CH:4 * s * CH]
                        w = CH if s == 0 else 4 * CH
                        mm = eng.transpose(ps[0:w, n % BANKS, j * P:j * P + P], src, ident[:, :])
                    mm.then_inc(psum_full, 1)

            in_unit(2)
            in_unit(3)
            for x in range(NJ * NC):
                j, c, t = lru_tile(x)
                u = 4 + x // 6
                if x % 6 == 0:
                    eng.wait_ge(wide_lo, 2 * (WIDE0["mix"] + u + 1))
                tile_product(bank(RING["in", u, c, t]), u % 2, t, c)
                conv_group(x // NC, x % NC)
                if x == 0:
                    conv_states()
                    eng.wait_ge(gw_lo_done, 1)
                lru_gates(x)

            def gelu_hook(n):
                if n % 4 == 3:
                    norm_sum("conv", n // 4)
                if n % 4 == 0 and n:
                    norm_spread("conv", n // 4 - 1)

            in_unit(6, gelu_hook)
            eng.wait_ge(scan_done, 12)
            n = RING["state"]
            eng.wait_ge(psum_free, n - BANKS + 1)
            for j in range(NJ):
                mm = eng.transpose(ps[0:36, n % BANKS, j * P:j * P + P], st_out[:, j, :], ident[:, :])
            mm.then_inc(psum_full, 1)
            in_unit(7, lambda n: gelu_hook(n + 6))

            def out_unit(c, q):
                v = WIDE0["mix"] + 8 + 4 * c + q
                eng.wait_ge(wide_lo, 2 * (v + 1))
                if q == 0:
                    eng.wait_ge(yc_lo_done, NJ * (c + 1))
                    eng.wait_ge(yb_lo_done, 8 + 2 * c)
                for t in range(2):
                    dst = bank(RING["wout", c, 2 * q + t])
                    for k in range(KT):
                        wh, wl = wide(v % 2, k, t)
                        mm = passes(dst, wh, wl, y_hi[:, k, cols(c)], y_lo[:, k, cols(c)],
                                    k == 0, k == KT - 1)
                    mm.then_inc(psum_full, 1)
                    out_norms(c, 2 * q + t)

            def out_norms(c, n):
                if c == 0:
                    if n == 0:
                        norm_spread("conv", 2)
                    return
                if c > 1 and n == 1:
                    norm_sum("pre3", c - 2)
                if n == 2:
                    if c > 1:
                        norm_spread("pre3", c - 2)
                    norm_sum("post2", c - 1)
                if n == 3:
                    norm_spread("post2", c - 1)

            for c in range(NC):
                for q in range(4):
                    out_unit(c, q)

            def hook(c, n):
                if c == 0:
                    out_norms(3, n)

            ffn_first(1, 3 * PAIRS, hook)
            with eng.Fori(1, NI - 1) as i:
                ffn_step(1, i)
            ffn_last(1, "post3", "pre4")

            def p_to_features():
                eng.wait_ge(p_read, 16 * 10)
                for c in range(NC):
                    for k in range(PT):
                        to_features(lambda i: p_in[:, i, :], RING["pT", c, k], c, k)

            behind = norms_behind("post3", "pre4")

            def ple_unit(c, q):
                v = WIDE0["ple"] + 4 * c + q
                eng.wait_ge(wide_lo, 2 * (v + 1))
                if q == 0:
                    eng.wait_ge(x_lo_done, 6 * PAIRS + PAIRS * (c + 1))
                for t in range(2):
                    tile_product(bank(RING["ple", c, q, t]), v % 2, t, c)
                    if (c, t) == (0, 0) and q in (1, 2):
                        behind(1 + q)
                if (c, q) == (0, 0):
                    p_to_features()
                    behind(1)
                if (c, q) == (0, 0):
                    eng.wait_ge(down_lo, 2 * NI + 1)
                    eng.wait_ge(psum_free, RING["pT", 2, 1] + 1)
                for t in range(2):
                    dst = bank(RING["ple", c, q, 2 + t])
                    for k in range(PT):
                        sl = slice(k * D + (2 * q + t) * P, k * D + (2 * q + t) * P + P)
                        mm = passes(dst, wd_hi[:, sl], wd_lo[:, sl], a_hi[:, k, cols(c)],
                                    a_lo[:, k, cols(c)], k == 0, k == PT - 1)
                    mm.then_inc(psum_full, 1)

            def to_tokens(c):
                for q in range(3):
                    w = min(P, C - P * q)
                    for half in range(2):
                        n = RING["yT", c, 2 * q + half]
                        eng.wait_ge(psum_free, n - BANKS + 1)
                        for k in range(4):
                            kk = 4 * half + k
                            eng.wait_ge(y_fin, PAIRS * c + kk // 2 + 1)
                            mm = eng.transpose(ps[0:w, n % BANKS, k * P:k * P + P],
                                               acc[:, kk, C * c + P * q:C * c + P * q + w],
                                               ident[:, :])
                        mm.then_inc(psum_full, 1)

            for q in range(4):
                ple_unit(0, q)
            ple_unit(1, 0)
            ple_unit(1, 1)
            ple_unit(1, 2)
            norm_sum("pre4", 2)
            ple_unit(1, 3)
            norm_spread("pre4", 2)
            norm_sum("post4", 0)
            ple_unit(2, 0)
            norm_spread("post4", 0)
            ple_unit(2, 1)
            norm_sum("post4", 1)
            ple_unit(2, 2)
            to_tokens(0)
            norm_spread("post4", 1)
            ple_unit(2, 3)
            norm_sum("post4", 2)
            norm_spread("post4", 2)
            to_tokens(1)
            to_tokens(2)

        @block.scalar
        def _(eng):
            own = [0]

            def done(ins):
                own[0] += 1
                ins.then_inc(act_own, 1)
                eng.wait_ge(act_own, own[0])

            def split_half(v, h, s=None, gain=None, last_use=None):
                if s is None:
                    s, gain = v % 2, wide_gain(v)
                if last_use is None and v >= 2:
                    last_use = wide_last_use(v - 2)
                if last_use is not None and h == 0:
                    eng.wait_ge(psum_full, last_use)
                eng.wait_ge(raw_in[h], v * 16 + 16)
                if gain is None:
                    sl = slice(h * HALF, (h + 1) * HALF)
                    eng.activation(w_hi[s][:, sl], raw[:, sl], ACT.Copy).then_inc(wide_hi, 1)
                    return
                for k in range(4 * h, 4 * h + 4):
                    sl = slice(k * WIDE, (k + 1) * WIDE)
                    ins = eng.activation(w_hi[s][:, sl], raw[:, sl], ACT.Copy, scale=vec(gain, k))
                ins.then_inc(wide_hi, 1)

            def split_wide(v):
                for h in range(2):
                    split_half(v, h)

            def split_down(d, last_use=None):
                if last_use is not None:
                    eng.wait_ge(psum_full, last_use)
                eng.wait_ge(rawd_in, d * 16 + 16)
                eng.activation(wd_hi[:, :], rawd[:, :], ACT.Copy).then_inc(down_hi, 1)

            def square(i, m, src, src_sem=None, count=None):
                if src_sem is not None:
                    eng.wait_ge(src_sem, count)
                if m == 0:
                    if i > 1:
                        eng.wait_ge(aux_full, AUX["norm", i - 2] + 1)
                    dst = ssum[:, i % 2, :]
                else:
                    n = ADD0[i] + m - 1
                    if n >= SQ:
                        eng.wait_ge(add_done, n - SQ + 1)
                    dst = sq[:, n % SQ, :]
                eng.activation(dst, src, ACT.Square).then_inc(sq_done, 1)

            def root(name, c):
                i = NORM[name, c]
                n = AUX["norm", i]
                eng.wait_ge(aux_full, n + 1)
                if i > 0:
                    eng.wait_ge(inv_done, i)
                eng.activation(std[:, 0:3], ps_aux[:, n % 2, 0:3], ACT.Sqrt,
                               scale=1.0 / (P * TILES[i]), bias=eps_t[:, :]).then_inc(aux_free, 1)

            def spread(name, c):
                i = NORM[name, c]
                n = AUX["spread", i]
                eng.wait_ge(aux_full, n + 1)
                eng.activation(rstd_tile(i), ps_aux[:, n % 2, 0:C], ACT.Copy).then_inc(aux_free, 1)

            def squares(name, c, src, sem_, count0):
                i = NORM[name, c]
                for m in range(TILES[i]):
                    square(i, m, src(m), sem_, count0 + m + 1)

            def apply_pair(name, c, x0, src, q):
                i = NORM[name, c]
                eng.wait_ge(x_new, x0 + PAIRS * c + q + 1)
                eng.activation(x_hi[:, 2 * q:2 * q + 2, cols(c)], src(c, 2 * q, 2), ACT.Copy
                               ).then_inc(x_hi_done, 1)
                for m in (2 * q, 2 * q + 1):
                    square(i, m, src(c, m)[:, 0, :])

            def silu(f, i, c, h):
                R, Q = RING["ffn", f], NI * NC * G * f
                q, n = NC * G * i + (Q + 2 * c + h), STEP * i + (gate_at(f, i, c) + h)
                eng.wait_ge(psum_free, n + 1)
                if f or not isinstance(i, int) or i or c:
                    eng.wait_ge(prod_done, q - 1)
                eng.activation(tmp_s[:, h, :], tmp_g[:, h, :], ACT.Silu).then_inc(silu_done, 1)

            def hidden_hi(f, i, c, h):
                R, Q = RING["ffn", f], NI * NC * G * f
                eng.wait_ge(prod_done, NC * G * i + (Q + 2 * c + h + 1))
                if not isinstance(i, int) or i:
                    eng.wait_ge(psum_full, STEP * i + (R - STEP + 4 * NC + KT * (c + 1)))
                eng.activation(a_hi[:, h, cols(c)], tmp_a[:, h, :], ACT.Copy).then_inc(a_hi_done, 1)

            def hidden_chunk(f, i, c, next_half, hook=None):
                hook = hook or (lambda at: None)
                silu(f, i, c, 0)
                hook("g0")
                silu(f, i, c, 1)
                hook("g1")
                hook("u0")
                last = isinstance(i, int) and (i == NI - 1 or f == 1)
                if c == 2 and not last:
                    next_half(0, 0)
                hidden_hi(f, i, c, 0)
                hidden_hi(f, i, c, 1)
                if c == 2 and not last:
                    next_half(0, 1)
                if c == 2 and last:
                    next_half(0, 0)
                    next_half(0, 1)
                hook("lo")

            def halves(f, i):
                def next_half(s, h):
                    V = WIDE0[f"ffn{f + 1}"]
                    if isinstance(i, int) and i == NI - 1:
                        split_half(V + 2 * NI + s, h)
                    else:
                        split_half(i * 2 + (V + 2 + s), h, s, f"ffn{f + 1}_pre_g",
                                   i * STEP + (gate_at(f, i, 2) + 2 + 2 * s))
                return next_half

            def down_hi_part(f, i):
                split_down(i + NI * f, None if isinstance(i, int) and i == 0
                           else i * STEP + RING["ffn", f])

            def ffn_step(f, i, hook=None):
                for c in range(NC):
                    hidden_chunk(f, i, c, halves(f, i), hook and (lambda at: hook(c, at)))
                    if c == 0:
                        down_hi_part(f, i)
                for h in range(2):
                    halves(f, i)(1, h)

            def down_squares(f, post, c):
                for m in range(KT):
                    square(NORM[post, c], m, acc_tile(c, m)[:, 0, :], psum_free,
                           (NI - 1) * STEP + down_at(f, NI - 1, c) + m + 1)

            def ffn_last(f, post, pre, x0):
                i = NI - 1
                for c in range(NC):
                    def hook(at):
                        if c == 0 and at == "g0":
                            down_hi_part(f, i)
                        if c == 1 and at == "g1":
                            root(post, 0)
                            spread(post, 0)
                        if c == 2 and at == "u0":
                            root(pre, 0)
                            spread(pre, 0)
                            root(post, 1)
                            spread(post, 1)
                    hidden_chunk(f, i, c, halves(f, i), hook)
                    for q in range(4 if c else 0):
                        apply_pair(pre, c - 1, x0, acc_tile, q)
                        if c == 2 and q > 1:
                            halves(f, i)(1, q - 2)
                    if (f, c) != (1, 2):
                        down_squares(f, post, c)

            for c in range(NC):
                for q in range(3):
                    n, r0 = (P, C * c + P * q) if q < 2 else (C - 2 * P, C * c + 2 * P)
                    if c == 2 and q == 2:
                        n = LAST - 2 * P
                        eng.dma_start(x_in8[n:n + NB * DEC, 0, :],
                                      a["x_sample"].rearrange("b t n -> (b t) n")
                                      ).then_inc(x_read[c], 16)
                    eng.dma_start(piece(3 * c + q)[0:n, :], a["x_prompt"][0, r0:r0 + n, :]
                                  ).then_inc(x_read[c], 16)
            eng.wait_ge(const_ready, 4)
            for c in range(NC):
                for k in range(KT):
                    n = RING["xT", c, k]
                    eng.wait_ge(psum_full, n + 1)
                    eng.activation(x_hi[:, k, cols(c)], ps[:, n % BANKS, 0:C], ACT.Copy)
                    square(NORM["pre1", c], k, ps[:, n % BANKS, 0:C])
                if c == 0:
                    eng.wait_ge(half_done, 1)
                    split_wide(0)
                    split_wide(1)
                root("pre1", c)
                spread("pre1", c)
                hidden_chunk(0, 0, c, halves(0, 0),
                             lambda at: (c, at) == (2, "g0") and down_hi_part(0, 0))
                if c == 0:
                    eng.activation(sp[:, 1, :], sp[:, 0, :], ACT.Exp).then_inc(sp_act, 1)
            for h in range(2):
                halves(0, 0)(1, h)
            with eng.Fori(1, NI - 1) as i:
                ffn_step(0, i)
            ffn_last(0, "post1", "pre2", 0)

            def p_to_features():
                for c in range(NC):
                    for k in range(PT):
                        n = RING["pT", c, k]
                        eng.wait_ge(psum_full, n + 1)
                        eng.activation(a_hi[:, k, cols(c)], ps[:, n % BANKS, 0:C], ACT.Copy
                                       ).then_inc(pt_hi, 1)

            def sigmoid_glu(n, ring_n):
                b = n % 2
                eng.wait_ge(psum_free, ring_n + 1)
                eng.activation(glu[:, b, :], glu[:, b, :], ACT.Sigmoid).then_inc(sig_done, 1)

            def glu_batch(c):
                for t in range(2):
                    sigmoid_glu(2 * c + t, RING["vg", c, 2 + t])

            root("pre2", 1)
            spread("pre2", 1)
            root("post1", 2)
            spread("post1", 2)
            glu_batch(0)
            for q in range(4):
                apply_pair("pre2", 2, 0, acc_tile, q)
            glu_batch(1)
            root("pre2", 2)
            spread("pre2", 2)
            split_wide(WIDE0["mix"] + 2)
            glu_batch(2)
            eng.wait_ge(gate_in, 64)
            eng.activation(gw_hi[:, :, :, :], gate_raw[:, :, :, :], ACT.Copy).then_inc(gw_hi_done, 1)
            split_wide(WIDE0["mix"] + 3)
            split_wide(WIDE0["mix"] + 4)
            for c in range(NC):
                for t in range(2):
                    sigmoid_glu(6 + 2 * c + t, RING["in", 3, c, t])
            split_wide(WIDE0["mix"] + 5)

            def lru_front(x):
                eng.wait_ge(xc_done, x + 1)
                if x >= 2:
                    eng.wait_ge(aux_full, AUX["i", x - 2] + 1)
                eng.activation(xc_hi[:, x % 2, :], xc[:, x % 2, :], ACT.Copy).then_inc(xc_hi_done, 1)

            def lru_gates(x):
                j, c, t = lru_tile(x)
                nr, ni = AUX["r", x], AUX["i", x]
                if x > 0:
                    eng.wait_ge(scan_done, x)
                eng.wait_ge(aux_full, nr + 1)
                eng.activation(lru_r[:, :], ps_aux[:, nr % 2, 0:C], ACT.Sigmoid,
                               bias=vec("lru_ba", j)).then_inc(aux_free, 1)
                eng.wait_ge(aux_full, ni + 1)
                eng.activation(lru_i[:, :], ps_aux[:, ni % 2, 0:C], ACT.Sigmoid,
                               bias=vec("lru_bx", j)).then_inc(aux_free, 1)
                eng.wait_ge(aux_free, nr + 1)
                eng.activation(lru_a[:, :], lru_r[:, :], ACT.Exp, scale=sp[:, 6, j:j + 1]
                               ).then_inc(lru_act, 1)
                eng.wait_ge(lru_act, 3 * x + 1)
                eng.activation(lru_r[:, :], lru_r[:, :], ACT.Tanh, scale=sp[:, 7, j:j + 1]
                               ).then_inc(lru_act, 1)
                eng.activation(lru_q[:, :], lru_a[:, :], ACT.Square).then_inc(lru_act, 1)

            def lru_root(x):
                eng.wait_ge(lru_gain, x + 1)
                eng.activation(lru_q[:, :], lru_q[:, :], ACT.Sqrt).then_inc(lru_sqrt, 1)

            def diagonals(j):
                for tap in range(TP):
                    if j and tap < TP - 1:
                        eng.wait_ge(diag_free, (TP - 1) * (j - 1) + tap + 1)
                    elif j:
                        eng.wait_ge(psum_full, RING["conv", j - 1, 2] + 1)
                    eng.activation(diag[:, tap, :], ident[:, :], ACT.Copy, scale=conv_w(tap, j)
                                   ).then_inc(diag_done, 1)

            diagonals(0)
            for x in range(12):
                lru_front(x)
                if x > 0:
                    lru_root(x - 1)
                if x % 3 == 2 and x < 11:
                    diagonals(x // 3 + 1)
                lru_gates(x)
                if x == 5:
                    split_wide(WIDE0["mix"] + 6)

            def gelu(n):
                j, c, t = lru_tile(n)
                eng.wait_ge(psum_free, RING["in", 6 + n // 6, c, t] + 1)
                eng.activation(ge[:, n % 2, :], ge[:, n % 2, :], ACT.Gelu_apprx_tanh
                               ).then_inc(gelu_done, 1)

            def yb_hi(n):
                j, c, t = lru_tile(n)
                eng.wait_ge(yb_done, n + 1)
                if n == 0:
                    eng.wait_ge(aux_full, AUX["i", 11] + 1)
                eng.activation(y_hi[:, NJ + j, cols(c)], ge[:, n % 2, :], ACT.Copy
                               ).then_inc(yb_hi_done, 1)

            def conv_squares(c):
                for j in range(NJ):
                    square(NORM["conv", c], j, conv[:, j, cols(c)], psum_free,
                           RING["conv", 3, c] + 1)

            def conv_silu(c):
                for j in range(NJ):
                    eng.wait_ge(cn_done, NJ * c + j + 1)
                    done(eng.activation(conv[:, j, cols(c)], conv[:, j, cols(c)], ACT.Silu,
                                        scale=vec("conv_norm_g", j)))
                    eng.activation(y_hi[:, j, cols(c)], conv[:, j, cols(c)], ACT.Copy
                                   ).then_inc(cn_silu, 1)

            lru_root(11)
            for n in range(12):
                c, part = divmod(n, 4)
                if n == 1:
                    split_wide(WIDE0["mix"] + 7)
                if n == 6:
                    split_wide(WIDE0["mix"] + 8)
                gelu(n)
                if n:
                    yb_hi(n - 1)
                if part == 1:
                    conv_squares(c)
                if part == 3:
                    root("conv", c)
                if part == 0 and c:
                    spread("conv", c - 1)
                    conv_silu(c - 1)
            yb_hi(11)
            split_wide(WIDE0["mix"] + 9)
            spread("conv", 2)
            conv_silu(2)

            def oc_copy(c, m):
                n = RING["wout", c, m]
                eng.wait_ge(psum_full, n + 1)
                if (c, m) == (0, 0):
                    eng.wait_ge(psum_free, n)
                eng.activation(oc_tile(c, m)[:, 0, :], ps[:, n % BANKS, 0:C], ACT.Copy
                               ).then_inc(psum_free, 1)

            def behind_out(c, m):
                if m == 1 and c > 1:
                    root("pre3", c - 2)
                if m == 2:
                    if c > 1:
                        spread("pre3", c - 2)
                    root("post2", c - 1)
                if m == 3:
                    spread("post2", c - 1)
                for q in {4: (0,), 5: (1,), 7: (2, 3)}.get(m, ()):
                    apply_pair("pre3", c - 1, 3 * PAIRS, oc_tile, q)

            for c in range(NC):
                for m in range(KT):
                    oc_copy(c, m)
                    if m % 2:
                        split_wide(WIDE0["mix"] + 8 + 4 * c + m // 2 + 2)
                    if c:
                        behind_out(c, m)
                for m in range(KT):
                    square(NORM["post2", c], m, oc_tile(c, m)[:, 0, :], psum_free,
                           RING["wout", c, m] + 1)

            def hook(c, at):
                if (c, at) == (0, "u0"):
                    for m in (1, 2, 3):
                        behind_out(3, m)
                if c < 2 and at == "lo":
                    for q in (2 * c, 2 * c + 1):
                        apply_pair("pre3", 2, 3 * PAIRS, oc_tile, q)
                if (c, at) == (1, "lo"):
                    root("pre3", 2)
                    spread("pre3", 2)

            ffn_step(1, 0, hook)
            with eng.Fori(1, NI - 1) as i:
                ffn_step(1, i)
            ffn_last(1, "post3", "pre4", 6 * PAIRS)

            def gate_unit(c, q, hook=None):
                for t in range(2):
                    eng.wait_ge(psum_free, RING["ple", c, q, t] + 1)
                    z = acc[:, 2 * q + t, cols(c)]
                    eng.activation(z, z, ACT.Sigmoid).then_inc(gate_sig, 1)
                if hook:
                    hook()
                v = WIDE0["ple"] + 4 * c + q + 2
                if v < N_WIDE:
                    split_wide(v)

            def z_squares(c):
                i = NORM["post4", c]
                for m in range(KT):
                    square(i, m, acc[:, m, cols(c)], psum_free,
                           RING["ple", c, m // 2, 2 + m % 2] + 1)

            def stage_out(c):
                for q in range(3):
                    w, n = min(P, C - P * q), 3 * c + q
                    if n >= 2:
                        eng.wait_ge(y_out[n % 2], 16 * (n // 2))
                    for half in range(2):
                        k = RING["yT", c, 2 * q + half]
                        eng.wait_ge(psum_full, k + 1)
                        if q + half == 0:
                            eng.wait_ge(psum_free, k)
                        eng.activation(y_stage[0:w, n % 2, 512 * half:512 * half + 512],
                                       ps[0:w, k % BANKS, :], ACT.Copy).then_inc(psum_free, 1)

            split_down(2 * NI, RING["ffn", 1] + NI * STEP)
            gate_unit(0, 0, p_to_features)
            root("pre4", 1)
            down_squares(1, "post3", 2)
            gate_unit(0, 1, lambda: spread("pre4", 1))
            root("post3", 2)
            spread("post3", 2)
            for q in range(4):
                apply_pair("pre4", 2, 6 * PAIRS, acc_tile, q)
                gate_unit(*divmod(q + 2, 4))
            z_squares(0)
            gate_unit(1, 2)
            root("pre4", 2)
            gate_unit(1, 3)
            spread("pre4", 2)
            root("post4", 0)
            gate_unit(2, 0)
            spread("post4", 0)
            z_squares(1)
            gate_unit(2, 1)
            root("post4", 1)
            gate_unit(2, 2)
            stage_out(0)
            spread("post4", 1)
            gate_unit(2, 3)
            z_squares(2)
            root("post4", 2)
            spread("post4", 2)
            stage_out(1)
            stage_out(2)

        @block.vector
        def _(eng):
            own = [0]

            def mark(ins):
                own[0] += 1
                ins.then_inc(dve_own, 1)
                return own[0]

            def done(ins):
                mark(ins)
                eng.wait_ge(dve_own, own[0])

            def bank(n):
                eng.wait_ge(psum_full, n + 1)
                return ps[:, n % BANKS, 0:C]

            def bank_at(reg, n):
                eng.wait_ge(psum_full, reg + (n + 1))
                return ps[:, n % BANKS, 0:C]

            def split_tile(v, k, s=None, gain=None):
                if s is None:
                    s, gain = v % 2, wide_gain(v)
                h = k // 4
                if k % 4 == 0:
                    eng.wait_ge(wide_hi, v * 2 + (h + 1))
                    if gain is None:
                        sl = slice(h * HALF, (h + 1) * HALF)
                        eng.tensor_tensor(w_lo[s][:, sl], raw[:, sl], f32(w_hi[s][:, sl]),
                                          ALU.subtract).then_inc(wide_lo, 1)
                if gain is None:
                    return
                sl = slice(k * WIDE, (k + 1) * WIDE)
                ins = eng.scalar_tensor_tensor(w_lo[s][:, sl], raw[:, sl], vec(gain, k),
                                               f32(w_hi[s][:, sl]), ALU.mult, ALU.subtract)
                if k % 4 == 3:
                    ins.then_inc(wide_lo, 1)

            def split_half(v, h):
                for k in range(4 * h, 4 * h + 4):
                    split_tile(v, k)

            def split_wide(v):
                for h in range(2):
                    split_half(v, h)

            def split_down(d):
                eng.wait_ge(down_hi, d + 1)
                eng.tensor_tensor(wd_lo[:, :], rawd[:, :], f32(wd_hi[:, :]), ALU.subtract
                                  ).then_inc(down_lo, 1)

            def add_square(i, m):
                eng.wait_ge(sq_done, SQ0[i] + m + 1)
                if ADD0[i] + m - 1 > 0:
                    eng.wait_ge(add_done, ADD0[i] + m - 1)
                eng.tensor_tensor(ssum[:, i % 2, :], ssum[:, i % 2, :], sq[:, (ADD0[i] + m - 1) % SQ, :],
                                  ALU.add
                                  ).then_inc(add_done, 1)

            def add_squares(name, c):
                i = NORM[name, c]
                for m in range(1, TILES[i]):
                    add_square(i, m)

            def invert(name, c):
                i = NORM[name, c]
                eng.wait_ge(aux_free, AUX["norm", i] + 1)
                if i:
                    eng.wait_ge(aux_full, AUX["spread", i - 1] + 1)
                eng.reciprocal(std[:, 4:7], std[:, 0:3]).then_inc(inv_done, 1)

            def rstd(name, c):
                i = NORM[name, c]
                eng.wait_ge(aux_free, AUX["spread", i] + 1)
                return rstd_tile(i)

            def apply_pair(post, c, x0, src, gain, pre, q):
                r, m, two = rstd(post, c), 2 * q, src(c, 2 * q, 2)
                n = mark(eng.tensor_tensor(two, two, r.unsqueeze(1).broadcast_to([P, 2, C]),
                                           ALU.mult))
                eng.wait_ge(dve_own, n)
                for h in range(2):
                    t = src(c, m + h)[:, 0, :]
                    n = mark(eng.scalar_tensor_tensor(t, t, gain(m + h),
                                                      f32(x_hi[:, m + h, cols(c)]),
                                                      ALU.mult, ALU.add))
                eng.wait_ge(dve_own, n)
                eng.tensor_tensor(two, two, f32(x_lo[:, m:m + 2, cols(c)]), ALU.add
                                  ).then_inc(x_new if pre else y_fin, 1)
                for p in ((q - 1, q) if q == 3 else (q - 1,)):
                    if pre and p >= 0:
                        eng.wait_ge(x_hi_done, x0 + PAIRS * c + p + 1)
                        eng.tensor_tensor(x_lo[:, 2 * p:2 * p + 2, cols(c)], src(c, 2 * p, 2),
                                          f32(x_hi[:, 2 * p:2 * p + 2, cols(c)]), ALU.subtract
                                          ).then_inc(x_lo_done, 1)
                        for k in (2 * p, 2 * p + 1):
                            if k:
                                add_square(NORM[pre, c], k)

            def scaled(f, i, c, h, up):
                R, Q = RING["ffn", f], NI * NC * G * f
                q, off = NC * G * i + (Q + 2 * c + h), gate_at(f, i, c) + 2 * up + h
                src = bank_at(i * STEP, off)
                if f or not isinstance(i, int) or i or c:
                    eng.wait_ge(prod_done if up else silu_done, q - 1)
                eng.tensor_tensor((tmp_u if up else tmp_g)[:, h, :], src, rstd_pre[:, cols(c)],
                                  ALU.mult).then_inc(psum_free, 1)

            def hidden(f, i, c, h):
                R, Q = RING["ffn", f], NI * NC * G * f
                q, n = NC * G * i + (Q + 2 * c + h), STEP * i + (gate_at(f, i, c) + 2 + h)
                eng.wait_ge(silu_done, q + 1)
                eng.wait_ge(psum_free, n + 1)
                if f or not isinstance(i, int) or i or c:
                    eng.wait_ge(a_lo_done, q - 1)
                eng.tensor_tensor(tmp_a[:, h, :], tmp_s[:, h, :], tmp_u[:, h, :], ALU.mult
                                  ).then_inc(prod_done, 1)

            def hidden_lo(f, i, c, h):
                q = NC * G * i + (NI * NC * G * f + 2 * c + h)
                eng.wait_ge(a_hi_done, q + 1)
                eng.tensor_tensor(a_lo[:, h, cols(c)], tmp_a[:, h, :], f32(a_hi[:, h, cols(c)]),
                                  ALU.subtract).then_inc(a_lo_done, 1)

            def hidden_chunk(f, i, c, next_tile, hook=None):
                hook = hook or (lambda at: None)
                if isinstance(i, int) and i == 0:
                    rstd(f"pre{1 + 2 * f}", c)
                scaled(f, i, c, 0, 0)
                hook("g0")
                scaled(f, i, c, 1, 0)
                hook("g1")
                scaled(f, i, c, 0, 1)
                hook("u0")
                last = isinstance(i, int) and (i == NI - 1 or f == 1)
                if c == 2 and not last:
                    for k in range(4):
                        next_tile(0, k)
                scaled(f, i, c, 1, 1)
                hidden(f, i, c, 0)
                hidden(f, i, c, 1)
                if c == 2 and not last:
                    return
                hidden_lo(f, i, c, 0)
                hidden_lo(f, i, c, 1)
                if c == 2:
                    for k in range(8):
                        next_tile(0, k)
                hook("lo")

            def tiles(f, i):
                def next_tile(s, k):
                    V = WIDE0[f"ffn{f + 1}"]
                    if isinstance(i, int) and i == NI - 1:
                        split_tile(V + 2 * NI + s, k)
                    else:
                        split_tile(i * 2 + (V + 2 + s), k, s, f"ffn{f + 1}_pre_g")
                return next_tile

            def down(f, i, c, m):
                off = down_at(f, i, c) + m
                src = bank_at(i * STEP, off)
                if isinstance(i, int) and i == 0:
                    eng.tensor_copy(acc[:, m, cols(c)], src).then_inc(psum_free, 1)
                    return
                before = down_at(f, None, c) + m - STEP
                eng.wait_ge(psum_free, STEP * i + (before + 1))
                eng.tensor_tensor(acc[:, m, cols(c)], src, acc[:, m, cols(c)], ALU.add
                                  ).then_inc(psum_free, 1)

            def ffn_step(f, i, hook=None):
                for c in range(NC):
                    hidden_chunk(f, i, c, tiles(f, i), hook and (lambda at: hook(c, at)))
                    if c == 0:
                        split_down(i + NI * f)
                down_sums(f, i)

            def down_sums(f, i):
                for c in range(NC):
                    for m in range(KT):
                        down(f, i, c, m)
                        if (c, m) == (0, 1):
                            hidden_lo(f, i, 2, 0)
                            hidden_lo(f, i, 2, 1)
                        if c == 0 and 2 <= m < 6:
                            tiles(f, i)(0, m + 2)
                        if c == 1:
                            tiles(f, i)(1, m)

            def half_gain(f):
                return lambda m: half_g[:, KT * f + m:KT * f + m + 1]

            def ffn_last(f, post, pre, x0):
                i = NI - 1
                for c in range(NC):
                    def pair(q):
                        if c:
                            apply_pair(post, c - 1, x0, acc_tile, half_gain(f), pre, q)

                    def hook(at):
                        if c == 0 and at == "g0":
                            split_down(i + NI * f)
                        if c and at == "g1":
                            invert(*((post, 0) if c == 1 else (pre, 0)))
                        if c == 2 and at == "u0":
                            invert(post, 1)
                    hidden_chunk(f, i, c, tiles(f, i), hook)
                    pair(0)
                    for m in range(KT):
                        down(f, i, c, m)
                        if m in (2, 5, 7):
                            q = 1 + (2, 5, 7).index(m)
                            pair(q)
                            if c == 2 and q > 1:
                                for k in range(4):
                                    tiles(f, i)(1, 4 * (q - 2) + k)
                    if (f, c) != (1, 2):
                        add_squares(post, c)

            def p_to_features():
                for c in range(NC):
                    for k in range(PT):
                        n = RING["pT", c, k]
                        eng.wait_ge(pt_hi, PT * c + k + 1)
                        eng.tensor_tensor(a_lo[:, k, cols(c)], ps[:, n % BANKS, 0:C],
                                          f32(a_hi[:, k, cols(c)]), ALU.subtract
                                          ).then_inc(psum_free, 1)

            def vectors():
                eng.wait_ge(psum_full, RING["params"] + 1)
                src = ps[:, RING["params"] % BANKS, :]
                width = 2 * P
                n = mark(eng.tensor_copy(params[:, 0:NROWS], src[:, 0:NROWS]))
                n = mark(eng.tensor_copy(params[:, P:P + CW * NJ], src[:, P:P + CW * NJ]))
                eng.tensor_copy(params[:, width:3 * P], src[:, width:3 * P]).then_inc(psum_free, 1)
                eng.wait_ge(dve_own, n)
                lam = params[:, ROW["lru_lambda"]:ROW["lru_lambda"] + NJ]
                done(eng.tensor_scalar(sp[:, 2, :], lam, -1.0, None, ALU.mult))
                eng.tensor_tensor(sp[:, 0, :], sp[:, 2, :], lam, ALU.min).then_inc(half_done, 1)
                for f in range(2):
                    g0 = ROW[f"ffn{f + 1}_post_g"]
                    done(eng.tensor_scalar(half_g[:, KT * f:KT * f + KT], params[:, g0:g0 + KT], 0.5,
                                           None, ALU.mult))

            def softplus():
                eng.wait_ge(sp_act, 1)
                done(eng.tensor_scalar(sp[:, 3, :], sp[:, 1, :], 2.0, None, ALU.add))
                done(eng.reciprocal(sp[:, 4, :], sp[:, 3, :]))
                done(eng.tensor_tensor(sp[:, 3, :], sp[:, 1, :], sp[:, 4, :], ALU.mult))
                done(eng.tensor_tensor(sp[:, 4, :], sp[:, 3, :], sp[:, 3, :], ALU.mult))
                done(eng.tensor_scalar(sp[:, 5, :], sp[:, 4, :], 1.0 / 17, 1.0 / 15, ALU.mult, ALU.add))
                for d in (13, 11, 9, 7, 5, 3, 1):
                    done(eng.tensor_tensor(sp[:, 5, :], sp[:, 5, :], sp[:, 4, :], ALU.mult))
                    done(eng.tensor_scalar(sp[:, 5, :], sp[:, 5, :], 1.0 / d, None, ALU.add))
                done(eng.tensor_tensor(sp[:, 5, :], sp[:, 5, :], sp[:, 3, :], ALU.mult))
                done(eng.tensor_scalar(sp[:, 2, :], sp[:, 2, :], 0.0, None, ALU.max))
                done(eng.scalar_tensor_tensor(sp[:, 5, :], sp[:, 5, :], 2.0, sp[:, 2, :], ALU.mult,
                                              ALU.add))
                done(eng.tensor_scalar(sp[:, 6, :], sp[:, 5, :], -8.0, None, ALU.mult))
                done(eng.tensor_scalar(sp[:, 7, :], sp[:, 5, :], 8.0, None, ALU.mult))

            for c in range(NC):
                i = NORM["pre1", c]
                for k in range(KT):
                    n = RING["xT", c, k]
                    eng.wait_ge(sq_done, SQ0[i] + k + 1)
                    eng.tensor_tensor(x_lo[:, k, cols(c)], ps[:, n % BANKS, 0:C],
                                      f32(x_hi[:, k, cols(c)]), ALU.subtract
                                      ).then_inc(psum_free, 1)
                    eng.wait_ge(psum_free, n + 1)
                    if k:
                        add_square(i, k)
                if c == 0:
                    vectors()
                    split_wide(0)
                    split_wide(1)
                invert("pre1", c)
                hidden_chunk(0, 0, c, tiles(0, 0),
                             lambda at: (c, at) == (2, "g0") and split_down(0))
            down_sums(0, 0)
            softplus()
            with eng.Fori(1, NI - 1) as i:
                ffn_step(0, i)
            ffn_last(0, "post1", "pre2", 0)

            glu_n = [0]

            def parts(c):
                return C if c < 2 else LAST

            def put_g(c, j, src, r, op_in1=None):
                w = parts(c)
                ins = eng.tensor_tensor(gp[:, j, CH + C * c:CH + C * c + w], src[:, 0:w],
                                        r[:, 0:w], ALU.mult)
                if c == 2:
                    ins = eng.tensor_tensor(
                        gs[:, j, :, CH:CH + DEC],
                        src[:, w:C].rearrange("p (b t) -> p b t", b=NB),
                        r[:, w:C].rearrange("p (b t) -> p b t", b=NB), ALU.mult)
                ins.then_inc(psum_free, 1)

            def value(n, c, j):
                put_g(c, j, bank(n), rstd("pre2", c))

            def glu_gate(n, c, j):
                b = glu_n[0] % 2
                src = bank(n)
                if glu_n[0] >= 2:
                    eng.wait_ge(glu_done, glu_n[0] - 1)
                eng.tensor_tensor(glu[:, b, :], src, rstd("pre2", c), ALU.mult
                                  ).then_inc(psum_free, 1)
                glu_n[0] += 1

            def glu_mult(k, c, j):
                eng.wait_ge(sig_done, k + 1)
                w = parts(c)
                dst = gp[:, j, CH + C * c:CH + C * c + w]
                ins = eng.tensor_tensor(dst, dst, glu[:, k % 2, 0:w], ALU.mult)
                if c == 2:
                    dst = gs[:, j, :, CH:CH + DEC]
                    ins = eng.tensor_tensor(
                        dst, dst, glu[:, k % 2, w:C].rearrange("p (b t) -> p b t", b=NB), ALU.mult)
                ins.then_inc(glu_done, 1)

            def vg_chunk(c, hook=None):
                for t in range(4):
                    if t < 2:
                        value(RING["vg", c, t], c, t)
                    else:
                        glu_gate(RING["vg", c, t], c, t - 2)
                    if hook:
                        hook(t)
                for j in range(2):
                    eng.wait_ge(psum_free, RING["vg", c, j] + 1)
                    glu_mult(2 * c + j, c, j)

            def last_pair(q):
                apply_pair("post1", 2, 0, acc_tile, half_gain(0), "pre2", q)

            def hook(t):
                if t == 1:
                    invert("pre2", 1)
                if t == 2:
                    invert("post1", 2)

            vg_chunk(0, hook)
            last_pair(0)
            last_pair(1)
            vg_chunk(1, lambda t: t < 2 and last_pair(2 + t))
            invert("pre2", 2)
            vg_chunk(2, lambda t: t == 1 and split_wide(WIDE0["mix"] + 2))
            eng.wait_ge(psum_full, RING["ffn", 0] + NI * STEP)
            eng.memset(gate_raw[:, :, :, :], 0.0).then_inc(gate_zero, 1)
            n_hist = mark(eng.memset(gp[:, :, 0:CH], 0.0))
            for s in range(2):
                n = RING["cache", s]
                eng.wait_ge(psum_full, n + 1)
                for j in range(NJ):
                    ins = eng.tensor_copy(
                        gs[:, j, 4 * s:4 * s + 4, 0:CH],
                        ps[:, n % BANKS, j * 4 * CH:(j + 1) * 4 * CH].rearrange(
                            "p (b w) -> p b w", b=4))
                ins.then_inc(psum_free, 1)
            eng.wait_ge(psum_free, RING["cache", 1] + 1)
            eng.wait_ge(dve_own, n_hist)
            eng.wait_ge(gw_hi_done, 1)
            eng.tensor_tensor(gw_lo[:, :, :, :], gate_raw[:, :, :, :], f32(gw_hi[:, :, :, :]),
                              ALU.subtract).then_inc(gw_lo_done, 1)
            split_wide(WIDE0["mix"] + 3)

            conv_n = [0]

            def conv_taps(count):
                own_taps = CW - TP
                for n in range(conv_n[0], min(conv_n[0] + count, own_taps * NJ)):
                    j, tap = divmod(n, own_taps)
                    tap += TP
                    if tap == TP:
                        eng.wait_ge(glu_done, 6 * (j // 2 + 1))
                    dst_p, src_p = conv[:, j, 0:SEQ], gp[:, j, tap:tap + SEQ]
                    dst_s = conv[:, j, SEQ:TOK].rearrange("p (b t) -> p b t", b=NB)
                    src_s = gs[:, j, :, tap:tap + DEC]
                    for part, (dst, src) in enumerate(((dst_p, src_p), (dst_s, src_s))):
                        if tap == TP:
                            ins = eng.tensor_scalar(dst, src, conv_w(tap, j), vec("conv_b", j),
                                                    ALU.mult, ALU.add)
                        else:
                            eng.wait_ge(conv_step, 2 * n - 1 + part)
                            ins = eng.scalar_tensor_tensor(dst, src, conv_w(tap, j), dst,
                                                           ALU.mult, ALU.add)
                        ins.then_inc(conv_step, 1)
                    conv_n[0] = n + 1

            def conv_join(j, c):
                assert conv_n[0] >= (CW - TP) * (j + 1)
                eng.wait_ge(conv_step, 2 * (CW - TP) * (j + 1))
                src = bank(RING["conv", j, c])
                eng.tensor_tensor(conv[:, j, cols(c)], src, conv[:, j, cols(c)], ALU.add
                                  ).then_inc(psum_free, 1)

            for c in range(NC):
                for t in range(2):
                    value(RING["in", 2, c, t], c, 2 + t)
                    conv_taps(2)
            split_wide(WIDE0["mix"] + 4)
            for c in range(NC):
                for t in range(2):
                    glu_gate(RING["in", 3, c, t], c, 2 + t)
                    conv_taps(1)
                    eng.wait_ge(psum_free, RING["in", 2, c, t] + 1)
                    glu_mult(6 + 2 * c + t, c, 2 + t)
            split_wide(WIDE0["mix"] + 5)
            def conv_states():
                for s in range(3):
                    n = RING["convout", s]
                    w = CH if s == 0 else 4 * CH
                    eng.wait_ge(psum_full, n + 1)
                    eng.tensor_copy(cv_stage[0:w, s, :], ps[0:w, n % BANKS, :]
                                    ).then_inc(psum_free, 1)

            eng.wait_ge(glu_done, 4 * NC)
            eng.tensor_copy(gs_new[:, :, :].rearrange("p j (b w) -> p (j b) w", w=CH),
                            gs[:, :, :, DEC:DEC + CH].rearrange("p j b w -> p (j b) w")
                            ).then_inc(gs_new_done, 1)

            def lru_front(x):
                j, c, t = lru_tile(x)
                if x >= 2:
                    eng.wait_ge(xc_done, x - 1)
                if c == 0:
                    mark(eng.memset(ux_p[:, t, 0:LH], 0.0))
                    mark(eng.tensor_copy(
                        ux_s[:, t, :, 0:LH],
                        st_in(j, 0, NB * LH).rearrange("p (b w) -> p b w", b=NB)))
                else:
                    done(eng.tensor_copy(ux_p[:, t, 0:LH], ux_p[:, t, C:C + LH]))
                src = bank(RING["in", 4 + x // 6, c, t])
                r = rstd("pre2", c)
                w = parts(c)
                ins = eng.tensor_tensor(ux_p[:, t, LH:LH + w], src[:, 0:w], r[:, 0:w], ALU.mult)
                if c == 2:
                    ins = eng.tensor_tensor(
                        ux_s[:, t, :, LH:LH + DEC], src[:, w:C].rearrange("p (b t) -> p b t", b=NB),
                        r[:, w:C].rearrange("p (b t) -> p b t", b=NB), ALU.mult)
                ins.then_inc(psum_free, 1)
                eng.wait_ge(psum_free, RING["in", 4 + x // 6, c, t] + 1)
                if x >= 2:
                    eng.wait_ge(scan_done, x - 1)
                eng.wait_ge(dve_own, own[0])
                b = x % 2
                for tap in range(LW):
                    wt = params[:, ROW["lru_conv_w"] + tap * NJ + j:][:, 0:1]
                    pieces = [(xc[:, b, 0:w], ux_p[:, t, tap:tap + w])]
                    if c == 2:
                        pieces.append((xc[:, b, w:C].rearrange("p (b t) -> p b t", b=NB),
                                       ux_s[:, t, :, tap:tap + DEC]))
                    if tap:
                        eng.wait_ge(dve_own, own[0])
                    for dst, s_ in pieces:
                        if tap == 0:
                            ins = eng.tensor_scalar(dst, s_, wt, vec("lru_conv_b", j), ALU.mult,
                                                    ALU.add)
                        else:
                            ins = eng.scalar_tensor_tensor(dst, s_, wt, dst, ALU.mult, ALU.add)
                        if tap < LW - 1:
                            mark(ins)
                ins.then_inc(xc_done, 1)
                if c == 2:
                    eng.tensor_copy(st_out[:, j, 0:LH], ux_p[:, t, LAST:LAST + LH])
                    done(eng.tensor_copy(
                        st_out[:, j, LH:LH + NB * LH].rearrange("p (b w) -> p b w", b=NB),
                        ux_s[:, t, :, DEC:DEC + LH]))
                eng.wait_ge(xc_hi_done, x + 1)
                eng.tensor_tensor(xc_lo[:, b, :], xc[:, b, :], f32(xc_hi[:, b, :]), ALU.subtract
                                  ).then_inc(xc_lo_done, 1)

            def lru_one_minus(x):
                eng.wait_ge(lru_act, 3 * x + 3)
                eng.scalar_tensor_tensor(lru_q[:, :], lru_q[:, :], 1.0, lru_r[:, :], ALU.add,
                                         ALU.mult).then_inc(lru_gain, 1)

            def lru_scan(x):
                j, c, t = lru_tile(x)
                if x == 0:
                    eng.wait_ge(gw_lo_done, 1)
                if x == 6:
                    eng.wait_ge(conv_out, 48)
                done(eng.tensor_tensor(lru_i[:, :], lru_i[:, :], xc[:, x % 2, :], ALU.mult))
                eng.wait_ge(lru_sqrt, x + 1)
                done(eng.tensor_tensor(lru_i[:, :], lru_i[:, :], lru_q[:, :], ALU.mult))
                w = parts(c)
                first = 0.0 if c == 0 else hs[:, j, C * c - 1:C * c]
                if c:
                    eng.wait_ge(scan_done, x - 1)
                ins = eng.tensor_tensor_scan(hs[:, j, C * c:C * c + w], lru_a[:, 0:w],
                                             lru_i[:, 0:w], first, ALU.mult, ALU.add)
                if c == 2:
                    mark(ins)
                    for b in range(NB):
                        o = LAST + DEC * b
                        ins = eng.tensor_tensor_scan(
                            hs[:, j, C * c + o:C * c + o + DEC], lru_a[:, o:o + DEC],
                            lru_i[:, o:o + DEC], st_in(j, 24 + b, 25 + b), ALU.mult, ALU.add)
                    done(ins)
                    n_st = LH + NB * LH
                    eng.tensor_copy(st_out[:, j, n_st:n_st + 1], hs[:, j, SEQ - 1:SEQ])
                    ins = eng.tensor_copy(
                        st_out[:, j, n_st + 1:n_st + 1 + NB],
                        hs[:, j, SEQ:TOK].rearrange("p (b t) -> p b t", b=NB)[:, :, DEC - 1])
                ins.then_inc(scan_done, 1)

            for x in range(12):
                lru_front(x)
                if x:
                    lru_one_minus(x - 1)
                conv_taps(5)
                if x == 0:
                    conv_join(0, 0)
                    conv_states()
                    continue
                lru_scan(x - 1)
                conv_join(x // NC, x % NC)
                if x == 5:
                    split_wide(WIDE0["mix"] + 6)

            def gelu_in(n):
                j, c, t = lru_tile(n)
                src = bank(RING["in", 6 + n // 6, c, t])
                if n >= 2:
                    eng.wait_ge(yb_lo_done, n - 1)
                eng.tensor_tensor(ge[:, n % 2, :], src, rstd("pre2", c), ALU.mult
                                  ).then_inc(psum_free, 1)

            def yb(n):
                j, c, t = lru_tile(n)
                eng.wait_ge(gelu_done, n + 1)
                eng.wait_ge(scan_done, n + 1)
                eng.tensor_tensor(ge[:, n % 2, :], ge[:, n % 2, :], hs[:, j, cols(c)], ALU.mult
                                  ).then_inc(yb_done, 1)

            def yb_lo(n):
                j, c, t = lru_tile(n)
                eng.wait_ge(yb_hi_done, n + 1)
                eng.tensor_tensor(y_lo[:, NJ + j, cols(c)], ge[:, n % 2, :],
                                  f32(y_hi[:, NJ + j, cols(c)]), ALU.subtract
                                  ).then_inc(yb_lo_done, 1)

            def conv_scale(c):
                r = rstd("conv", c)
                for j in range(NJ):
                    eng.tensor_tensor(conv[:, j, cols(c)], conv[:, j, cols(c)], r, ALU.mult
                                      ).then_inc(cn_done, 1)

            def conv_lo(c):
                for j in range(NJ):
                    eng.wait_ge(cn_silu, NJ * c + j + 1)
                    eng.tensor_tensor(y_lo[:, j, cols(c)], conv[:, j, cols(c)],
                                      f32(y_hi[:, j, cols(c)]), ALU.subtract
                                      ).then_inc(yc_lo_done, 1)

            lru_one_minus(11)
            lru_scan(11)
            for n in range(12):
                c, part = divmod(n, 4)
                if n == 1:
                    split_wide(WIDE0["mix"] + 7)
                if n == 6:
                    split_wide(WIDE0["mix"] + 8)
                    k = RING["state"]
                    eng.wait_ge(psum_full, k + 1)
                    eng.tensor_copy(st_stage[0:36, :], ps[0:36, k % BANKS, :]).then_inc(psum_free, 1)
                if n >= 2:
                    yb_lo(n - 2)
                gelu_in(n)
                if n:
                    yb(n - 1)
                if part == 1:
                    for j in range(1, NJ):
                        add_square(NORM["conv", c], j)
                if part == 3:
                    invert("conv", c)
                if part == 0 and c:
                    conv_scale(c - 1)
                if part == 1 and c:
                    conv_lo(c - 1)
            yb_lo(10)
            yb(11)
            yb_lo(11)
            split_wide(WIDE0["mix"] + 9)
            conv_scale(2)
            conv_lo(2)

            mix_gain = lambda m: vec("mix_post_g", m)

            def out_pair(c, q):
                apply_pair("post2", c, 3 * PAIRS, oc_tile, mix_gain, "pre3", q)

            for c in range(NC):
                for q in range(4):
                    split_wide(WIDE0["mix"] + 8 + 4 * c + q + 2)
                    if c > 1 and q == 0:
                        invert("pre3", c - 2)
                    if c and q == 0:
                        invert("post2", c - 1)
                    if c and q:
                        out_pair(c - 1, q - 1)
                    if c and q == 3:
                        out_pair(c - 1, 3)
                add_squares("post2", c)

            def hook(c, at):
                if (c, at) == (0, "g1"):
                    invert("pre3", 1)
                if (c, at) == (0, "u0"):
                    invert("post2", 2)
                if (c, at) == (0, "lo"):
                    out_pair(2, 0)
                    out_pair(2, 1)

            eng.wait_ge(psum_free, RING["ffn", 1])
            for c in range(NC):
                hidden_chunk(1, 0, c, tiles(1, 0), lambda at: hook(c, at))
                if c == 0:
                    split_down(NI)
                if c == 1:
                    for d in range(2):
                        for m in range(KT):
                            down(1, 0, d, m)
                            if d == 0 and m in (2, 5):
                                out_pair(2, 2 + m // 5)
                        if d == 0:
                            invert("pre3", 2)
            for m in range(KT):
                down(1, 0, 2, m)
                tiles(1, 0)(1, m)
            with eng.Fori(1, NI - 1) as i:
                ffn_step(1, i)
            ffn_last(1, "post3", "pre4", 6 * PAIRS)
            split_down(2 * NI)

            def ple_unit(c, q):
                for t in range(2):
                    src = bank(RING["ple", c, q, t])
                    eng.tensor_tensor(acc[:, 2 * q + t, cols(c)], src, rstd("pre4", c), ALU.mult
                                      ).then_inc(psum_free, 1)
                if (c, q) == (0, 0):
                    p_to_features()
                for t in range(2):
                    n = 8 * c + 2 * q + t
                    src = bank(RING["ple", c, q, 2 + t])
                    eng.wait_ge(gate_sig, n + 1)
                    z = acc[:, 2 * q + t, cols(c)]
                    eng.tensor_tensor(z, src, z, ALU.mult).then_inc(psum_free, 1)
                v = WIDE0["ple"] + 4 * c + q + 2
                if v < N_WIDE:
                    split_wide(v)

            def finish(c, q):
                apply_pair("post4", c, None, acc_tile, lambda m: vec("ple_post_g", m), None, q)

            ple_unit(0, 0)
            invert("pre4", 1)
            add_squares("post3", 2)
            ple_unit(0, 1)
            invert("post3", 2)
            for q in range(4):
                apply_pair("post3", 2, 6 * PAIRS, acc_tile, half_gain(1), "pre4", q)
                ple_unit(*divmod(q + 2, 4))
            add_squares("post4", 0)
            ple_unit(1, 2)
            invert("pre4", 2)
            ple_unit(1, 3)
            invert("post4", 0)
            ple_unit(2, 0)
            finish(0, 0)
            finish(0, 1)
            add_squares("post4", 1)
            ple_unit(2, 1)
            invert("post4", 1)
            finish(0, 2)
            finish(0, 3)
            ple_unit(2, 2)
            eng.wait_ge(psum_free, RING["ple", 2, 3, 0])
            finish(1, 0)
            finish(1, 1)
            ple_unit(2, 3)
            add_squares("post4", 2)
            invert("post4", 2)
            finish(1, 2)
            finish(1, 3)
            for q in range(4):
                finish(2, q)


def lru_tile(x):
    u, r = divmod(x, 6)
    c, t = divmod(r, 2)
    return 2 * u + t, c, t


_INS = ["x_prompt", "x_sample", "cache_conv", "state_lru_conv", "state_lru_h", "p_prompt",
        "p_sample", "ffn1_pre_g", "ffn1_post_g", "ffn1_w_gu", "ffn1_w_down", "mix_pre_g",
        "mix_post_g", "w_in", "conv_w", "conv_b", "conv_norm_g", "lru_conv_w", "lru_conv_b",
        "lru_wa", "lru_ba", "lru_wx", "lru_bx", "lru_lambda", "w_out", "ffn2_pre_g",
        "ffn2_post_g", "ffn2_w_gu", "ffn2_w_down", "ple_norm_g", "ple_w_gate", "ple_w_proj",
        "ple_post_g"]
_OUTS = [("y_prompt", (1, SEQ, D)), ("y_sample", (NB, DEC, D)), ("conv_p", (1, 1, CH, NJ * P)),
         ("lconv_p", (1, 1, LH, NJ * P)), ("h_p", (1, 1, NJ * P)),
         ("conv_s", (1, NB, CH, NJ * P)), ("lconv_s", (1, NB, LH, NJ * P)),
         ("h_s", (1, NB, NJ * P))]


def kernel(**inputs):
    import numpy as _np
    import concourse.bacc as _bacc
    from concourse.bass_utils import run_bass_kernel_spmd as _run

    nc = _bacc.Bacc("TRN2", target_bir_lowering=False, num_devices=1)
    arrays, ins, outs = {}, {}, {}
    for name in _INS:
        arr = _np.ascontiguousarray(inputs[name])
        arrays[f"in_{name}_dram"] = arr
        ins[name] = nc.dram_tensor(f"in_{name}_dram", arr.shape, mybir.dt.from_np(arr.dtype),
                                   kind="ExternalInput").ap()
    for i, (name, shape) in enumerate(_OUTS):
        outs[name] = nc.dram_tensor(f"out_{i}_dram", shape, F32, kind="ExternalOutput").ap()
    build(nc, ins, outs)
    r = _run(nc, [arrays], core_ids=[0])
    return tuple(r.results[0][f"out_{i}_dram"] for i in range(len(_OUTS)))
```
